# Optimizing a Trainium2 kernel written in Bass

```python
import math
import jax, jax.numpy as jnp
from jax import lax
import numpy as np

D_MODEL = 1024
BATCH = 1
SEQ = 256
DEPTH = 1

D_MIX = D_MODEL
ATT_HEADS = 8
HEAD_DIM = 64
D_ATT = ATT_HEADS * HEAD_DIM
D_CONV = D_MIX - D_ATT
DILATED_PATTERNS = ((128, 1), (512, 4), (2048, 16))
ROPE_THETA = 500000.0
ROT_DIM = HEAD_DIM // 4
CONV_WIDTH = 31
N_MEM = 256
XATT_HEADS = 4
XATT_HEAD_DIM = D_MODEL // XATT_HEADS
D_FF = 4 * D_MODEL
D_IN = 3 * D_ATT + 2 * D_CONV
EPS = 1e-6
NEG_INF = -1e30


def rmsnorm(x, g):
    xf = x.astype(jnp.float32)
    var = jnp.mean(xf * xf, axis=-1, keepdims=True)
    return (xf * lax.rsqrt(var + EPS) * g.astype(jnp.float32)).astype(x.dtype)

def layernorm(x, g, b):
    xf = x.astype(jnp.float32)
    mu = jnp.mean(xf, axis=-1, keepdims=True)
    var = jnp.mean(jnp.square(xf - mu), axis=-1, keepdims=True)
    y = (xf - mu) * lax.rsqrt(var + EPS) * g.astype(jnp.float32) + b.astype(jnp.float32)
    return y.astype(x.dtype)

def partial_rotary(t):
    S = t.shape[1]
    half = ROT_DIM // 2
    freqs = ROPE_THETA ** (-jnp.arange(0, ROT_DIM, 2, dtype=jnp.float32) / ROT_DIM)
    ang = jnp.arange(S, dtype=jnp.float32)[:, None] * freqs[None, :]
    cos = jnp.cos(ang)[None, :, None, :]
    sin = jnp.sin(ang)[None, :, None, :]
    tf = t.astype(jnp.float32)
    x1, x2, rest = tf[..., :half], tf[..., half:ROT_DIM], tf[..., ROT_DIM:]
    rot = jnp.concatenate([x1 * cos - x2 * sin, x2 * cos + x1 * sin, rest], axis=-1)
    return rot.astype(t.dtype)

def to_strided(t, d):
    B, S = t.shape[:2]
    rest = t.shape[2:]
    t = jnp.moveaxis(t.reshape(B, S // d, d, *rest), 2, 1)
    return t.reshape(B * d, S // d, *rest)

def from_strided(t, d, B):
    N, L = t.shape[:2]
    rest = t.shape[2:]
    t = jnp.moveaxis(t.reshape(B, d, L, *rest), 1, 2)
    return t.reshape(B, L * d, *rest)

def banded_attention(q, k, v, half):
    N, L, H, Dh = q.shape
    blk = half
    nb = -(-L // blk)
    Lp = nb * blk
    pad = Lp - L
    qb = jnp.pad(q, ((0, 0), (0, pad), (0, 0), (0, 0))).reshape(N, nb, blk, H, Dh)
    kp = jnp.pad(k, ((0, 0), (blk, blk + pad), (0, 0), (0, 0)))
    vp = jnp.pad(v, ((0, 0), (blk, blk + pad), (0, 0), (0, 0)))

    def window(t):
        return jnp.concatenate(
            [t[:, i * blk:i * blk + Lp].reshape(N, nb, blk, H, Dh) for i in range(3)], axis=2)

    kb, vb = window(kp), window(vp)
    s = jnp.einsum('nbqhd,nbkhd->nbhqk', qb, kb).astype(jnp.float32) * (Dh ** -0.5)
    qpos = jnp.arange(nb)[:, None] * blk + jnp.arange(blk)[None, :]
    kpos = jnp.arange(nb)[:, None] * blk - blk + jnp.arange(3 * blk)[None, :]
    valid = ((jnp.abs(kpos[:, None, :] - qpos[:, :, None]) <= half)
             & (kpos >= 0)[:, None, :] & (kpos < L)[:, None, :])
    s = jnp.where(valid[None, :, None], s, NEG_INF)
    m = jnp.max(s, axis=-1, keepdims=True)
    p = jnp.exp(s - m)
    den = jnp.sum(p, axis=-1, keepdims=True)
    o = jnp.einsum('nbhqk,nbkhd->nbqhd', (p / den).astype(v.dtype), vb)
    lse = (m + jnp.log(den))[..., 0]
    o = o.reshape(N, Lp, H, Dh)[:, :L]
    lse = jnp.transpose(lse, (0, 1, 3, 2)).reshape(N, Lp, H)[:, :L]
    return o, lse

def dilated_sliding_attention(q, k, v):
    B = q.shape[0]
    outs, lses = [], []
    for window, d in DILATED_PATTERNS:
        half = window // (2 * d)
        o, lse = banded_attention(to_strided(q, d), to_strided(k, d), to_strided(v, d), half)
        outs.append(from_strided(o, d, B))
        lses.append(from_strided(lse, d, B))
    w = jax.nn.softmax(jnp.stack(lses, axis=0), axis=0)
    o = jnp.sum(w[..., None] * jnp.stack(outs, axis=0).astype(jnp.float32), axis=0)
    return o.astype(q.dtype)

def conformer_conv(a, g, conv_w, conv_b, ln_g, ln_b):
    u = a * jax.nn.sigmoid(g)
    C = u.shape[-1]
    u = lax.conv_general_dilated(
        u, conv_w.reshape(CONV_WIDTH, 1, C).astype(u.dtype),
        window_strides=(1,), padding=[((CONV_WIDTH - 1) // 2, (CONV_WIDTH - 1) // 2)],
        dimension_numbers=('NWC', 'WIO', 'NWC'), feature_group_count=C) + conv_b
    u = layernorm(u, ln_g, ln_b)
    return jax.nn.silu(u)

def first_inputs(seed: int = 0) -> dict:
    key = jax.random.key(seed)
    ks = jax.random.split(key, 20)
    f32 = jnp.float32

    def w(k, shape, fan_in):
        return jax.random.normal(k, shape, f32) * (fan_in ** -0.5)

    def gain(k, shape):
        return 1.0 + 0.02 * jax.random.normal(k, shape, f32)

    return {
        "x": jax.random.normal(ks[0], (BATCH, SEQ, D_MODEL), f32),
        "mem": jax.random.normal(ks[1], (BATCH, N_MEM, D_MODEL), f32),
        "norm_mix_g": gain(ks[2], (DEPTH, D_MODEL)),
        "w_in": w(ks[3], (DEPTH, D_MODEL, D_IN), D_MODEL),
        "conv_w": w(ks[4], (DEPTH, CONV_WIDTH, D_CONV), CONV_WIDTH),
        "conv_b": 0.02 * jax.random.normal(ks[5], (DEPTH, D_CONV), f32),
        "conv_ln_g": gain(ks[6], (DEPTH, D_CONV)),
        "conv_ln_b": 0.02 * jax.random.normal(ks[7], (DEPTH, D_CONV), f32),
        "w_out": w(ks[8], (DEPTH, D_MIX, D_MODEL), D_MIX),
        "norm_x_g": gain(ks[9], (DEPTH, D_MODEL)),
        "norm_mem_g": gain(ks[10], (DEPTH, D_MODEL)),
        "w_xq": w(ks[11], (DEPTH, D_MODEL, D_MODEL), D_MODEL),
        "w_xk": w(ks[12], (DEPTH, D_MODEL, D_MODEL), D_MODEL),
        "w_xv": w(ks[13], (DEPTH, D_MODEL, D_MODEL), D_MODEL),
        "w_xo": w(ks[14], (DEPTH, D_MODEL, D_MODEL), D_MODEL),
        "norm_mlp_g": gain(ks[15], (DEPTH, D_MODEL)),
        "w_up": w(ks[16], (DEPTH, D_MODEL, D_FF), D_MODEL),
        "w_down": w(ks[17], (DEPTH, D_FF, D_MODEL), D_FF),
        "norm_final_g": gain(ks[18], (D_MODEL,)),
    }

def first_block(x, mem, norm_mix_g, w_in, conv_w, conv_b, conv_ln_g, conv_ln_b, w_out,
              norm_x_g, norm_mem_g, w_xq, w_xk, w_xv, w_xo, norm_mlp_g, w_up, w_down,
              norm_final_g):
    B, S, _ = x.shape
    M = mem.shape[1]
    h = x
    for l in range(DEPTH):
        y = rmsnorm(h, norm_mix_g[l]) @ w_in[l]
        q = partial_rotary(y[..., 0:D_ATT].reshape(B, S, ATT_HEADS, HEAD_DIM))
        k = partial_rotary(y[..., D_ATT:2 * D_ATT].reshape(B, S, ATT_HEADS, HEAD_DIM))
        v = y[..., 2 * D_ATT:3 * D_ATT].reshape(B, S, ATT_HEADS, HEAD_DIM)
        att = dilated_sliding_attention(q, k, v).reshape(B, S, D_ATT)
        c0 = 3 * D_ATT
        conv = conformer_conv(y[..., c0:c0 + D_CONV], y[..., c0 + D_CONV:c0 + 2 * D_CONV],
                              conv_w[l], conv_b[l], conv_ln_g[l], conv_ln_b[l])
        h = h + jnp.concatenate([att, conv], axis=-1) @ w_out[l]

        xq = (rmsnorm(h, norm_x_g[l]) @ w_xq[l]).reshape(B, S, XATT_HEADS, XATT_HEAD_DIM)
        mn = rmsnorm(mem, norm_mem_g[l])
        xk = (mn @ w_xk[l]).reshape(B, M, XATT_HEADS, XATT_HEAD_DIM)
        xv = (mn @ w_xv[l]).reshape(B, M, XATT_HEADS, XATT_HEAD_DIM)
        sc = jnp.einsum('bshd,bmhd->bhsm', xq, xk).astype(jnp.float32) * (XATT_HEAD_DIM ** -0.5)
        pr = jax.nn.softmax(sc, axis=-1).astype(xv.dtype)
        xo = jnp.einsum('bhsm,bmhd->bshd', pr, xv).reshape(B, S, D_MODEL)
        h = h + xo @ w_xo[l]

        u = rmsnorm(h, norm_mlp_g[l]) @ w_up[l]
        h = h + jnp.square(jax.nn.relu(u)) @ w_down[l]
    return rmsnorm(h, norm_final_g)


DEPTH_2 = 2

D_MIX_2 = D_MODEL
DN_HEADS = 6
DN_WIDTH = DN_HEADS * HEAD_DIM
FX_HEADS = 6
FX_WIDTH = FX_HEADS * HEAD_DIM
POOL_GROUPS = 4
POOL_WIDTH = D_MIX_2 - DN_WIDTH - FX_WIDTH
POOL_GROUP_DIM = POOL_WIDTH // POOL_GROUPS
POOL_WINDOWS = (2, 4, 8, 16)
CONV_WIDTH_2 = 4
DN_CHUNK = 64
FX_BLOCK = 128
D_FF_2 = 2816
N_EXPERTS = 8
TOP_K = 2
D_FF_EXPERT = 1536
N_DENSE = (DEPTH_2 + 1) // 2
N_MOE = DEPTH_2 // 2
N_IN = 4 * DN_WIDTH + 2 * DN_HEADS + 3 * FX_WIDTH + FX_HEADS + POOL_WIDTH


F32 = jnp.float32

def rmsnorm_2(x, g):
    xf = x.astype(F32)
    y = xf * lax.rsqrt(jnp.mean(xf * xf, axis=-1, keepdims=True) + EPS)
    return (y * g.astype(F32)).astype(x.dtype)

def l2norm(x):
    return x * lax.rsqrt(jnp.sum(x * x, axis=-1, keepdims=True) + EPS)

def causal_conv(x, w):
    c = x.shape[-1]
    return lax.conv_general_dilated(x, w.astype(x.dtype)[:, None, :], window_strides=(1,),
                                    padding=[(CONV_WIDTH_2 - 1, 0)],
                                    dimension_numbers=('NWC', 'WIO', 'NWC'),
                                    feature_group_count=c)

def chunk_gated_delta_rule(q, k, v, g, beta):
    B, T, H, Dk = q.shape
    Dv = v.shape[-1]
    C = DN_CHUNK
    N = T // C

    def to_chunks(a):
        a = a.reshape((B, N, C, H) + a.shape[3:])
        return jnp.moveaxis(a, 3, 1)

    q, k, v, g, beta = (to_chunks(a) for a in (q, k, v, g, beta))
    G = jnp.cumsum(g, axis=-1)
    causal = jnp.tril(jnp.ones((C, C), bool))
    strict = jnp.tril(jnp.ones((C, C), bool), -1)
    diff = G[..., :, None] - G[..., None, :]
    decay = jnp.where(causal, jnp.exp(jnp.where(causal, diff, 0.0)), 0.0)
    kb = k * beta[..., None]
    a_mat = jnp.where(strict, jnp.einsum('bhnid,bhnjd->bhnij', kb, k) * decay, 0.0)
    eye = jnp.eye(C, dtype=q.dtype)
    rhs = jnp.concatenate([v * beta[..., None], kb * jnp.exp(G)[..., None]], axis=-1)
    uw = lax.linalg.triangular_solve(a_mat + eye, rhs, left_side=True, lower=True,
                                     transpose_a=False, conjugate_a=False, unit_diagonal=True)
    u, w = uw[..., :Dv], uw[..., Dv:]
    qk = jnp.where(causal, jnp.einsum('bhnid,bhnjd->bhnij', q, k) * decay, 0.0)
    q_dec = q * jnp.exp(G)[..., None]
    k_dec = k * jnp.exp(G[..., -1:] - G)[..., None]
    last = jnp.exp(G[..., -1])

    def step(S, xs):
        u_n, w_n, qk_n, q_n, k_n, l_n = xs
        v_new = u_n - jnp.einsum('bhck,bhkv->bhcv', w_n, S)
        o_n = jnp.einsum('bhck,bhkv->bhcv', q_n, S) + jnp.einsum('bhij,bhjv->bhiv', qk_n, v_new)
        S = S * l_n[..., None, None] + jnp.einsum('bhck,bhcv->bhkv', k_n, v_new)
        return S, o_n

    xs = tuple(jnp.moveaxis(a, 2, 0) for a in (u, w, qk, q_dec, k_dec, last))
    S0 = jnp.zeros((B, H, Dk, Dv), q.dtype)
    _, o = lax.scan(step, S0, xs)
    return jnp.transpose(o, (1, 0, 3, 2, 4)).reshape(B, T, H, Dv)

def gated_deltanet(q, k, v, z, a, b, conv_w, a_log, dt_bias, onorm_g):
    B, T, _ = q.shape
    dt = q.dtype
    qkv = jax.nn.silu(causal_conv(jnp.concatenate([q, k, v], axis=-1), conv_w)).astype(F32)
    q, k, v = jnp.split(qkv, 3, axis=-1)
    heads = lambda t: t.reshape(B, T, DN_HEADS, HEAD_DIM)
    q = l2norm(heads(q)) * (HEAD_DIM ** -0.5)
    k = l2norm(heads(k))
    v = heads(v)
    beta = jax.nn.sigmoid(b.astype(F32))
    g = -jnp.exp(a_log.astype(F32)) * jax.nn.softplus(a.astype(F32) + dt_bias.astype(F32))
    o = chunk_gated_delta_rule(q, k, v, g, beta)
    o = rmsnorm_2(o, onorm_g) * jax.nn.silu(heads(z).astype(F32))
    return o.reshape(B, T, DN_WIDTH).astype(dt)

def forgetting_attention(q, k, v, f, qnorm_g, knorm_g, f_bias):
    B, T, _ = q.shape
    dt = q.dtype
    heads = lambda t: t.reshape(B, T, FX_HEADS, HEAD_DIM).transpose(0, 2, 1, 3)
    q = rmsnorm_2(heads(q), qnorm_g)
    k = rmsnorm_2(heads(k), knorm_g)
    v = heads(v)
    logf = jax.nn.log_sigmoid(f.astype(F32) + f_bias.astype(F32))
    c = jnp.cumsum(logf, axis=1).transpose(0, 2, 1)
    scale = HEAD_DIM ** -0.5
    outs = []
    for i in range(T // FX_BLOCK):
        lo, hi = i * FX_BLOCK, (i + 1) * FX_BLOCK
        s = jnp.einsum('bhqd,bhkd->bhqk', q[:, :, lo:hi], k[:, :, :hi]).astype(F32) * scale
        s = s + c[:, :, lo:hi, None] - c[:, :, None, :hi]
        q_pos = jnp.arange(lo, hi)[:, None]
        k_pos = jnp.arange(hi)[None, :]
        s = jnp.where(k_pos <= q_pos, s, -jnp.inf)
        p = jax.nn.softmax(s, axis=-1).astype(dt)
        outs.append(jnp.einsum('bhqk,bhkd->bhqd', p, v[:, :, :hi]))
    o = jnp.concatenate(outs, axis=2)
    return o.transpose(0, 2, 1, 3).reshape(B, T, FX_WIDTH)

def pool_mixer(xp, pool_w, pool_scale):
    B, T, _ = xp.shape
    xg = xp.reshape(B, T, POOL_GROUPS, POOL_GROUP_DIM).astype(F32)
    cs = jnp.concatenate([jnp.zeros((B, 1, POOL_GROUPS, POOL_GROUP_DIM), F32),
                          jnp.cumsum(xg, axis=1)], axis=1)
    win = jnp.array(POOL_WINDOWS, jnp.int32)
    t1 = jnp.arange(1, T + 1, dtype=jnp.int32)[:, None]
    start = jnp.maximum(t1 - win[None, :], 0)
    count = (t1 - start).astype(F32)
    gidx = jnp.arange(POOL_GROUPS)[None, :]
    window_sum = cs[:, 1:] - cs[:, start, gidx]
    y = (window_sum / count[..., None] - xg).astype(xp.dtype)
    y = jnp.einsum('btgc,gcd->btgd', y, pool_w)
    return y.reshape(B, T, POOL_WIDTH) * pool_scale

def hybrid_mixer(h, w_in, dn_conv, dn_a_log, dn_dt_bias, dn_onorm, fx_qnorm, fx_knorm, fx_f_bias,
                 pool_w, pool_scale, w_out):
    proj = h @ w_in
    sizes = (DN_WIDTH, DN_WIDTH, DN_WIDTH, DN_WIDTH, DN_HEADS, DN_HEADS,
             FX_WIDTH, FX_WIDTH, FX_WIDTH, FX_HEADS, POOL_WIDTH)
    (dn_q, dn_k, dn_v, dn_z, dn_a, dn_b, fx_q, fx_k, fx_v, fx_f, pl_x) = jnp.split(
        proj, np.cumsum(sizes)[:-1].tolist(), axis=-1)
    o_dn = gated_deltanet(dn_q, dn_k, dn_v, dn_z, dn_a, dn_b, dn_conv, dn_a_log, dn_dt_bias, dn_onorm)
    o_fx = forgetting_attention(fx_q, fx_k, fx_v, fx_f, fx_qnorm, fx_knorm, fx_f_bias)
    o_pl = pool_mixer(pl_x, pool_w, pool_scale)
    return jnp.concatenate([o_dn, o_fx, o_pl], axis=-1) @ w_out

def swiglu(h, w_gate, w_up, w_down):
    return (jax.nn.silu(h @ w_gate) * (h @ w_up)) @ w_down

def moe_swiglu(h, router, w_gate, w_up, w_down):
    B, T, D = h.shape
    ht = h.reshape(B * T, D)
    probs = jax.nn.softmax((ht @ router).astype(F32), axis=-1)
    top_p, top_i = lax.top_k(probs, TOP_K)
    top_p = top_p / jnp.sum(top_p, axis=-1, keepdims=True)
    gates = jnp.sum(jax.nn.one_hot(top_i, N_EXPERTS, dtype=F32) * top_p[..., None], axis=1).astype(h.dtype)
    out = jnp.zeros_like(ht)
    for e in range(N_EXPERTS):
        out = out + gates[:, e:e + 1] * swiglu(ht, w_gate[e], w_up[e], w_down[e])
    return out.reshape(B, T, D)

def second_inputs(seed: int = 0) -> dict:
    key = jax.random.key(seed)
    ks = list(jax.random.split(key, 32))
    counter = [0]

    def nk():
        counter[0] += 1
        return ks[counter[0] - 1]

    def nrm(shape, scale):
        return scale * jax.random.normal(nk(), shape, F32)

    def gain(shape):
        return 1.0 + nrm(shape, 0.05)

    L = DEPTH_2
    x = nrm((BATCH, SEQ, D_MODEL), 1.0)
    norm1 = gain((L, D_MODEL))
    w_in = nrm((L, D_MODEL, N_IN), D_MODEL ** -0.5)
    dn_conv = nrm((L, CONV_WIDTH_2, 3 * DN_WIDTH), CONV_WIDTH_2 ** -0.5)
    dn_a_log = jnp.log(jax.random.uniform(nk(), (L, DN_HEADS), F32, 1.0, 16.0))
    dt0 = jnp.exp(jax.random.uniform(nk(), (L, DN_HEADS), F32, math.log(1e-3), math.log(1e-1)))
    dn_dt_bias = dt0 + jnp.log(-jnp.expm1(-dt0))
    dn_onorm = gain((L, HEAD_DIM))
    fx_qnorm = gain((L, HEAD_DIM))
    fx_knorm = gain((L, HEAD_DIM))
    fx_f_bias = 2.0 + nrm((L, FX_HEADS), 0.5)
    pool_w = nrm((L, POOL_GROUPS, POOL_GROUP_DIM, POOL_GROUP_DIM), POOL_GROUP_DIM ** -0.5)
    pool_scale = 1.0 + nrm((L, POOL_WIDTH), 0.1)
    w_out = nrm((L, D_MIX_2, D_MODEL), 0.5 * D_MIX_2 ** -0.5)
    norm2 = gain((L, D_MODEL))
    ffn_gate = nrm((N_DENSE, D_MODEL, D_FF_2), D_MODEL ** -0.5)
    ffn_up = nrm((N_DENSE, D_MODEL, D_FF_2), D_MODEL ** -0.5)
    ffn_down = nrm((N_DENSE, D_FF_2, D_MODEL), 0.5 * D_FF_2 ** -0.5)
    router = nrm((N_MOE, D_MODEL, N_EXPERTS), D_MODEL ** -0.5)
    moe_gate = nrm((N_MOE, N_EXPERTS, D_MODEL, D_FF_EXPERT), D_MODEL ** -0.5)
    moe_up = nrm((N_MOE, N_EXPERTS, D_MODEL, D_FF_EXPERT), D_MODEL ** -0.5)
    moe_down = nrm((N_MOE, N_EXPERTS, D_FF_EXPERT, D_MODEL), 0.5 * D_FF_EXPERT ** -0.5)
    return {'x': x, 'norm1': norm1, 'w_in': w_in, 'dn_conv': dn_conv, 'dn_a_log': dn_a_log,
            'dn_dt_bias': dn_dt_bias, 'dn_onorm': dn_onorm, 'fx_qnorm': fx_qnorm, 'fx_knorm': fx_knorm,
            'fx_f_bias': fx_f_bias, 'pool_w': pool_w, 'pool_scale': pool_scale, 'w_out': w_out,
            'norm2': norm2, 'ffn_gate': ffn_gate, 'ffn_up': ffn_up, 'ffn_down': ffn_down,
            'router': router, 'moe_gate': moe_gate, 'moe_up': moe_up, 'moe_down': moe_down}

def second_block(x, norm1, w_in, dn_conv, dn_a_log, dn_dt_bias, dn_onorm, fx_qnorm, fx_knorm, fx_f_bias,
              pool_w, pool_scale, w_out, norm2, ffn_gate, ffn_up, ffn_down, router, moe_gate, moe_up,
              moe_down):
    for layer in range(DEPTH_2):
        h = rmsnorm_2(x, norm1[layer])
        x = x + hybrid_mixer(h, w_in[layer], dn_conv[layer], dn_a_log[layer], dn_dt_bias[layer],
                             dn_onorm[layer], fx_qnorm[layer], fx_knorm[layer], fx_f_bias[layer],
                             pool_w[layer], pool_scale[layer], w_out[layer])
        h = rmsnorm_2(x, norm2[layer])
        j = layer // 2
        if layer % 2 == 0:
            x = x + swiglu(h, ffn_gate[j], ffn_up[j], ffn_down[j])
        else:
            x = x + moe_swiglu(h, router[j], moe_gate[j], moe_up[j], moe_down[j])
    return x


def setup_inputs(seed=0):
    out = dict(first_inputs(seed))
    for name, value in second_inputs(seed + 1).items():
        if name != "x":
            out[name + "_2"] = value
    return out


def reference(
    x, mem, norm_mix_g, w_in, conv_w, conv_b, conv_ln_g, conv_ln_b, w_out, norm_x_g, norm_mem_g,
    w_xq, w_xk, w_xv, w_xo, norm_mlp_g, w_up, w_down, norm_final_g, norm1_2, w_in_2, dn_conv_2,
    dn_a_log_2, dn_dt_bias_2, dn_onorm_2, fx_qnorm_2, fx_knorm_2, fx_f_bias_2, pool_w_2,
    pool_scale_2, w_out_2, norm2_2, ffn_gate_2, ffn_up_2, ffn_down_2, router_2, moe_gate_2,
    moe_up_2, moe_down_2,
):
    x = first_block(
        x, mem, norm_mix_g, w_in, conv_w, conv_b, conv_ln_g, conv_ln_b, w_out, norm_x_g,
        norm_mem_g, w_xq, w_xk, w_xv, w_xo, norm_mlp_g, w_up, w_down, norm_final_g,
    )
    return second_block(
        x, norm1_2, w_in_2, dn_conv_2, dn_a_log_2, dn_dt_bias_2, dn_onorm_2, fx_qnorm_2,
        fx_knorm_2, fx_f_bias_2, pool_w_2, pool_scale_2, w_out_2, norm2_2, ffn_gate_2, ffn_up_2,
        ffn_down_2, router_2, moe_gate_2, moe_up_2, moe_down_2,
    )


_drawn_inputs = setup_inputs


def setup_inputs(seed=0):
    import zlib

    import numpy as np

    out = dict(_drawn_inputs(seed))
    spreads = {}
    factors = {'norm_mix_g': 3.899,
     'conv_ln_g': 3.298,
     'conv_ln_b': 3.757,
     'norm_x_g': 8.0,
     'norm_mem_g': 8.0,
     'dn_onorm_2': 2.81,
     'fx_qnorm_2': 4.902,
     'fx_knorm_2': 7.517,
     'norm_mlp_g': 3.104}
    for name, (base, spread) in spreads.items():
        noise = np.random.default_rng([zlib.crc32(name.encode()), seed]).standard_normal(out[name].shape)
        drawn = base * np.exp(spread * noise) if base else spread * noise
        out[name] = __import__('jax').numpy.asarray(drawn.astype(out[name].dtype))
    for name, factor in factors.items():
        out[name] = (out[name] * factor).astype(out[name].dtype)
    return out
```

```python
import numpy as np
import concourse.bass as bass
from concourse import mybir
from contextlib import ExitStack

F32 = mybir.dt.float32
ACT = mybir.ActivationFunctionType
ALU = mybir.AluOpType
AX = mybir.AxisListType

P = 128
S = 256
TT = S // P
D = 1024
KD_ = D // P
HD = 64
EPS = 1e-6
NEG = -1e30
ATT = 512
AH = ATT // HD
TAPS = 31
PAD = TAPS // 2
XH = 4
MLP_SLOTS = 8
LAYERS = 2
NH = 6
HW = NH * HD
DTAPS = 4
FF2 = 2816
FFE = 1536
NE = 8
RING = 3
SLOT = 4096
LEVELS = 7

TABLE = {}
TABLE_COLS = 0
for _name, _n in (("ident", P), ("logc", TT * S), ("causal", TT * S), ("upper", P), ("ones", P),
                  ("levels", LEVELS * P), ("poolinv", TT * S), ("cos", TT * 8), ("sin", TT * 8),
                  ("mean", P), ("sel", NH * P)):
    TABLE[_name] = (TABLE_COLS, _n)
    TABLE_COLS += _n


def table():
    t = np.zeros((P, TABLE_COLS), np.float32)

    def put(name, a):
        at, n = TABLE[name]
        t[:a.shape[0], at:at + n] = a.reshape(a.shape[0], n)

    p = np.arange(P)
    put("ident", np.eye(P))
    q = (np.arange(TT)[None, :, None] * P + p[:, None, None])
    k = np.arange(S)[None, None, :]
    count = (np.abs(q - k) <= 64).astype(int) + ((q - k) % 4 == 0) + ((q - k) % 16 == 0)
    put("logc", np.where(count > 0, np.log(np.maximum(count, 1)), NEG))
    put("causal", np.where(k <= q, 0.0, NEG))
    put("upper", p[:, None] <= p[None, :])
    put("ones", np.ones((P, P)))
    lev = []
    for n in range(LEVELS):
        b = 1 << n
        j, i = p[:, None], p[None, :]
        lev.append((j // (2 * b) == i // (2 * b)) & (j // b % 2 == 0) & (i // b % 2 == 1))
    put("levels", np.stack(lev, 1))
    win = np.array([[2, 4], [8, 16]])[:, p // 64].T
    put("poolinv", 1.0 / np.minimum(np.arange(S)[None, None, :] + 1, win[:, :, None]))
    freqs = (np.float32(500000.0) ** (-np.arange(0, 16, 2, dtype=np.float32) / np.float32(16))).astype(np.float32)
    ang = (np.arange(S, dtype=np.float32)[:, None] * freqs[None, :]).astype(np.float32)
    ang = ang.reshape(TT, P, 8).transpose(1, 0, 2)
    put("cos", np.cos(ang))
    put("sin", np.sin(ang))
    put("mean", np.full((P, P), 1.0 / ATT))
    sel = np.zeros((NH, NH, P))
    sel[np.arange(NH), np.arange(NH)] = 1.0
    put("sel", sel)
    return t


ROWS = [
    [("norm_mix_g", 8), ("norm_x_g", 8), ("norm_mem_g", 8), ("norm_mlp_g", 8), ("norm1_2", 16), ("norm2_2", 16)],
    [("conv_w", 124)],
    [("conv_b", 4), ("conv_ln_g", 4), ("conv_ln_b", 4), ("pool_scale_2", 4), ("dn_conv_2", 72)],
]
COLS = {}
_at = 0
for _tile in ROWS:
    for _name, _n in _tile:
        COLS[_name] = _at
        _at += _n
NCOLS = _at

WIDE = {}
_at = 0
for _name, _n in (("norm_final_g", D), ("fx_qnorm_2", LAYERS * HD), ("fx_knorm_2", LAYERS * HD),
                  ("dn_onorm_2", LAYERS * HD), ("dn_a_log_2", LAYERS * NH), ("dn_dt_bias_2", LAYERS * NH),
                  ("fx_f_bias_2", LAYERS * NH)):
    WIDE[_name] = (_at, _n)
    _at += _n
NWIDE = _at


class Counter:

    def __init__(self, sem, key, points):
        self.sem, self.key, self.points, self.n = sem, key, points, 0

    def mark(self, *name):
        self.n += 1
        if name:
            self.points[name] = (self.key, self.n)
        return self.sem, 1

    def also(self, *name):
        self.points[name] = (self.key, self.n)

    def last(self, back=0):
        return self.sem, self.n - back


def program(nc, A, out, points, stop):
    ctx = ExitStack()
    with ctx:
        def sb(name, shape, dt=F32):
            return ctx.enter_context(nc.sbuf_tensor(name, shape, dt))

        def sem(name):
            return ctx.enter_context(nc.semaphore(name))

        T_ = sb("shape_table", [P, TABLE_COLS])
        X = sb("residual", [P, TT, D])
        XN = sb("normed", [P, TT, D])
        HT = sb("normedT", [P, KD_, S])
        CAT = sb("mixedT", [P, KD_, S])
        W = sb("weights", [P, RING, SLOT])
        GR = sb("vector_rows", [P, 3, P])
        COL = sb("vector_cols", [P, NCOLS])
        WD = sb("vector_wide", [P, NWIDE])
        PR = sb("probs", [P, 3, TT, S])
        PT = sb("probsT", [P, 2, TT, S])
        PW = sb("pool_weights", [P, LAYERS, 2, P])
        RT = sb("router", [P, KD_, NE])
        NHALF = sb("minus_half", [P, 24])
        SS = sb("sumsq", [P, 24])
        MS = sb("meansq", [P, 24])
        RS = sb("rstd", [P, 24])
        NM = sb("negmax", [P, 3, TT])
        DEN = sb("den", [P, 3, TT])
        RDEN = sb("rden", [P, 3, TT])
        SM = sb("small", [P, 16, 16])
        ARENA = sb("arena", [P, 22300])

        def ar(at, *shape):
            n = int(np.prod(shape))
            v = ARENA[:, at:at + n]
            if len(shape) == 2:
                v = v.rearrange("p (a b) -> p a b", a=shape[0])
            elif len(shape) == 3:
                v = v.rearrange("p (a b c) -> p a b c", a=shape[0], b=shape[1])
            elif len(shape) == 4:
                v = v.rearrange("p (a b c d) -> p a b c d", a=shape[0], b=shape[1], c=shape[2])
            return v

        QK = ar(0, TT, 1024)
        QKT = ar(2048, 8, S)
        V = ar(4096, TT, ATT)
        U = ar(5120, 4, S + 2 * PAD)
        C = ar(6264, 4, S)
        SIG = ar(7288, 4, S)
        MT = ar(8312, 8, S)
        XKT = ar(10360, 8, S)
        XV = ar(12408, TT, 1024)
        XQT = ar(14456, 8, S)
        MEM = ar(12408, TT, 1024)
        RT1 = ar(16504, 4, 256)
        UH = ar(0, 3, 4, S)
        SG = ar(3072, 2, 2 * S)
        CI = ar(0, 9, S + 4)
        CO = ar(2340, 9, S)
        KB = ar(0, TT, HW)
        DI = ar(0, 12, P)
        DIT = ar(1536, 12, P)
        PM = ar(3072, 12, P)
        QT3 = ar(4644, TT, 3 * HW)
        ZAB = ar(6948, TT, HW + 12)
        FQ = ar(7740, TT, 2 * HW)
        FV = ar(9276, TT, HW + 6)
        KQ = ar(10056, 3, TT, 2, P)
        KT = ar(11592, 3, TT, P)
        DD = ar(12360, 12, P)
        AQ = ar(13896, 12, 2, P)
        XP = ar(13896, 2, 16 + S)
        SA = ar(13896 + 544, 2, 16 + S)
        SBf = ar(13896 + 1088, 2, 16 + S)
        SC = ar(13896 + 1632, 2, 16 + S)
        YP = ar(13896 + 2176, 2, S)
        LT = HT[:, 0:6, :].rearrange("p a (b c) -> p (a b) c", c=P)
        O = ar(16968, TT, HW)
        VN = ar(17736, TT, HW)
        BV = ar(18504, TT, HW)
        KDC = ar(19272, HW)
        FT = ar(19656, 6, S)
        NCT = ARENA[0:NH, 21192:21192 + S]
        GT = ARENA[0:NH, 21448:21448 + S]
        SST = ar(21704, 3, HD)
        GATE = ar(21896, TT, NE)
        SQ = XN[:, :, 0:2 * HW]

        def system(t, h):
            return (h % 2) * NH + t * (NH // 2) + h // 2

        def chunk_head(s):
            return s % NH // (NH // 2), 2 * (s % (NH // 2)) + s // NH

        ident = T_[:, 0:P]

        def tab(name, n=P):
            return T_[0:n, TABLE[name][0]:TABLE[name][0] + TABLE[name][1]]

        logc = tab("logc").rearrange("p (t k) -> p t k", t=TT)
        causal = tab("causal").rearrange("p (t k) -> p t k", t=TT)
        upper, ones, mean_w = tab("upper"), tab("ones"), tab("mean")
        upper_ones = T_[:, TABLE["upper"][0]:TABLE["upper"][0] + 2 * P]
        levels = tab("levels").rearrange("p (n k) -> p n k", n=LEVELS)
        poolinv = tab("poolinv").rearrange("p (t k) -> p t k", t=2)
        cos = tab("cos").rearrange("p (t k) -> p t k", t=TT)
        sin = tab("sin").rearrange("p (t k) -> p t k", t=TT)
        sel = tab("sel", NH).rearrange("p (h k) -> p h k", h=NH)

        def col(name, i=0):
            return COL[:, COLS[name] + i:COLS[name] + i + 1]

        def cols(name, i, n):
            return COL[:, COLS[name] + i:COLS[name] + i + n]

        def wide(name, l, n):
            at = WIDE[name][0] + l * n
            return WD[:, at:at + n]

        banks = [ctx.enter_context(nc.psum_tensor(f"bank{i}", [P, 512], F32)) for i in range(8)]
        SC_BANK, PT_BANK, RING_BANK = banks[0:2], banks[2:4], banks[4:8]

        matmul_done, scalar_done = sem("matmul_done"), sem("scalar_done")
        vector_done, pool_done = sem("vector_done"), sem("pool_done")
        x_in, mem_in, rows_in, table_in = sem("x_in"), sem("mem_in"), sem("rows_in"), sem("table_in")
        ident_in = sem("ident_in")
        wide_in, poolw_in, out_written = sem("wide_in"), sem("poolw_in"), sem("out_written")
        w_in = [sem(f"weights_in{i}") for i in range(RING)]
        sems = {"pe": matmul_done, "act": scalar_done, "dve": vector_done, "pool": pool_done}
        cpe = Counter(matmul_done, "pe", points)
        cact = Counter(scalar_done, "act", points)
        cdve = Counter(vector_done, "dve", points)
        cpool = Counter(pool_done, "pool", points)

        def after(*name):
            key, n = points.get(name, ("pe", 1))
            return sems[key], n

        def in_loop(e, key, *name, before=False):
            n = points.get(name, (key, 1))[1]
            per = points.get(("per", key), (key, 1))[1]
            return sems[key], e * per + max(1, n - per if before else n)

        slots = []

        def kview(w, a, b):
            return w[:, a:b].rearrange("(k p) n -> p k n", p=P)

        def slot_f(stage, w, a, b):
            slots.append((stage, [((0, b - a, b - a), kview(w, a, b))]))

        def slot_gu(stage, g, u, c):
            slots.append((stage, [((0, 256, 512), kview(g, c, c + 256)), ((256, 512, 512), kview(u, c, c + 256))]))

        def slot_d(stage, w, r, n):
            slots.append((stage, [((0, 1024, 1024), w[r:r + n * P, :].rearrange("(k p) n -> p k n", p=P))]))

        w1 = A["w_in"][0]
        for name, at in (("g", 4), ("a", 3), ("q", 0), ("k", 1), ("v", 2)):
            slot_f(name, w1, at * ATT, (at + 1) * ATT)
        for i in range(2):
            slot_f("xk", A["w_xk"][0], i * 512, i * 512 + 512)
        for i in range(2):
            slot_f("xv", A["w_xv"][0], i * 512, i * 512 + 512)
        for i in range(2):
            slot_f("wout", A["w_out"][0], i * 512, i * 512 + 512)
        for i in range(2):
            slot_f("xq", A["w_xq"][0], i * 512, i * 512 + 512)
        for i in range(2):
            slot_f("xo", A["w_xo"][0], i * 512, i * 512 + 512)
        for i in range(MLP_SLOTS + 1):
            if i < MLP_SLOTS:
                slot_f("up", A["w_up"][0], i * 512, i * 512 + 512)
            if i >= 1:
                slot_d("down", A["w_down"][0], (i - 1) * 512, 4)
        N1 = len(slots)
        GU2 = FF2 // 256
        DN2 = (GU2 + 1) // 2
        expert_slots = []
        for l in range(LAYERS):
            w2 = A["w_in_2"][l]
            for i in range(3):
                slot_f("cqkv", w2, i * HW, i * HW + HW)
            slot_f("pool", w2, 2706, 2962)
            slot_f("zab", w2, 1152, 1548)
            slot_f("fq", w2, 1548, 1932)
            slot_f("fk", w2, 1932, 2316)
            slot_f("fv", w2, 2316, 2706)
            for i in range(2):
                slot_f("wout2", A["w_out_2"][l], i * 512, i * 512 + 512)
            if l == 0:
                for i in range(GU2):
                    slot_gu("gu", A["ffn_gate_2"][0], A["ffn_up_2"][0], i * 256)
                    if i >= 2 and i % 2 == 0:
                        slot_d("dn", A["ffn_down_2"][0], (i - 2) * 256, 4)
                slot_d("dn", A["ffn_down_2"][0], (DN2 - 1) * 512, FF2 // P - 4 * (DN2 - 1))
        EXPERT0 = len(slots)
        EXPERT = ["gu", "gu", "gu", "dn", "gu", "gu", "dn", "gu", "dn"]
        loads = []
        total = [0] * RING
        for j, s in enumerate(slots):
            total[j % RING] += 16 * len(s[1])
            loads.append(total[j % RING])
        expert_loads, expert_total = [], [0] * RING
        for s, kind in enumerate(EXPERT):
            r = (EXPERT0 + s) % RING
            expert_total[r] += 32 if kind == "gu" else 16
            expert_loads.append(total[r] + expert_total[r])

        def slot_view(j, n, k=8):
            return W[:, j % RING, 0:k * n].rearrange("p (k n) -> p k n", k=k)

        bank_of = {}
        order = []

        with nc.Block() as block:

            @block.tensor
            def _(pe):
                nslot = [0]

                def weights(stage, n, k=8):
                    j = nslot[0]
                    assert slots[j][0] == stage, (j, slots[j][0], stage)
                    nslot[0] += 1
                    pe.wait_ge(w_in[j % RING], loads[j])
                    return j, slot_view(j, n, k)

                def open_bank(*name):
                    k = len(order)
                    if k >= 4:
                        pe.wait_ge(*after("read", *order[k - 4]))
                    order.append(name)
                    bank_of[name] = RING_BANK[k % 4]
                    return RING_BANK[k % 4]

                def tokens_out(stage, actT, n, i=0, tag=()):
                    j, w = weights(stage, n)
                    for t in range(TT):
                        ps = open_bank(stage, *tag, i, t)
                        for k in range(KD_):
                            mm = pe.matmul(ps[:, 0:n], actT[:, k, t * P:(t + 1) * P], w[:, k, :],
                                           start=(k == 0), stop=(k == KD_ - 1))
                        mm.then_inc(*cpe.mark("filled", stage, *tag, i, t))
                    cpe.also("slot", j)

                def features_out(stage, actT, n, i=0, tag=()):
                    j, w = weights(stage, n)
                    for b in range(0, n, 256):
                        ps = open_bank(stage, *tag, i, b // 256)
                        for c in range(b, min(b + 256, n), P):
                            for k in range(KD_):
                                mm = pe.matmul(ps[:, (c - b) * 2:(c - b) * 2 + S], w[:, k, c:c + P],
                                               actT[:, k, :], start=(k == 0), stop=(k == KD_ - 1))
                        mm.then_inc(*cpe.mark("filled", stage, *tag, i, b // 256))
                    cpe.also("slot", j)

                def turn_norm(i):
                    for t in range(TT):
                        pe.wait_ge(*after("xn", i, t))
                        for b in range(2):
                            ps = open_bank("normT", i, t, b)
                            for k in range(4):
                                mm = pe.transpose(ps[:, k * P:(k + 1) * P],
                                                  XN[:, t, (4 * b + k) * P:(4 * b + k + 1) * P], ident)
                            mm.then_inc(*cpe.mark("filled", "normT", i, t, b))

                def attention(u0, heads, scores, outs):
                    for s in range(heads + 2):
                        if s < heads:
                            u = u0 + s
                            if u >= 2:
                                pe.wait_ge(*after("scores_read", u - 2))
                            scores(s, SC_BANK[u % 2]).then_inc(*cpe.mark("scores", u))
                        if 1 <= s <= heads:
                            u = u0 + s - 1
                            pe.wait_ge(*after("probs", u))
                            if u >= 2:
                                pe.wait_ge(*after("pt_copied", u - 2))
                            ps = PT_BANK[u % 2]
                            for kt in range(TT):
                                for qt in range(TT):
                                    mm = pe.transpose(ps[:, kt * S + qt * P:kt * S + (qt + 1) * P],
                                                      PR[:, u % 3, qt, kt * P:(kt + 1) * P], ident)
                            mm.then_inc(*cpe.mark("pt", u))
                        if s >= 2:
                            u = u0 + s - 2
                            pe.wait_ge(*after("pt_copied", u))
                            outs(s - 2, PT[:, u % 2], u)

                def pair_outs(stage, tag, v):
                    def outs(h, pt, u):
                        if h % 2 == 0:
                            ps = open_bank(stage, *tag, h // 2)
                        else:
                            ps = bank_of[(stage, *tag, h // 2)]
                        o = 64 * (h % 2)
                        for kt in range(TT):
                            mm = pe.matmul(ps[o:o + HD, 0:S], v[:, kt, h * HD:(h + 1) * HD], pt[:, kt, :],
                                           start=(kt == 0), stop=(kt == TT - 1))
                        mm.then_inc(*cpe.mark("o", u))
                        if h % 2:
                            cpe.also("filled", stage, *tag, h // 2)
                    return outs

                pe.wait_ge(rows_in, 16 * 12)
                pe.wait_ge(ident_in, 16)
                ps = open_bank("cols")
                at = 0
                for i, n in enumerate((64, 124, 88)):
                    mm = pe.transpose(ps[:, at:at + n], GR[0:n, i, :], ident[0:n, 0:n])
                    at += n
                mm.then_inc(*cpe.mark("filled", "cols"))

                turn_norm(0)
                pe.wait_ge(*after("ht", 0))
                features_out("g", HT, 512)
                features_out("a", HT, 512)
                tokens_out("q", HT, 512)
                tokens_out("k", HT, 512)
                tokens_out("v", HT, 512)
                turn_norm(1)
                pe.wait_ge(*after("ht", 1))
                for i in range(2):
                    features_out("xk", MT, 512, i)
                pe.wait_ge(*after("rotated"))
                for b in range(4):
                    ps = open_bank("qkT", b)
                    for c in range(2):
                        for t in range(TT):
                            mm = pe.transpose(ps[:, c * S + t * P:c * S + (t + 1) * P],
                                              QK[:, t, (2 * b + c) * P:(2 * b + c + 1) * P], ident)
                    mm.then_inc(*cpe.mark("filled", "qkT", b))
                pe.wait_ge(*after("read", "qkT", 3))
                pe.wait_ge(*after("read", "v", 0, 1))

                def scores1(h, ps):
                    o = 64 * (h % 2)
                    for t in range(TT):
                        mm = pe.matmul(ps[:, t * S:(t + 1) * S], QKT[o:o + HD, h // 2, t * P:(t + 1) * P],
                                       QKT[o:o + HD, 4 + h // 2, :], start=True, stop=True)
                    return mm

                attention(0, AH, scores1, pair_outs("att_o", (), V))
                for i in range(2):
                    tokens_out("xv", MT, 512, i)
                for name, need in (("cmean", "conv"), ("cvar", "csq")):
                    pe.wait_ge(*after(need))
                    src = C if name == "cmean" else SIG
                    ps = open_bank(name)
                    for k in range(4):
                        mm = pe.matmul(ps[:, 0:S], mean_w, src[:, k, :], start=(k == 0), stop=(k == 3))
                    mm.then_inc(*cpe.mark("filled", name))
                pe.wait_ge(*after("convT"))
                pe.wait_ge(*after("read", "att_o", 3))
                for i in range(2):
                    tokens_out("wout", CAT, 512, i)

                turn_norm(2)
                pe.wait_ge(*after("ht", 2))
                for i in range(2):
                    features_out("xq", HT, 512, i)
                pe.wait_ge(*after("read", "xq", 1, 1))
                pe.wait_ge(*after("read", "xv", 1, 1))

                def scoresx(h, ps):
                    for t in range(TT):
                        for c in range(2):
                            mm = pe.matmul(ps[:, t * S:(t + 1) * S], XQT[:, 2 * h + c, t * P:(t + 1) * P],
                                           XKT[:, 2 * h + c, :], start=(c == 0), stop=(c == 1))
                    return mm

                def outsx(h, pt, u):
                    ps = open_bank("xatt_o", h)
                    for c in range(2):
                        for kt in range(TT):
                            mm = pe.matmul(ps[:, c * S:(c + 1) * S],
                                           XV[:, kt, h * 256 + c * P:h * 256 + (c + 1) * P], pt[:, kt, :],
                                           start=(kt == 0), stop=(kt == TT - 1))
                    mm.then_inc(*cpe.mark("o", u))
                    cpe.also("filled", "xatt_o", h)

                attention(AH, XH, scoresx, outsx)
                pe.wait_ge(*after("read", "xatt_o", 3))
                for i in range(2):
                    tokens_out("xo", CAT, 512, i)

                def down(j, w, hbuf, n, first, last, *done):
                    for k in range(n):
                        for t in range(TT):
                            for c in range(2):
                                mm = pe.matmul(banks[2 * t + c][:, :], hbuf[:, k, t * P:(t + 1) * P],
                                               w[:, k, c * 512:(c + 1) * 512],
                                               start=(first and k == 0), stop=(last and k == n - 1))
                    mm.then_inc(*cpe.mark(*done))

                turn_norm(3)
                pe.wait_ge(*after("ht", 3))
                for i in range(MLP_SLOTS + 1):
                    if i < MLP_SLOTS:
                        features_out("up", HT, 512, i)
                    if i >= 1:
                        j, w = weights("down", 1024, 4)
                        if i == 1:
                            pe.wait_ge(*after("scores_read", AH + XH - 1))
                            pe.wait_ge(*after("pt_copied", AH + XH - 1))
                        pe.wait_ge(*after("hidden", "mlp", i - 1, 1))
                        down(j, w, UH[:, (i - 1) % 3], 4, i == 1, i == MLP_SLOTS, "down", "mlp", i - 1)
                        cpe.also("slot", j)

                if stop == 1:
                    return

                for l in range(LAYERS):
                    turn_norm(5 + 2 * l)
                    pe.wait_ge(*after("ht", 5 + 2 * l))
                    for i in range(3):
                        features_out("cqkv", HT, HW, i, (l,))
                    features_out("pool", HT, 256, 0, (l,))
                    tokens_out("zab", HT, HW + 12, 0, (l,))
                    for name, n in (("fq", HW), ("fk", HW), ("fv", HW + 6)):
                        tokens_out(name, HT, n, 0, (l,))
                    pe.wait_ge(*after("pooled", l))
                    if l == 0:
                        pe.wait_ge(poolw_in, 16 * 8)
                        pe.wait_ge(*after("poolw_zero"))
                    ps = open_bank("poolw", l)
                    for i in range(2):
                        mm = pe.matmul(ps[:, i * S:(i + 1) * S], PW[:, l, i, :], YP[:, i, :], start=True, stop=True)
                    mm.then_inc(*cpe.mark("filled", "poolw", l))
                    for b in range(5):
                        ps = open_bank("dnT", l, b)
                        for c in range(2 * b, min(2 * b + 2, 9)):
                            pe.wait_ge(*after("conv2", l, c))
                            for t in range(TT):
                                mm = pe.transpose(ps[:, t * S + (c % 2) * P:t * S + (c % 2 + 1) * P],
                                                  CO[:, c, t * P:(t + 1) * P], ident)
                        mm.then_inc(*cpe.mark("filled", "dnT", l, b))
                    pe.wait_ge(*after("gates", l))
                    ps = open_bank("cum", l)
                    g, nf = SM[:, 0, 0:12], SM[:, 1, 0:12]
                    for t in range(TT):
                        pe.matmul(ps[:, 6 * t:6 * t + 6], upper, g[:, 6 * t:6 * t + 6], start=True, stop=True)
                        pe.matmul(ps[0:NH, 128 + t * P:128 + (t + 1) * P], g[:, 6 * t:6 * t + 6], upper,
                                  start=True, stop=True)
                        mm = pe.matmul(ps[:, 16 + 6 * t:22 + 6 * t], ones, g[:, 6 * t:6 * t + 6],
                                       start=True, stop=True)
                    mm.then_inc(*cpe.mark("filled", "cum", l))
                    ps = open_bank("ncum", l)
                    pe.matmul(ps[0:NH, 0:S], nf[:, 0:6], upper_ones, start=True, stop=False)
                    pe.matmul(ps[0:NH, P:S], nf[:, 6:12], upper, start=False, stop=True)\
                      .then_inc(*cpe.mark("filled", "ncum", l))
                    pe.wait_ge(*after("fx_normed", l))
                    for b in range(3):
                        ps = open_bank("fT", l, b)
                        for c in range(2):
                            for t in range(TT):
                                mm = pe.transpose(ps[:, c * S + t * P:c * S + (t + 1) * P],
                                                  FQ[:, t, (2 * b + c) * P:(2 * b + c + 1) * P], ident)
                        mm.then_inc(*cpe.mark("filled", "fT", l, b))
                    for p in range(3):
                        pe.wait_ge(*after("dn_ready", l))
                        ps = open_bank("kqT", l, p)
                        for t in range(TT):
                            pe.transpose(ps[:, (2 * t) * P:(2 * t + 1) * P], KB[:, t, p * P:(p + 1) * P], ident)
                            mm = pe.transpose(ps[:, (2 * t + 1) * P:(2 * t + 2) * P],
                                              QT3[:, t, p * P:(p + 1) * P], ident)
                        mm.then_inc(*cpe.mark("filled", "kqT", l, p))
                    for p in range(3):
                        ps = open_bank("kT", l, p)
                        for t in range(TT):
                            mm = pe.transpose(ps[:, t * P:(t + 1) * P],
                                              QT3[:, t, HW + p * P:HW + (p + 1) * P], ident)
                        mm.then_inc(*cpe.mark("filled", "kT", l, p))
                    pe.wait_ge(*after("read", "cum", l))
                    for b in range(4):
                        ps = open_bank("grow", l, b)
                        for c in range(3):
                            t, h = chunk_head(3 * b + c)
                            mm = pe.matmul(ps[:, c * P:(c + 1) * P], sel[:, h, :], GT[:, t * P:(t + 1) * P],
                                           start=True, stop=True)
                        mm.then_inc(*cpe.mark("filled", "grow", l, b))
                    pe.wait_ge(*after("read", "kT", l, 2))
                    for b in range(6):
                        ps = open_bank("aq", l, b)
                        for c in range(2):
                            t, h = chunk_head(2 * b + c)
                            o = 64 * (h % 2)
                            mm = pe.matmul(ps[:, c * S:(c + 1) * S], KT[o:o + HD, h // 2, t, :],
                                           KQ[o:o + HD, h // 2, t, :, :].rearrange("p a b -> p (a b)"),
                                           start=True, stop=True)
                        mm.then_inc(*cpe.mark("filled", "aq", l, b))

                    pe.wait_ge(*after("read", "fT", l, 2))
                    pe.wait_ge(*after("read", "ncum", l))

                    def scores2(h, ps):
                        o = 64 * (h % 2)
                        for t in range(TT):
                            pe.matmul(ps[:, t * S:(t + 1) * S], FT[o:o + HD, h // 2, t * P:(t + 1) * P],
                                      FT[o:o + HD, 3 + h // 2, :], start=True, stop=False)
                            mm = pe.matmul(ps[:, t * S:(t + 1) * S], sel[:, h, :], NCT, start=False, stop=True)
                        return mm

                    if l == 0:
                        pe.wait_ge(*after("x", "mlp"))
                    else:
                        pe.wait_ge(*after("x", "ffn"))
                    attention(AH + XH + NH * l, NH, scores2, pair_outs("fx_o", (l,), FV))

                    for lev in range(LEVELS):
                        for gi in range(3):
                            sy = range(4 * gi, 4 * gi + 4)
                            pe.wait_ge(*after("level", l, lev, gi))
                            if lev == 0:
                                ps = open_bank("inv0", l, gi)
                                for i, s in enumerate(sy):
                                    mm = pe.transpose(ps[:, i * P:(i + 1) * P], LT[:, s, :], ident)
                                mm.then_inc(*cpe.mark("filled", "inv0", l, gi))
                                continue
                            pe.wait_ge(*after("inv", l, lev - 1, gi))
                            ps = open_bank("invp", l, lev, gi)
                            for i, s in enumerate(sy):
                                mm = pe.matmul(ps[:, i * P:(i + 1) * P], LT[:, s, :], DI[:, s, :],
                                               start=True, stop=True)
                            mm.then_inc(*cpe.mark("filled", "invp", l, lev, gi))
                        if lev == 0:
                            continue
                        for gi in range(3):
                            sy = range(4 * gi, 4 * gi + 4)
                            pe.wait_ge(*after("read", "invp", l, lev, gi))
                            if lev < LEVELS - 1:
                                ps = open_bank("invd", l, lev, gi)
                                for i, s in enumerate(sy):
                                    mm = pe.matmul(ps[:, i * P:(i + 1) * P], DIT[:, s, :], PM[:, s, :],
                                                   start=True, stop=True)
                                mm.then_inc(*cpe.mark("filled", "invd", l, lev, gi))
                            ps = open_bank("invt", l, lev, gi)
                            for i, s in enumerate(sy):
                                mm = pe.matmul(ps[:, i * P:(i + 1) * P], PM[:, s, :], DIT[:, s, :],
                                               start=True, stop=True)
                            mm.then_inc(*cpe.mark("filled", "invt", l, lev, gi))
                    pe.wait_ge(*after("inv", l, LEVELS - 1, 2))

                    def per_head(name, lhs, rhs):
                        ps = open_bank(name, l)
                        for h in range(NH):
                            mm = pe.matmul(ps[:, h * HD:(h + 1) * HD], lhs(h), rhs(h), start=True, stop=True)
                        mm.then_inc(*cpe.mark("filled", name, l))

                    def hs(h):
                        return slice(h * HD, (h + 1) * HD)

                    pe.wait_ge(*after("bv", l))
                    per_head("vn0", lambda h: DIT[:, system(0, h), :], lambda h: BV[:, 0, hs(h)])
                    pe.wait_ge(*after("read", "vn0", l))
                    ps = open_bank("state", l)
                    for h in range(NH):
                        o = 64 * (h % 2)
                        mm = pe.matmul(ps[o:o + HD, (h // 2) * HD:(h // 2 + 1) * HD], KDC[:, hs(h)],
                                       VN[:, 0, hs(h)], start=True, stop=True)
                    mm.then_inc(*cpe.mark("filled", "state", l))
                    per_head("o0", lambda h: AQ[:, system(0, h), 1, :], lambda h: VN[:, 0, hs(h)])
                    pe.wait_ge(*after("read", "state", l))

                    def half(h):
                        return slice(64 * (h % 2), 64 * (h % 2) + HD)

                    for par in range(2):
                        ps = open_bank("ks", l, par)
                        for p in range(3):
                            for a in range(2):
                                at = (3 * a + p) * HD
                                mm = pe.matmul(ps[:, at:at + HD], KQ[half(par), p, 1, a, :], SST[half(par), p, :],
                                               start=True, stop=True)
                        mm.then_inc(*cpe.mark("filled", "ks", l, par))
                    pe.wait_ge(*after("bv1", l))
                    per_head("vn1", lambda h: DIT[:, system(1, h), :], lambda h: BV[:, 1, hs(h)])
                    pe.wait_ge(*after("read", "vn1", l))
                    per_head("o1", lambda h: AQ[:, system(1, h), 1, :], lambda h: VN[:, 1, hs(h)])
                    pe.wait_ge(*after("dn_out", l))
                    for b in range(2):
                        ps = open_bank("dnoT", l, b)
                        for c in range(2 * b, min(2 * b + 2, 3)):
                            for t in range(TT):
                                mm = pe.transpose(ps[:, (c % 2) * S + t * P:(c % 2) * S + (t + 1) * P],
                                                  O[:, t, c * P:(c + 1) * P], ident)
                        mm.then_inc(*cpe.mark("filled", "dnoT", l, b))
                    pe.wait_ge(*after("read", "dnoT", l, 1))
                    pe.wait_ge(*after("read", "fx_o", l, 2))
                    pe.wait_ge(*after("read", "poolw", l))
                    for i in range(2):
                        tokens_out("wout2", CAT, 512, i, (l,))

                    turn_norm(6 + 2 * l)
                    pe.wait_ge(*after("ht", 6 + 2 * l))

                    def gate_up(w, *name):
                        for c in range(2):
                            ps = open_bank(*name, c)
                            for m in range(2):
                                for k in range(KD_):
                                    mm = pe.matmul(ps[:, m * S:(m + 1) * S],
                                                   w[:, k, m * 256 + c * P:m * 256 + (c + 1) * P], HT[:, k, :],
                                                   start=(k == 0), stop=(k == KD_ - 1))
                            mm.then_inc(*cpe.mark("filled", *name, c))

                    if l == 0:
                        gu = dn = 0
                        pe.wait_ge(*after("scores_read", AH + XH + NH - 1))
                        pe.wait_ge(*after("pt_copied", AH + XH + NH - 1))
                        while nslot[0] < len(slots) and slots[nslot[0]][0] in ("gu", "dn"):
                            if slots[nslot[0]][0] == "gu":
                                j, w = weights("gu", 512)
                                gate_up(w, "gu", gu)
                                gu += 1
                            else:
                                n = min(4, FF2 // P - 4 * dn)
                                j, w = weights("dn", 1024, 4)
                                pe.wait_ge(*after("hidden", "ffn", min(2 * dn + 1, GU2 - 1), 1))
                                down(j, w, UH[:, dn % 3], n, dn == 0, dn == DN2 - 1, "down", "ffn", dn)
                                dn += 1
                            cpe.also("slot", j)
                        continue

                    ps = open_bank("router")
                    for t in range(TT):
                        for k in range(KD_):
                            mm = pe.matmul(ps[:, t * NE:(t + 1) * NE], HT[:, k, t * P:(t + 1) * P], RT[:, k, :],
                                           start=(k == 0), stop=(k == KD_ - 1))
                    mm.then_inc(*cpe.mark("filled", "router"))
                    for b in range(1, 5):
                        pe.wait_ge(*after("read", *order[-b]))
                    pe.wait_ge(*after("scores_read", AH + XH + 2 * NH - 1))
                    pe.wait_ge(*after("pt_copied", AH + XH + 2 * NH - 1))
                    base = cpe.n
                    job0 = len(order)
                    points[("job0",)] = ("pe", job0)
                    with pe.Fori(0, NE) as e:
                        gu = dn = 0
                        for s, kind in enumerate(EXPERT):
                            r = (EXPERT0 + s) % RING
                            pe.wait_ge(w_in[r], e * expert_total[r] + expert_loads[s])
                            if kind == "gu":
                                w = slot_view(EXPERT0 + s, 512)
                                for c in range(2):
                                    k_ = 2 * gu + c
                                    ps = RING_BANK[(job0 + k_) % 4]
                                    pe.wait_ge(*in_loop(e, "dve", "hidden", "moe", (k_ - 4) % 12 // 2, c,
                                                        before=k_ < 4))
                                    for m in range(2):
                                        for k in range(KD_):
                                            mm = pe.matmul(ps[:, m * S:(m + 1) * S],
                                                           w[:, k, m * 256 + c * P:m * 256 + (c + 1) * P],
                                                           HT[:, k, :], start=(k == 0), stop=(k == KD_ - 1))
                                    mm.then_inc(*cpe.mark("filled", "moe", gu, c))
                                gu += 1
                            else:
                                w = slot_view(EXPERT0 + s, 1024, 4)
                                pe.wait_ge(*in_loop(e, "dve", "hidden", "moe", 2 * dn + 1, 1))
                                if dn == 0:
                                    pe.wait_ge(*in_loop(e, "dve", "moe_added", 3, before=True))
                                down(0, w, UH[:, dn], 4, dn == 0, dn == 2, "down", "moe", dn)
                                dn += 1
                            cpe.also("expert_slot", s)
                    per_pe = cpe.n - base
                    points[("per", "pe")] = ("pe", per_pe)
                    cpe.n += (NE - 1) * per_pe

            @block.sync
            def _(sp):
                xv = A["x"][0].rearrange("(t p) n -> p t n", p=P)
                for t in range(TT):
                    sp.dma_start(X[:, t, :], xv[:, t, :]).then_inc(x_in, 16)
                sp.dma_start(T_[:, 0:P], A["table"][:, 0:P]).then_inc(ident_in, 16)

                def load(j):
                    if j >= RING:
                        sp.wait_ge(*after("slot", j - RING))
                    for (a, b, n), src in slots[j][1]:
                        k = src.shape[1]
                        sp.dma_start(slot_view(j, n, k)[:, :, a:b], src).then_inc(w_in[j % RING], 16)

                for j in range(RING):
                    load(j)
                for t in range(TT):
                    sp.dma_start(MEM[:, t, :], A["mem"][0].rearrange("(t p) n -> p t n", p=P)[:, t, :])\
                      .then_inc(mem_in, 16)
                sp.dma_start(T_[:, P:], A["table"][:, P:]).then_inc(table_in, 16)
                for name in WIDE:
                    at, n = WIDE[name]
                    src = A[name].rearrange("a b -> (a b)") if len(A[name].shape) == 2 else A[name]
                    sp.dma_start(WD[:, at:at + n], src.partition_broadcast(P)).then_inc(wide_in, 16)
                sp.dma_start(RT[:, :, :], A["router_2"][0].rearrange("(k p) n -> p k n", p=P)).then_inc(wide_in, 16)
                sp.wait_ge(*after("poolw_zero"))
                for l in range(LAYERS):
                    for g in range(4):
                        o = 64 * (g % 2)
                        sp.dma_start(PW[o:o + 64, l, g // 2, o:o + 64], A["pool_w_2"][l, g]).then_inc(poolw_in, 16)
                for j in range(RING, len(slots) if stop == 0 else N1):
                    load(j)
                if stop == 1:
                    sp.wait_ge(*after("x_final"))
                else:
                    with sp.Fori(0, NE) as e:
                        gu = dn = 0
                        for s, kind in enumerate(EXPERT):
                            j = EXPERT0 + s
                            sp.wait_ge(*in_loop(e, "pe", "expert_slot", (s - RING) % len(EXPERT),
                                                before=s < RING))
                            r = j % RING
                            if kind == "gu":
                                for m, w in enumerate((A["moe_gate_2"], A["moe_up_2"])):
                                    sp.dma_start(slot_view(j, 512)[:, :, m * 256:(m + 1) * 256],
                                                 w[0, bass.ds(e, 1), :, gu * 256:(gu + 1) * 256]
                                                 .rearrange("e (k p) n -> p (e k) n", p=P)).then_inc(w_in[r], 16)
                                gu += 1
                            else:
                                sp.dma_start(slot_view(j, 1024, 4),
                                             A["moe_down_2"][0, bass.ds(e, 1), dn * 512:(dn + 1) * 512, :]
                                             .rearrange("e (k p) n -> p (e k) n", p=P)).then_inc(w_in[r], 16)
                                dn += 1
                    sp.wait_ge(*after("x_final"))
                sp.dma_start(out[0].rearrange("(t p) n -> p t n", p=P), X[:, :, :]).then_inc(out_written, 16)
                sp.wait_ge(out_written, 16)

            @block.scalar
            def _(act):
                for i, tile in enumerate(ROWS):
                    at = 0
                    for name, n in tile:
                        src = A[name]
                        if len(src.shape) == 3:
                            src = src.rearrange("a b (r p) -> (a b r) p", p=P)
                        else:
                            src = src.rearrange("a (r p) -> (a r) p", p=P)
                        act.dma_start(GR[at:at + n, i, :], src).then_inc(rows_in, 16)
                        at += n

                def do(ins, *name):
                    ins.then_inc(*cact.mark(*name))

                def own():
                    act.wait_ge(*cact.last())

                def sumsq(i, src):
                    for t in range(TT):
                        do(act.activation(XN[:, t, :], src[:, t, :], ACT.Square, accum_out=SS[:, t:t + 1]),
                           "ss", i, t)

                def copy_out(dst, src, *name):
                    act.wait_ge(*after("filled", *name))
                    do(act.activation(dst, src, ACT.Copy), "read", *name)

                def exps(u):
                    act.wait_ge(*after("negmax", u))
                    for t in range(TT):
                        do(act.activation(PR[:, u % 3, t, :], PR[:, u % 3, t, :], ACT.Exp,
                                          bias=NM[:, u % 3, t:t + 1], accum_out=DEN[:, u % 3, t:t + 1]),
                           "exp", u, t)

                def attention(u0, heads, outs):
                    for s in range(heads + 3):
                        if s < heads:
                            exps(u0 + s)
                        if 1 <= s <= heads:
                            u = u0 + s - 1
                            act.wait_ge(*after("pt", u))
                            if u >= 2:
                                act.wait_ge(*after("o", u - 2))
                            do(act.activation(PT[:, u % 2], PT_BANK[u % 2][:, :].rearrange("p (a b) -> p a b", a=2),
                                              ACT.Copy), "pt_copied", u)
                        if s >= 3:
                            outs(s - 3)

                def psum(*name):
                    return bank_of[name]

                def two(ps):
                    return ps[:, :].rearrange("p (a b) -> p a b", a=2)

                act.wait_ge(x_in, 32)
                sumsq(0, X)
                for b in range(2):
                    act.wait_ge(*after("filled", "g", 0, b))
                    do(act.activation(SIG[:, 2 * b:2 * b + 2, :], two(psum("g", 0, b)), ACT.Sigmoid),
                       "read", "g", 0, b)
                for t in range(TT):
                    copy_out(QK[:, t, 0:512], psum("q", 0, t)[:, :], "q", 0, t)
                for t in range(TT):
                    copy_out(QK[:, t, 512:1024], psum("k", 0, t)[:, :], "k", 0, t)
                act.wait_ge(mem_in, 32)
                act.wait_ge(*after("filled", "normT", 0, 1, 1))
                sumsq(1, MEM)
                for t in range(TT):
                    copy_out(V[:, t, :], psum("v", 0, t)[:, :], "v", 0, t)
                for i in range(2):
                    for b in range(2):
                        copy_out(XKT[:, 4 * i + 2 * b:4 * i + 2 * b + 2, :], two(psum("xk", i, b)), "xk", i, b)
                for b in range(4):
                    copy_out(QKT[:, 2 * b:2 * b + 2, :], two(psum("qkT", b)), "qkT", b)

                def outs1(h):
                    if h % 2:
                        copy_out(CAT[:, h // 2, :], psum("att_o", h // 2)[:, 0:S], "att_o", h // 2)

                attention(0, AH, outs1)
                for i in range(2):
                    for t in range(TT):
                        copy_out(XV[:, t, i * 512:(i + 1) * 512], psum("xv", i, t)[:, :], "xv", i, t)
                act.wait_ge(*after("read", "cmean"))
                do(act.activation(SIG[:, :, :], C[:, :, :], ACT.Square), "csq")
                act.wait_ge(*after("read", "cvar"))
                do(act.activation(U[:, 0, 0:S], U[:, 0, 0:S], ACT.Sqrt), "csd")
                act.wait_ge(*after("cnormed"))
                for i in range(4):
                    do(act.activation(CAT[:, 4 + i, :], C[:, i, :], ACT.Silu, bias=col("conv_ln_b", i),
                                      scale=col("conv_ln_g", i)), "convT")
                act.wait_ge(*after("read", "wout", 1, 1))
                sumsq(2, X)
                for i in range(2):
                    for b in range(2):
                        copy_out(XQT[:, 4 * i + 2 * b:4 * i + 2 * b + 2, :], two(psum("xq", i, b)), "xq", i, b)

                def outsx(h):
                    copy_out(CAT[:, 2 * h:2 * h + 2, :], two(psum("xatt_o", h)), "xatt_o", h)

                attention(AH, XH, outsx)
                act.wait_ge(*after("read", "xo", 1, 1))
                sumsq(3, X)
                n = 0
                for i in range(MLP_SLOTS):
                    for b in range(2):
                        act.wait_ge(*after("filled", "up", i, b))
                        if n >= 2:
                            act.wait_ge(*after("hidden", "mlp", (n - 2) // 2, n % 2))
                        do(act.activation(SG[:, n % 2, :], psum("up", i, b)[:, :], ACT.Relu), "read", "up", i, b)
                        n += 1
                act.wait_ge(*after("x", "mlp"))
                sumsq(4, X)
                if stop == 1:
                    return
                for l in range(LAYERS):
                    i0 = 5 + 2 * l
                    act.wait_ge(*after("x_final1") if l == 0 else after("x", "ffn"))
                    sumsq(i0, X)
                    for i in range(3):
                        copy_out(CI[:, 3 * i:3 * i + 2, 3:3 + S], two(psum("cqkv", l, i, 0)), "cqkv", l, i, 0)
                        copy_out(CI[:, 3 * i + 2, 3:3 + S], psum("cqkv", l, i, 1)[:, 0:S], "cqkv", l, i, 1)
                    copy_out(XP[:, :, 16:], two(psum("pool", l, 0, 0)), "pool", l, 0, 0)
                    for t in range(TT):
                        copy_out(ZAB[:, t, :], psum("zab", l, 0, t)[:, 0:HW + 12], "zab", l, 0, t)
                    for t in range(TT):
                        copy_out(FQ[:, t, 0:HW], psum("fq", l, 0, t)[:, 0:HW], "fq", l, 0, t)
                    for t in range(TT):
                        copy_out(FQ[:, t, HW:], psum("fk", l, 0, t)[:, 0:HW], "fk", l, 0, t)
                    for t in range(TT):
                        copy_out(FV[:, t, :], psum("fv", l, 0, t)[:, 0:HW + 6], "fv", l, 0, t)
                    for i in range(9):
                        act.wait_ge(*after("taps", l, i))
                        do(act.activation(CO[:, i, :], CO[:, i, :], ACT.Silu), "conv2", l, i)
                    own()
                    do(act.activation(ZAB[:, :, 0:HW], ZAB[:, :, 0:HW], ACT.Silu), "silu_z", l)
                    do(act.activation(SM[:, 2, 0:12].rearrange("p (t h) -> p t h", t=2), ZAB[:, :, HW + 6:],
                                      ACT.Sigmoid), "beta", l)
                    act.wait_ge(*after("absneg", l))
                    do(act.activation(SM[:, 5:7, 0:12], SM[:, 5:7, 0:12], ACT.Exp))
                    do(act.activation(SM[:, 7, 0:6], wide("dn_a_log_2", l, NH), ACT.Exp))
                    own()
                    do(act.activation(SM[:, 5:7, 0:12], SM[:, 5:7, 0:12], ACT.Ln, bias=1.0), "softlog", l)
                    act.wait_ge(*after("filled", "normT", i0, 1, 1))
                    do(act.activation(SQ[:, :, :], FQ[:, :, :], ACT.Square), "fx_sq", l)
                    for b in range(5):
                        n = 256 if b < 4 else P
                        copy_out(QT3[:, :, b * 256:b * 256 + n], two(psum("dnT", l, b))[:, :, 0:n], "dnT", l, b)
                    own()
                    act.wait_ge(*after("fx_ssum", l))
                    do(act.activation(SQ[:, :, :], QT3[:, :, 0:2 * HW], ACT.Square), "dn_sq", l)
                    act.wait_ge(*after("read", "cum", l))
                    do(act.activation(SM[:, 9, 0:12], SM[:, 8, 0:12], ACT.Exp))
                    do(act.activation(SM[:, 10, 0:6], SM[:, 11, 0:6], ACT.Exp), "expg", l)
                    for b in range(3):
                        copy_out(FT[:, 2 * b:2 * b + 2, :], two(psum("fT", l, b)), "fT", l, b)
                    for p in range(3):
                        copy_out(KQ[:, p].rearrange("p a b c -> p (a b c)"), psum("kqT", l, p)[:, :], "kqT", l, p)
                    for p in range(3):
                        copy_out(KT[:, p].rearrange("p a b -> p (a b)"), psum("kT", l, p)[:, 0:S], "kT", l, p)
                    act.wait_ge(*after("read", "grow", l, 3))
                    do(act.activation(DD[:, :, :], DD[:, :, :], ACT.Exp), "decay", l)

                    def outs2(h):
                        if h % 2:
                            copy_out(CAT[:, 3 + h // 2, :], psum("fx_o", l, h // 2)[:, 0:S], "fx_o", l, h // 2)

                    attention(AH + XH + NH * l, NH, outs2)
                    for lev in range(1, LEVELS):
                        for gi in range(3):
                            copy_out(PM[:, 4 * gi:4 * gi + 4, :],
                                     psum("invp", l, lev, gi)[:, :].rearrange("p (a b) -> p a b", a=4),
                                     "invp", l, lev, gi)
                    copy_out(VN[:, 0, :], psum("vn0", l)[:, 0:HW], "vn0", l)
                    copy_out(SST[:, :, :], psum("state", l)[:, 0:3 * HD].rearrange("p (a b) -> p a b", a=3), "state", l)
                    copy_out(O[:, 0, :], psum("o0", l)[:, 0:HW], "o0", l)
                    copy_out(VN[:, 1, :], psum("vn1", l)[:, 0:HW], "vn1", l)
                    act.wait_ge(*after("read", "o1", l))
                    do(act.activation(SQ[:, :, 0:HW], O[:, :, :], ACT.Square), "o_sq", l)
                    copy_out(CAT[:, 0:2, :], two(psum("dnoT", l, 0)), "dnoT", l, 0)
                    copy_out(CAT[:, 2, :], psum("dnoT", l, 1)[:, 0:S], "dnoT", l, 1)
                    act.wait_ge(*after("read", "wout2", l, 1, 1))
                    sumsq(i0 + 1, X)
                    if l == 0:
                        n = 0
                        for i in range(GU2):
                            for c in range(2):
                                act.wait_ge(*after("filled", "gu", i, c))
                                if n >= 2:
                                    act.wait_ge(*after("hidden", "ffn", (n - 2) // 2, n % 2))
                                do(act.activation(SG[:, n % 2, 0:S], psum("gu", i, c)[:, 0:S], ACT.Silu),
                                   "silu", "ffn", i, c)
                                n += 1
                        continue
                    act.wait_ge(*after("logit_shift"))
                    do(act.activation(SM[:, 3, :], SM[:, 2, :], ACT.Exp), "gate_exp")
                    act.wait_ge(*after("gates_ready"))
                    base = cact.n
                    job0 = points.get(("job0",), ("pe", 0))[1]
                    with act.Fori(0, NE) as e:
                        for i in range(6):
                            for c in range(2):
                                k_ = 2 * i + c
                                act.wait_ge(*in_loop(e, "pe", "filled", "moe", i, c))
                                act.wait_ge(*in_loop(e, "dve", "hidden", "moe", (k_ - 2) % 12 // 2, c,
                                                     before=k_ < 2))
                                ps = RING_BANK[(job0 + k_) % 4]
                                do(act.activation(SG[:, c, 0:S], ps[:, 0:S], ACT.Silu), "silu", "moe", i, c)
                    points[("per", "act")] = ("act", cact.n - base)
                    cact.n += (NE - 1) * (cact.n - base)

            @block.gpsimd
            def _(pool):
                def do(ins, *name):
                    ins.then_inc(*cpool.mark(*name))

                do(pool.memset(NHALF[:, :], -0.5), "nhalf")
                do(pool.memset(U[:, :, 0:PAD], 0.0))
                do(pool.memset(U[:, :, PAD + S:], 0.0), "u_padded")
                do(pool.memset(PW[:, :, :, :], 0.0), "poolw_zero")
                pool.wait_ge(*cpool.last())

                def power(n, need, *name):
                    pool.wait_ge(*after(*need))
                    do(pool.tensor_tensor(RS[:, 0:n], MS[:, 0:n], NHALF[:, 0:n], ALU.pow), *name)

                for i in range(5):
                    power(2, ("ms", i), "rstd", i)
                if stop == 1:
                    return
                for l in range(LAYERS):
                    power(2, ("ms", 5 + 2 * l), "rstd", 5 + 2 * l)
                    pool.wait_ge(*after("read", "pool", l, 0, 0))
                    do(pool.memset(XP[:, :, 0:16], 0.0))
                    do(pool.memset(SA[:, :, 0:16], 0.0))
                    do(pool.memset(SBf[:, :, 0:16], 0.0))
                    do(pool.memset(SC[:, :, 0:16], 0.0))
                    last = XP
                    for n, nxt in ((1, SA), (2, SBf), (4, SC)):
                        pool.wait_ge(*cpool.last())
                        do(pool.tensor_tensor(nxt[:, :, 16:], last[:, :, 16:], last[:, :, 16 - n:16 + S - n], ALU.add))
                        last = nxt
                    pool.wait_ge(*cpool.last())
                    for i, (half_, src) in enumerate(((slice(0, 64), SA), (slice(64, 128), SBf))):
                        do(pool.tensor_tensor(YP[half_, 0, :], src[half_, 0, 16:], poolinv[half_, 0, :], ALU.mult))
                    do(pool.tensor_tensor(YP[0:64, 1, :], SC[0:64, 1, 16:], poolinv[0:64, 1, :], ALU.mult))
                    pool.wait_ge(*cpool.last())
                    do(pool.tensor_tensor(SA[64:128, 1, 16:], SC[64:128, 1, 16:], SC[64:128, 1, 8:8 + S], ALU.add))
                    pool.wait_ge(*cpool.last())
                    do(pool.tensor_tensor(YP[64:128, 1, :], SA[64:128, 1, 16:], poolinv[64:128, 1, :], ALU.mult))
                    pool.wait_ge(*cpool.last())
                    do(pool.tensor_tensor(YP[:, :, :], YP[:, :, :], XP[:, :, 16:], ALU.subtract), "pooled", l)
                    power(24, ("fx_ms", l), "fx_rstd", l)
                    power(24, ("dn_ms", l), "dn_rstd", l)
                    power(12, ("o_ms", l), "o_rstd", l)
                    power(2, ("ms", 6 + 2 * l), "rstd", 6 + 2 * l)

            @block.vector
            def _(dve):
                def do(ins, *name):
                    ins.then_inc(*cdve.mark(*name))

                def own(back=0):
                    dve.wait_ge(*cdve.last(back))

                def psum(*name):
                    return bank_of[name]

                def norm(i, src, gain, gi, dst):
                    rows_norm(i, src)
                    for t in range(TT):
                        for b in range(2):
                            dve.wait_ge(*after("filled", "normT", i, t, b))
                            do(dve.tensor_tensor(dst[:, 4 * b:4 * b + 4, t * P:(t + 1) * P],
                                                 psum("normT", i, t, b)[:, :].rearrange("p (k n) -> p k n", k=4),
                                                 cols(gain, gi + 4 * b, 4).unsqueeze(2).broadcast_to([P, 4, P]),
                                                 ALU.mult), "read", "normT", i, t, b)
                    cdve.also("ht", i)

                def rows_norm(i, src, final=False):
                    dve.wait_ge(*after("ss", i, 1))
                    do(dve.tensor_scalar(MS[:, 0:TT], SS[:, 0:TT], 1.0 / D, EPS, ALU.mult, ALU.add), "ms", i)
                    dve.wait_ge(*after("rstd", i))
                    for t in range(TT):
                        if final:
                            do(dve.scalar_tensor_tensor(src[:, t, :], src[:, t, :], RS[:, t:t + 1],
                                                        wide("norm_final_g", 0, D), ALU.mult, ALU.mult), "xn", i, t)
                        else:
                            do(dve.tensor_scalar(XN[:, t, :], src[:, t, :], RS[:, t:t + 1], None, ALU.mult),
                               "xn", i, t)

                def add_residual(*name):
                    for i in range(2):
                        for t in range(TT):
                            dve.wait_ge(*after("filled", *name, i, t))
                            part = X[:, t, i * 512:(i + 1) * 512]
                            do(dve.tensor_tensor(part, psum(*name, i, t)[:, :], part, ALU.add), "read", *name, i, t)

                def add_banks(*name):
                    for b in range(4):
                        part = X[:, b // 2, (b % 2) * 512:(b % 2 + 1) * 512]
                        do(dve.tensor_tensor(part, banks[b][:, :], part, ALU.add))
                    cdve.also(*name)

                def attention(u0, heads, scale, mask):
                    for s in range(heads + 1):
                        if s < heads:
                            u = u0 + s
                            dve.wait_ge(*after("scores", u))
                            if u >= 3:
                                dve.wait_ge(*after("pt", u - 3))
                            ps = SC_BANK[u % 2][:, :]
                            pr = PR[:, u % 3].rearrange("p a b -> p (a b)")
                            if mask is None:
                                do(dve.tensor_scalar(pr, ps, scale, None, ALU.mult), "scores_read", u)
                            else:
                                do(dve.scalar_tensor_tensor(pr, ps, scale, mask.rearrange("p a b -> p (a b)"),
                                                            ALU.mult, ALU.add), "scores_read", u)
                            own()
                            do(dve.tensor_reduce(NM[:, u % 3, :], PR[:, u % 3], AX.X, ALU.max, negate=True),
                               "negmax", u)
                        if s >= 1:
                            u = u0 + s - 1
                            dve.wait_ge(*after("exp", u, 1))
                            do(dve.reciprocal(RDEN[:, u % 3, :], DEN[:, u % 3, :]))
                            own()
                            for t in range(TT):
                                do(dve.tensor_scalar(PR[:, u % 3, t, :], PR[:, u % 3, t, :],
                                                     RDEN[:, u % 3, t:t + 1], None, ALU.mult), "probs", u)

                dve.wait_ge(*after("filled", "cols"))
                do(dve.tensor_copy(COL[:, :], psum("cols")[:, 0:NCOLS]), "read", "cols")
                own()
                dve.wait_ge(*after("nhalf"))
                norm(0, X, "norm_mix_g", 0, HT)
                dve.wait_ge(*after("u_padded"))
                for b in range(2):
                    dve.wait_ge(*after("filled", "a", 0, b))
                    dve.wait_ge(*after("read", "g", 0, b))
                    do(dve.tensor_tensor(U[:, 2 * b:2 * b + 2, PAD:PAD + S],
                                         psum("a", 0, b)[:, :].rearrange("p (a b) -> p a b", a=2),
                                         SIG[:, 2 * b:2 * b + 2, :], ALU.mult), "read", "a", 0, b)
                own()
                def conv_taps(lo, hi):
                    for k in range(lo, hi):
                        for i in range(4):
                            w = col("conv_w", 4 * k + i)
                            if k == 0:
                                do(dve.tensor_scalar(C[:, i, :], U[:, i, 0:S], w, col("conv_b", i), ALU.mult, ALU.add))
                            else:
                                own(3)
                                do(dve.scalar_tensor_tensor(C[:, i, :], U[:, i, k:k + S], w, C[:, i, :],
                                                            ALU.mult, ALU.add))

                conv_taps(0, 20)
                rows_norm(1, MEM)
                for n in (0, 1):
                    dve.wait_ge(*after("read", "q" if n == 0 else "k", 0, 1))
                dve.wait_ge(table_in, 16)
                own()
                heads = QK.rearrange("p t (h c) -> p t h c", c=HD)
                x1, x2 = heads[:, :, :, 0:8], heads[:, :, :, 8:16]
                cb = cos.unsqueeze(2).broadcast_to([P, TT, 16, 8])
                sbr = sin.unsqueeze(2).broadcast_to([P, TT, 16, 8])
                r = [RT1[:, i, :].rearrange("p (t h c) -> p t h c", t=TT, h=16) for i in range(4)]
                do(dve.tensor_tensor(r[0], x1, cb, ALU.mult))
                do(dve.tensor_tensor(r[1], x2, sbr, ALU.mult))
                do(dve.tensor_tensor(r[2], x2, cb, ALU.mult))
                do(dve.tensor_tensor(r[3], x1, sbr, ALU.mult))
                own()
                do(dve.tensor_tensor(x1, r[0], r[1], ALU.subtract))
                do(dve.tensor_tensor(x2, r[2], r[3], ALU.add), "rotated")
                for t in range(TT):
                    for b in range(2):
                        dve.wait_ge(*after("filled", "normT", 1, t, b))
                        do(dve.tensor_tensor(MT[:, 4 * b:4 * b + 4, t * P:(t + 1) * P],
                                             psum("normT", 1, t, b)[:, :].rearrange("p (k n) -> p k n", k=4),
                                             cols("norm_mem_g", 4 * b, 4).unsqueeze(2).broadcast_to([P, 4, P]),
                                             ALU.mult), "read", "normT", 1, t, b)
                cdve.also("ht", 1)
                conv_taps(20, TAPS)
                cdve.also("conv")
                attention(0, AH, 0.125, logc)
                dve.wait_ge(*after("filled", "cmean"))
                do(dve.tensor_tensor(C[:, :, :], C[:, :, :],
                                     psum("cmean")[:, 0:S].unsqueeze(1).broadcast_to([P, 4, S]), ALU.subtract),
                   "read", "cmean")
                dve.wait_ge(*after("filled", "cvar"))
                do(dve.tensor_scalar(U[:, 0, 0:S], psum("cvar")[:, 0:S], EPS, None, ALU.add), "read", "cvar")
                dve.wait_ge(*after("csd"))
                do(dve.reciprocal(U[:, 1, 0:S], U[:, 0, 0:S]))
                own()
                do(dve.tensor_tensor(C[:, :, :], C[:, :, :],
                                     U[:, 1, 0:S].unsqueeze(1).broadcast_to([P, 4, S]), ALU.mult), "cnormed")
                add_residual("wout")
                norm(2, X, "norm_x_g", 0, HT)
                attention(AH, XH, 0.0625, None)
                add_residual("xo")
                norm(3, X, "norm_mlp_g", 0, HT)
                for i in range(MLP_SLOTS):
                    for b in range(2):
                        n = 2 * i + b
                        dve.wait_ge(*after("read", "up", i, b))
                        if i >= 3:
                            dve.wait_ge(*after("down", "mlp", i - 3))
                        sg = SG[:, n % 2, :].rearrange("p (a b) -> p a b", a=2)
                        do(dve.tensor_tensor(UH[:, i % 3, 2 * b:2 * b + 2, :], sg, sg, ALU.mult),
                           "hidden", "mlp", i, b)
                dve.wait_ge(*after("down", "mlp", MLP_SLOTS - 1))
                add_banks("x", "mlp")
                dve.wait_ge(wide_in, 16 * 8)
                rows_norm(4, X, final=True)
                cdve.also("x_final1")
                if stop == 1:
                    cdve.also("x_final")
                    return

                for l in range(LAYERS):
                    i0 = 5 + 2 * l
                    norm(i0, X, "norm1_2", 8 * l, HT)
                    do(dve.memset(CI[:, :, 0:3], 0.0))
                    own()
                    for i in range(9):
                        dve.wait_ge(*after("read", "cqkv", l, i // 3, (i % 3) // 2))
                        for k in range(DTAPS):
                            w = col("dn_conv_2", 36 * l + 9 * k + i)
                            if k == 0:
                                do(dve.tensor_scalar(CO[:, i, :], CI[:, i, 0:S], w, None, ALU.mult))
                            else:
                                own()
                                do(dve.scalar_tensor_tensor(CO[:, i, :], CI[:, i, k:k + S], w, CO[:, i, :],
                                                            ALU.mult, ALU.add), "taps", l, i)
                    dve.wait_ge(*after("read", "fv", l, 0, 1))
                    dve.wait_ge(*after("beta", l))

                    def six(v):
                        return v.rearrange("p (t h) -> p t h", t=TT)

                    def bc6(v):
                        return v.unsqueeze(1).broadcast_to([P, TT, NH])

                    do(dve.tensor_tensor(six(SM[:, 3, 0:12]), ZAB[:, :, HW:HW + 6], bc6(wide("dn_dt_bias_2", l, NH)),
                                         ALU.add))
                    do(dve.tensor_tensor(six(SM[:, 4, 0:12]), FV[:, :, HW:HW + 6], bc6(wide("fx_f_bias_2", l, NH)),
                                         ALU.add))
                    own()
                    do(dve.tensor_scalar(SM[:, 4, 0:12], SM[:, 4, 0:12], -1.0, None, ALU.mult))
                    own()
                    do(dve.tensor_scalar(SM[:, 12:14, 0:12], SM[:, 3:5, 0:12], -1.0, None, ALU.mult))
                    own()
                    do(dve.tensor_tensor(SM[:, 5:7, 0:12], SM[:, 3:5, 0:12], SM[:, 12:14, 0:12], ALU.min), "absneg", l)
                    dve.wait_ge(*after("softlog", l))
                    do(dve.scalar_tensor_tensor(SM[:, 0:2, 0:12], SM[:, 3:5, 0:12], 0.0, SM[:, 5:7, 0:12],
                                                ALU.max, ALU.add))
                    own()
                    do(dve.scalar_tensor_tensor(six(SM[:, 0, 0:12]), six(SM[:, 0, 0:12]), -1.0, bc6(SM[:, 7, 0:6]),
                                                ALU.mult, ALU.mult), "gates", l)
                    dve.wait_ge(*after("filled", "poolw", l))
                    for i in range(2):
                        do(dve.tensor_scalar(CAT[:, 6 + i, :], psum("poolw", l)[:, i * S:(i + 1) * S],
                                             col("pool_scale_2", 2 * l + i), None, ALU.mult), "read", "poolw", l)

                    def head_norm(name, src, scale_q, width, sq_done, div, last_name):
                        n = TT * width
                        dve.wait_ge(*after(*sq_done))
                        sq = SQ[:, :, 0:width * HD].rearrange("p t (h c) -> p t h c", c=HD)
                        do(dve.tensor_reduce(SS[:, 0:n].rearrange("p (t h) -> p t h", t=TT), sq, AX.X, ALU.add),
                           name + "_ssum", l)
                        own()
                        do(dve.tensor_scalar(MS[:, 0:n], SS[:, 0:n], 1.0 / div, EPS, ALU.mult, ALU.add),
                           name + "_ms", l)
                        dve.wait_ge(*after(name + "_rstd", l))
                        rs = RS[:, 0:n].rearrange("p (t h) -> p t h", t=TT)
                        if scale_q != 1.0:
                            do(dve.tensor_scalar(rs[:, :, 0:NH], rs[:, :, 0:NH], scale_q, None, ALU.mult))
                            own()
                        v = src.rearrange("p t (h c) -> p t h c", c=HD)
                        do(dve.tensor_tensor(v, v, rs.unsqueeze(3).broadcast_to([P, TT, width, HD]), ALU.mult),
                           last_name, l)

                    head_norm("fx", FQ, 1.0, 12, ("fx_sq", l), HD, "fx_scaled")
                    own()
                    for i, name in enumerate(("fx_qnorm_2", "fx_knorm_2")):
                        for t in range(TT):
                            v = FQ[:, t, i * HW:(i + 1) * HW].rearrange("p (h c) -> p h c", c=HD)
                            do(dve.tensor_tensor(v, v, wide(name, l, HD).unsqueeze(1).broadcast_to([P, NH, HD]),
                                                 ALU.mult), "fx_normed", l)
                    dve.wait_ge(*after("filled", "cum", l))
                    ps = psum("cum", l)
                    do(dve.tensor_copy(GT, ps[0:NH, 128:128 + S]))
                    do(dve.tensor_copy(SM[:, 8, 0:12], ps[:, 0:12]))
                    own()
                    do(dve.scalar_tensor_tensor(SM[:, 11, 0:6], SM[:, 8, 0:6], -1.0, ps[:, 16:22], ALU.mult, ALU.add),
                       "read", "cum", l)
                    dve.wait_ge(*after("filled", "ncum", l))
                    do(dve.tensor_scalar(NCT, psum("ncum", l)[0:NH, 0:S], 8.0, None, ALU.mult), "read", "ncum", l)
                    head_norm("dn", QT3[:, :, 0:2 * HW], HD ** -0.5, 12, ("dn_sq", l), 1.0, "dn_scaled")
                    own()
                    beta = six(SM[:, 2, 0:12])

                    def heads3(v):
                        return v.rearrange("p t (h c) -> p t h c", c=HD)

                    bb = beta.unsqueeze(3).broadcast_to([P, TT, NH, HD])
                    do(dve.tensor_tensor(heads3(KB), heads3(QT3[:, :, HW:2 * HW]), bb, ALU.mult), "dn_ready", l)
                    do(dve.tensor_tensor(heads3(BV), heads3(QT3[:, :, 2 * HW:]), bb, ALU.mult), "bv", l)
                    dve.wait_ge(*after("expg", l))
                    do(dve.tensor_tensor(KDC.rearrange("p (h c) -> p h c", c=HD),
                                         QT3[:, 0, HW:2 * HW].rearrange("p (h c) -> p h c", c=HD),
                                         SM[:, 10, 0:6].unsqueeze(2).broadcast_to([P, NH, HD]), ALU.mult), "kdc", l)
                    for b in range(4):
                        dve.wait_ge(*after("filled", "grow", l, b))
                        for c in range(3):
                            s = 3 * b + c
                            t, h = chunk_head(s)
                            do(dve.tensor_scalar(DD[:, s, :], psum("grow", l, b)[:, c * P:(c + 1) * P],
                                                 SM[:, 8, NH * t + h:NH * t + h + 1], 0.0, ALU.subtract, ALU.min), "read", "grow", l, b)
                    dve.wait_ge(*after("decay", l))
                    do(dve.tensor_tensor(DD[:, :, :], DD[:, :, :], upper.unsqueeze(1).broadcast_to([P, 12, P]),
                                         ALU.mult))
                    own()
                    for b in range(6):
                        dve.wait_ge(*after("filled", "aq", l, b))
                        do(dve.tensor_tensor(AQ[:, 2 * b:2 * b + 2],
                                             psum("aq", l, b)[:, :].rearrange("p (a b c) -> p a b c", a=2, b=2),
                                             DD[:, 2 * b:2 * b + 2, :].unsqueeze(2).broadcast_to([P, 2, 2, P]),
                                             ALU.mult), "read", "aq", l, b)
                    attention(AH + XH + NH * l, NH, 0.125, causal)

                    def level_mask(lev, gi):
                        do(dve.tensor_tensor(LT[:, 4 * gi:4 * gi + 4, :], AQ[:, 4 * gi:4 * gi + 4, 0, :],
                                             levels[:, lev, :].unsqueeze(1).broadcast_to([P, 4, P]), ALU.mult),
                           "level", l, lev, gi)

                    idb = ident.unsqueeze(1).broadcast_to([P, 4, P])
                    for gi in range(3):
                        level_mask(0, gi)
                    own()
                    for gi in range(3):
                        do(dve.tensor_tensor(DIT[:, 4 * gi:4 * gi + 4, :], idb, LT[:, 4 * gi:4 * gi + 4, :],
                                             ALU.subtract))
                    for gi in range(3):
                        g4 = slice(4 * gi, 4 * gi + 4)
                        dve.wait_ge(*after("filled", "inv0", l, gi))
                        do(dve.tensor_tensor(DI[:, g4, :], idb,
                                             psum("inv0", l, gi)[:, :].rearrange("p (a b) -> p a b", a=4),
                                             ALU.subtract), "read", "inv0", l, gi)
                        cdve.also("inv", l, 0, gi)
                        own()
                        level_mask(1, gi)
                    for lev in range(1, LEVELS):
                        for gi in range(3):
                            g4 = slice(4 * gi, 4 * gi + 4)
                            names = (("invd", DI), ("invt", DIT)) if lev < LEVELS - 1 else (("invt", DIT),)
                            for name, dst in names:
                                dve.wait_ge(*after("filled", "invt", l, lev, gi))
                                do(dve.tensor_tensor(dst[:, g4, :], dst[:, g4, :],
                                                     psum(name, l, lev, gi)[:, :].rearrange("p (a b) -> p a b", a=4),
                                                     ALU.subtract), "read", name, l, lev, gi)
                            cdve.also("inv", l, lev, gi)
                            if lev < LEVELS - 1:
                                level_mask(lev + 1, gi)
                    def h6(v):
                        return v.rearrange("p (h c) -> p h c", c=HD)

                    def parity(v, par):
                        return v.rearrange("p (g two c) -> p g two c", two=2, c=HD)[:, :, par, :]

                    for par in range(2):
                        eg = SM[:, 9, 6:12].rearrange("p (g two) -> p g two", two=2)[:, :, par].unsqueeze(2)\
                            .broadcast_to([P, 3, HD])
                        dve.wait_ge(*after("filled", "ks", l, par))
                        ps = psum("ks", l, par)
                        do(dve.tensor_tensor(parity(VN[:, 1, :], par), h6(ps[:, 0:3 * HD]), eg, ALU.mult))
                        do(dve.tensor_tensor(parity(O[:, 1, :], par), h6(ps[:, 3 * HD:6 * HD]), eg, ALU.mult),
                           "read", "ks", l, par)
                    own()
                    do(dve.tensor_tensor(BV[:, 1, :], BV[:, 1, :], VN[:, 1, :], ALU.subtract), "bv1", l)
                    dve.wait_ge(*after("filled", "o1", l))
                    do(dve.tensor_tensor(O[:, 1, :], psum("o1", l)[:, 0:HW], O[:, 1, :], ALU.add), "read", "o1", l)
                    dve.wait_ge(*after("silu_z", l))
                    head_norm("o", O, 1.0, NH, ("o_sq", l), HD, "o_scaled")
                    own()
                    for t in range(TT):
                        v = h6(O[:, t, :])
                        do(dve.tensor_tensor(v, v, wide("dn_onorm_2", l, HD).unsqueeze(1).broadcast_to([P, NH, HD]),
                                             ALU.mult))
                    own()
                    do(dve.tensor_tensor(O[:, :, :], O[:, :, :], ZAB[:, :, 0:HW], ALU.mult), "dn_out", l)
                    add_residual("wout2", l)
                    norm(i0 + 1, X, "norm2_2", 8 * l, HT)
                    if l == 0:
                        for i in range(GU2):
                            for c in range(2):
                                n = 2 * i + c
                                dve.wait_ge(*after("silu", "ffn", i, c))
                                if i // 2 >= 3:
                                    dve.wait_ge(*after("down", "ffn", i // 2 - 3))
                                do(dve.tensor_tensor(UH[:, i // 2 % 3, 2 * (i % 2) + c, :], SG[:, n % 2, 0:S],
                                                     psum("gu", i, c)[:, S:2 * S], ALU.mult), "hidden", "ffn", i, c)
                                cdve.also("read", "gu", i, c)
                        dve.wait_ge(*after("down", "ffn", DN2 - 1))
                        add_banks("x", "ffn")
                        continue

                    LG = GATE
                    dve.wait_ge(*after("filled", "router"))
                    do(dve.tensor_copy(LG[:, :, :], psum("router")[:, 0:TT * NE].rearrange("p (t e) -> p t e", t=TT)),
                       "read", "router")
                    RKs = SM[:, 0, :].rearrange("p (t e) -> p t e", t=TT)
                    lane = SM[:, 1, 0:NE]
                    hot = SM[:, 4, :].rearrange("p (t e) -> p t e", t=TT)
                    hot2 = SM[:, 5, :].rearrange("p (t e) -> p t e", t=TT)
                    cur = SM[:, 6, :].rearrange("p (t e) -> p t e", t=TT)
                    m1, m2, mr = SM[:, 7, 0:2], SM[:, 7, 2:4], SM[:, 7, 4:6]
                    for k in range(NE):
                        do(dve.memset(lane[:, k:k + 1], float(NE - k)))
                    own()

                    def bce(v):
                        return v.unsqueeze(2).broadcast_to([P, TT, NE])

                    def one_hot(src, m, dst):
                        do(dve.tensor_reduce(m, src, AX.X, ALU.max))
                        own()
                        do(dve.tensor_tensor(RKs, src, bce(m), ALU.is_equal))
                        own()
                        do(dve.tensor_tensor(RKs, RKs, lane.unsqueeze(1).broadcast_to([P, TT, NE]), ALU.mult))
                        own()
                        do(dve.tensor_reduce(mr, RKs, AX.X, ALU.max))
                        own()
                        do(dve.tensor_tensor(dst, RKs, bce(mr), ALU.is_equal))
                        own()

                    one_hot(LG, m1, hot)
                    do(dve.scalar_tensor_tensor(cur, hot, NEG, LG, ALU.mult, ALU.add))
                    own()
                    one_hot(cur, m2, hot2)
                    do(dve.tensor_tensor(hot, hot, hot2, ALU.add))
                    do(dve.tensor_tensor(SM[:, 2, :].rearrange("p (t e) -> p t e", t=TT), LG, bce(m1), ALU.subtract),
                       "logit_shift")
                    dve.wait_ge(*after("gate_exp"))
                    own()
                    ex = SM[:, 3, :].rearrange("p (t e) -> p t e", t=TT)
                    do(dve.tensor_tensor(ex, ex, hot, ALU.mult))
                    own()
                    do(dve.tensor_reduce(mr, ex, AX.X, ALU.add))
                    own()
                    do(dve.reciprocal(m2, mr))
                    own()
                    do(dve.tensor_tensor(GATE[:, :, :], ex, bce(m2), ALU.mult), "gates_ready")
                    own()
                    base = cdve.n
                    job0 = points.get(("job0",), ("pe", 0))[1]
                    GE = SM[:, 8, 0:TT]
                    with dve.Fori(0, NE) as e:
                        dve.wait_ge(*in_loop(e, "dve", "moe_added", 3, before=True))
                        do(dve.tensor_copy(GE.unsqueeze(2), GATE[:, :, bass.ds(e, 1)]), "gate_copied")
                        dve.wait_ge(*in_loop(e, "dve", "gate_copied"))
                        for i in range(6):
                            for c in range(2):
                                dve.wait_ge(*in_loop(e, "act", "silu", "moe", i, c))
                                k_ = 2 * i + c
                                if c == 0 and i % 2 == 0:
                                    dve.wait_ge(*in_loop(e, "pe", "down", "moe", i // 2, before=True))
                                ps = RING_BANK[(job0 + k_) % 4]
                                do(dve.tensor_tensor(UH[:, i // 2, 2 * (i % 2) + c, :], SG[:, c, 0:S],
                                                     ps[:, S:2 * S], ALU.mult), "hidden", "moe", i, c)
                        dve.wait_ge(*in_loop(e, "pe", "down", "moe", 2))
                        for b in range(4):
                            t = b // 2
                            part = X[:, t, (b % 2) * 512:(b % 2 + 1) * 512]
                            do(dve.scalar_tensor_tensor(part, banks[b][:, :], GE[:, t:t + 1], part,
                                                        ALU.mult, ALU.add), "moe_added", b)
                    points[("per", "dve")] = ("dve", cdve.n - base)
                    cdve.n += (NE - 1) * (cdve.n - base)
                    cdve.also("x_final")


_INS = ['x', 'mem', 'norm_mix_g', 'w_in', 'conv_w', 'conv_b', 'conv_ln_g', 'conv_ln_b', 'w_out', 'norm_x_g',
        'norm_mem_g', 'w_xq', 'w_xk', 'w_xv', 'w_xo', 'norm_mlp_g', 'w_up', 'w_down', 'norm_final_g', 'norm1_2',
        'w_in_2', 'dn_conv_2', 'dn_a_log_2', 'dn_dt_bias_2', 'dn_onorm_2', 'fx_qnorm_2', 'fx_knorm_2',
        'fx_f_bias_2', 'pool_w_2', 'pool_scale_2', 'w_out_2', 'norm2_2', 'ffn_gate_2', 'ffn_up_2', 'ffn_down_2',
        'router_2', 'moe_gate_2', 'moe_up_2', 'moe_down_2']
_OUTS = [((1, S, D), 'float32')]
STOP = 0


def kernel(**inputs):
    import numpy as _np
    import concourse.bacc as _bacc
    from concourse import mybir as _mybir
    from concourse.bass_utils import run_bass_kernel_spmd as _run

    arrays = {f"in_{name}_dram": _np.ascontiguousarray(inputs[name]) for name in _INS}
    arrays["in_table_dram"] = table()
    points = {}
    for _ in range(2):
        nc = _bacc.Bacc("TRN2", target_bir_lowering=False, num_devices=1)
        args = {name[3:-5]: nc.dram_tensor(name, a.shape, _mybir.dt.from_np(a.dtype), kind="ExternalInput").ap()
                for name, a in arrays.items()}
        outs = [nc.dram_tensor(f"out_{i}_dram", shape, _mybir.dt.from_np(_np.dtype(dtype)), kind="ExternalOutput").ap()
                for i, (shape, dtype) in enumerate(_OUTS)]
        program(nc, args, outs[0], points, STOP)
    r = _run(nc, [arrays], core_ids=[0])
    return r.results[0]["out_0_dram"]
```

```python
import numpy as np
import concourse.bass as bass
from concourse import mybir
from contextlib import ExitStack

F32 = mybir.dt.float32
ACT = mybir.ActivationFunctionType
ALU = mybir.AluOpType
AX = mybir.AxisListType

P = 128
S = 256
TT = S // P
D = 1024
KD_ = D // P
HD = 64
EPS = 1e-6
NEG = -1e30
ATT = 512
AH = ATT // HD
TAPS = 31
PAD = TAPS // 2
XH = 4
MLP_SLOTS = 8
LAYERS = 2
NH = 6
HW = NH * HD
DTAPS = 4
FF2 = 2816
FFE = 1536
NE = 8
TOP = 2
MORE = (TOP * S - 1) // (P + 1) if TOP * S < NE * (P + 1) else NE
RING = 3
SLOT = 4096
LEVELS = 7

TABLE = {}
TABLE_COLS = 0
for _name, _n in (("ident", P), ("logc", TT * S), ("causal", TT * S), ("upper", P), ("ones", P),
                  ("levels", LEVELS * P), ("poolinv", TT * S), ("cos", TT * 8), ("sin", TT * 8),
                  ("mean", P), ("iota", P), ("sel", NH * P)):
    TABLE[_name] = (TABLE_COLS, _n)
    TABLE_COLS += _n


def table():
    t = np.zeros((P, TABLE_COLS), np.float32)

    def put(name, a):
        at, n = TABLE[name]
        t[:a.shape[0], at:at + n] = a.reshape(a.shape[0], n)

    p = np.arange(P)
    put("ident", np.eye(P))
    q = (np.arange(TT)[None, :, None] * P + p[:, None, None])
    k = np.arange(S)[None, None, :]
    count = (np.abs(q - k) <= 64).astype(int) + ((q - k) % 4 == 0) + ((q - k) % 16 == 0)
    put("logc", np.where(count > 0, np.log(np.maximum(count, 1)), NEG))
    put("causal", np.where(k <= q, 0.0, NEG))
    put("upper", p[:, None] <= p[None, :])
    put("ones", np.ones((P, P)))
    lev = []
    for n in range(LEVELS):
        b = 1 << n
        j, i = p[:, None], p[None, :]
        lev.append((j // (2 * b) == i // (2 * b)) & (j // b % 2 == 0) & (i // b % 2 == 1))
    put("levels", np.stack(lev, 1))
    win = np.array([[2, 4], [8, 16]])[:, p // 64].T
    put("poolinv", 1.0 / np.minimum(np.arange(S)[None, None, :] + 1, win[:, :, None]))
    freqs = (np.float32(500000.0) ** (-np.arange(0, 16, 2, dtype=np.float32) / np.float32(16))).astype(np.float32)
    ang = (np.arange(S, dtype=np.float32)[:, None] * freqs[None, :]).astype(np.float32)
    ang = ang.reshape(TT, P, 8).transpose(1, 0, 2)
    put("cos", np.cos(ang))
    put("sin", np.sin(ang))
    put("mean", np.full((P, P), 1.0 / ATT))
    put("iota", np.tile(np.arange(P), (P, 1)))
    sel = np.zeros((NH, NH, P))
    sel[np.arange(NH), np.arange(NH)] = 1.0
    put("sel", sel)
    return t


ROWS = [
    [("norm_mix_g", 8), ("norm_x_g", 8), ("norm_mem_g", 8), ("norm_mlp_g", 8), ("norm1_2", 16), ("norm2_2", 16)],
    [("conv_w", 124)],
    [("conv_b", 4), ("conv_ln_g", 4), ("conv_ln_b", 4), ("pool_scale_2", 4), ("dn_conv_2", 72)],
]
COLS = {}
_at = 0
for _tile in ROWS:
    for _name, _n in _tile:
        COLS[_name] = _at
        _at += _n
NCOLS = _at

WIDE = {}
_at = 0
for _name, _n in (("norm_final_g", D), ("fx_qnorm_2", LAYERS * HD), ("fx_knorm_2", LAYERS * HD),
                  ("dn_onorm_2", LAYERS * HD), ("dn_a_log_2", LAYERS * NH), ("dn_dt_bias_2", LAYERS * NH),
                  ("fx_f_bias_2", LAYERS * NH)):
    WIDE[_name] = (_at, _n)
    _at += _n
NWIDE = _at


class Counter:

    def __init__(self, sem, key, points):
        self.sem, self.key, self.points, self.n = sem, key, points, 0

    def mark(self, *name):
        self.n += 1
        if name:
            self.points[name] = (self.key, self.n)
        return self.sem, 1

    def also(self, *name):
        self.points[name] = (self.key, self.n)

    def last(self, back=0):
        return self.sem, self.n - back


def program(nc, A, out, points, stop):
    ctx = ExitStack()
    with ctx:
        def sb(name, shape, dt=F32):
            return ctx.enter_context(nc.sbuf_tensor(name, shape, dt))

        def sem(name):
            return ctx.enter_context(nc.semaphore(name))

        T_ = sb("shape_table", [P, TABLE_COLS])
        X = sb("residual", [P, TT, D])
        XN = sb("normed", [P, TT, D])
        HT = sb("normedT", [P, KD_, S])
        CAT = sb("mixedT", [P, KD_, S])
        W = sb("weights", [P, RING, SLOT])
        GR = sb("vector_rows", [P, 3, P])
        COL = sb("vector_cols", [P, NCOLS])
        WD = sb("vector_wide", [P, NWIDE])
        PR = sb("probs", [P, 3, TT, S])
        PT = sb("probsT", [P, 2, TT, S])
        PW = sb("pool_weights", [P, LAYERS, 2, P])
        RT = sb("router", [P, KD_, NE])
        NHALF = sb("minus_half", [P, 24])
        SS = sb("sumsq", [P, 24])
        MS = sb("meansq", [P, 24])
        RS = sb("rstd", [P, 24])
        NM = sb("negmax", [P, 3, TT])
        DEN = sb("den", [P, 3, TT])
        RDEN = sb("rden", [P, 3, TT])
        SM = sb("small", [P, 16, 16])
        ARENA = sb("arena", [P, 22300])
        ITEM = sb("items", [1, 16], mybir.dt.int32)

        def ar(at, *shape):
            n = int(np.prod(shape))
            v = ARENA[:, at:at + n]
            if len(shape) == 2:
                v = v.rearrange("p (a b) -> p a b", a=shape[0])
            elif len(shape) == 3:
                v = v.rearrange("p (a b c) -> p a b c", a=shape[0], b=shape[1])
            elif len(shape) == 4:
                v = v.rearrange("p (a b c d) -> p a b c d", a=shape[0], b=shape[1], c=shape[2])
            return v

        QK = ar(0, TT, 1024)
        QKT = ar(2048, 8, S)
        V = ar(4096, TT, ATT)
        U = ar(5120, 4, S + 2 * PAD)
        C = ar(6264, 4, S)
        SIG = ar(7288, 4, S)
        MT = ar(8312, 8, S)
        XKT = ar(10360, 8, S)
        XV = ar(12408, TT, 1024)
        XQT = ar(14456, 8, S)
        MEM = ar(12408, TT, 1024)
        RT1 = ar(16504, 4, 256)
        UH = ar(0, 3, 4, S)
        SG = ar(3072, 2, 2 * S)
        CI = ar(0, 9, S + 4)
        CO = ar(2340, 9, S)
        KB = ar(0, TT, HW)
        DI = ar(0, 12, P)
        DIT = ar(1536, 12, P)
        PM = ar(3072, 12, P)
        QT3 = ar(4644, TT, 3 * HW)
        ZAB = ar(6948, TT, HW + 12)
        FQ = ar(7740, TT, 2 * HW)
        FV = ar(9276, TT, HW + 6)
        KQ = ar(10056, 3, TT, 2, P)
        KT = ar(11592, 3, TT, P)
        DD = ar(12360, 12, P)
        AQ = ar(13896, 12, 2, P)
        XP = ar(13896, 2, 16 + S)
        SA = ar(13896 + 544, 2, 16 + S)
        SBf = ar(13896 + 1088, 2, 16 + S)
        SC = ar(13896 + 1632, 2, 16 + S)
        YP = ar(13896 + 2176, 2, S)
        LT = HT[:, 0:6, :].rearrange("p a (b c) -> p (a b) c", c=P)
        O = ar(16968, TT, HW)
        VN = ar(17736, TT, HW)
        BV = ar(18504, TT, HW)
        KDC = ar(19272, HW)
        FT = ar(19656, 6, S)
        NCT = ARENA[0:NH, 21192:21192 + S]
        GT = ARENA[0:NH, 21448:21448 + S]
        SST = ar(21704, 3, HD)
        GATE = ar(21896, TT, NE)
        GSEL = ar(0, TT, P)
        GGATE = ar(256, TT, P)
        HG = ar(512, KD_, P)
        GST = ar(1536, TT, P)
        SGE = ar(1792, 3, 512)
        HH = ar(3328, 3, 512)
        HHT = ar(4864, 12, P)
        Y = ar(6400, 2, 512)
        PG = ar(7424, NE + MORE + 1, 4)
        PC = ar(7500, 8)
        SQ = XN[:, :, 0:2 * HW]

        def system(t, h):
            return (h % 2) * NH + t * (NH // 2) + h // 2

        def chunk_head(s):
            return s % NH // (NH // 2), 2 * (s % (NH // 2)) + s // NH

        ident = T_[:, 0:P]

        def tab(name, n=P):
            return T_[0:n, TABLE[name][0]:TABLE[name][0] + TABLE[name][1]]

        logc = tab("logc").rearrange("p (t k) -> p t k", t=TT)
        causal = tab("causal").rearrange("p (t k) -> p t k", t=TT)
        upper, ones, mean_w, iota = tab("upper"), tab("ones"), tab("mean"), tab("iota")
        upper_ones = T_[:, TABLE["upper"][0]:TABLE["upper"][0] + 2 * P]
        levels = tab("levels").rearrange("p (n k) -> p n k", n=LEVELS)
        poolinv = tab("poolinv").rearrange("p (t k) -> p t k", t=2)
        cos = tab("cos").rearrange("p (t k) -> p t k", t=TT)
        sin = tab("sin").rearrange("p (t k) -> p t k", t=TT)
        sel = tab("sel", NH).rearrange("p (h k) -> p h k", h=NH)

        def col(name, i=0):
            return COL[:, COLS[name] + i:COLS[name] + i + 1]

        def cols(name, i, n):
            return COL[:, COLS[name] + i:COLS[name] + i + n]

        def wide(name, l, n):
            at = WIDE[name][0] + l * n
            return WD[:, at:at + n]

        banks = [ctx.enter_context(nc.psum_tensor(f"bank{i}", [P, 512], F32)) for i in range(8)]
        SC_BANK, PT_BANK, RING_BANK = banks[0:2], banks[2:4], banks[4:8]

        matmul_done, scalar_done = sem("matmul_done"), sem("scalar_done")
        vector_done, pool_done = sem("vector_done"), sem("pool_done")
        x_in, mem_in, rows_in, table_in = sem("x_in"), sem("mem_in"), sem("rows_in"), sem("table_in")
        ident_in, moe_out = sem("ident_in"), sem("moe_out")
        wide_in, poolw_in, out_written = sem("wide_in"), sem("poolw_in"), sem("out_written")
        w_in = [sem(f"weights_in{i}") for i in range(RING)]
        sems = {"pe": matmul_done, "act": scalar_done, "dve": vector_done, "pool": pool_done}
        cpe = Counter(matmul_done, "pe", points)
        cact = Counter(scalar_done, "act", points)
        cdve = Counter(vector_done, "dve", points)
        cpool = Counter(pool_done, "pool", points)

        def after(*name):
            key, n = points.get(name, ("pe", 1))
            return sems[key], n

        def in_loop(e, key, *name, before=False):
            n = points.get(name, (key, 1))[1]
            per = points.get(("per", key), (key, 1))[1]
            return sems[key], e * per + max(1, n - per if before else n)

        slots = []

        def kview(w, a, b):
            return w[:, a:b].rearrange("(k p) n -> p k n", p=P)

        def slot_f(stage, w, a, b):
            slots.append((stage, [((0, b - a, b - a), kview(w, a, b))]))

        def slot_gu(stage, g, u, c):
            slots.append((stage, [((0, 256, 512), kview(g, c, c + 256)), ((256, 512, 512), kview(u, c, c + 256))]))

        def slot_d(stage, w, r, n):
            slots.append((stage, [((0, 1024, 1024), w[r:r + n * P, :].rearrange("(k p) n -> p k n", p=P))]))

        w1 = A["w_in"][0]
        for name, at in (("g", 4), ("a", 3), ("q", 0), ("k", 1), ("v", 2)):
            slot_f(name, w1, at * ATT, (at + 1) * ATT)
        for i in range(2):
            slot_f("xk", A["w_xk"][0], i * 512, i * 512 + 512)
        for i in range(2):
            slot_f("xv", A["w_xv"][0], i * 512, i * 512 + 512)
        for i in range(2):
            slot_f("wout", A["w_out"][0], i * 512, i * 512 + 512)
        for i in range(2):
            slot_f("xq", A["w_xq"][0], i * 512, i * 512 + 512)
        for i in range(2):
            slot_f("xo", A["w_xo"][0], i * 512, i * 512 + 512)
        for i in range(MLP_SLOTS + 1):
            if i < MLP_SLOTS:
                slot_f("up", A["w_up"][0], i * 512, i * 512 + 512)
            if i >= 1:
                slot_d("down", A["w_down"][0], (i - 1) * 512, 4)
        N1 = len(slots)
        GU2 = FF2 // 256
        DN2 = (GU2 + 1) // 2
        expert_slots = []
        for l in range(LAYERS):
            w2 = A["w_in_2"][l]
            for i in range(3):
                slot_f("cqkv", w2, i * HW, i * HW + HW)
            slot_f("pool", w2, 2706, 2962)
            slot_f("zab", w2, 1152, 1548)
            slot_f("fq", w2, 1548, 1932)
            slot_f("fk", w2, 1932, 2316)
            slot_f("fv", w2, 2316, 2706)
            for i in range(2):
                slot_f("wout2", A["w_out_2"][l], i * 512, i * 512 + 512)
            if l == 0:
                for i in range(GU2):
                    slot_gu("gu", A["ffn_gate_2"][0], A["ffn_up_2"][0], i * 256)
                    if i >= 2 and i % 2 == 0:
                        slot_d("dn", A["ffn_down_2"][0], (i - 2) * 256, 4)
                slot_d("dn", A["ffn_down_2"][0], (DN2 - 1) * 512, FF2 // P - 4 * (DN2 - 1))
        EXPERT0 = len(slots)
        EXPERT = ["gate", "up"] * 3 + ["down"] * 3
        loads = []
        total = [0] * RING
        for j, s in enumerate(slots):
            total[j % RING] += 16 * len(s[1])
            loads.append(total[j % RING])
        expert_loads, expert_total = [], [0] * RING
        for s, kind in enumerate(EXPERT):
            r = (EXPERT0 + s) % RING
            expert_total[r] += 16
            expert_loads.append(total[r] + expert_total[r])

        def slot_view(j, n, k=8):
            return W[:, j % RING, 0:k * n].rearrange("p (k n) -> p k n", k=k)

        ITEM_JOBS = ["gate0", "up0", "scatterT", "gate1", "up1", "hT0", "gate2", "up2", "hT1", "down0", "down1",
                     "hT2", "gather0", "gather1"]

        def item_bank(name):
            return RING_BANK[ITEM_JOBS.index(name) % 4]

        def item_reader_before(name):
            n = ITEM_JOBS.index(name)
            if n >= 4:
                return ITEM_JOBS[n - 4], False
            last = max(m for m in range(len(ITEM_JOBS)) if m % 4 == n)
            return ITEM_JOBS[last], True

        bank_of = {}
        order = []

        with nc.Block() as block:

            @block.tensor
            def _(pe):
                nslot = [0]

                def weights(stage, n, k=8):
                    j = nslot[0]
                    assert slots[j][0] == stage, (j, slots[j][0], stage)
                    nslot[0] += 1
                    pe.wait_ge(w_in[j % RING], loads[j])
                    return j, slot_view(j, n, k)

                def open_bank(*name):
                    k = len(order)
                    if k >= 4:
                        pe.wait_ge(*after("read", *order[k - 4]))
                    order.append(name)
                    bank_of[name] = RING_BANK[k % 4]
                    return RING_BANK[k % 4]

                def tokens_out(stage, actT, n, i=0, tag=()):
                    j, w = weights(stage, n)
                    for t in range(TT):
                        ps = open_bank(stage, *tag, i, t)
                        for k in range(KD_):
                            mm = pe.matmul(ps[:, 0:n], actT[:, k, t * P:(t + 1) * P], w[:, k, :],
                                           start=(k == 0), stop=(k == KD_ - 1))
                        mm.then_inc(*cpe.mark("filled", stage, *tag, i, t))
                    cpe.also("slot", j)

                def features_out(stage, actT, n, i=0, tag=()):
                    j, w = weights(stage, n)
                    for b in range(0, n, 256):
                        ps = open_bank(stage, *tag, i, b // 256)
                        for c in range(b, min(b + 256, n), P):
                            for k in range(KD_):
                                mm = pe.matmul(ps[:, (c - b) * 2:(c - b) * 2 + S], w[:, k, c:c + P],
                                               actT[:, k, :], start=(k == 0), stop=(k == KD_ - 1))
                        mm.then_inc(*cpe.mark("filled", stage, *tag, i, b // 256))
                    cpe.also("slot", j)

                def turn_norm(i):
                    for t in range(TT):
                        pe.wait_ge(*after("xn", i, t))
                        for b in range(2):
                            ps = open_bank("normT", i, t, b)
                            for k in range(4):
                                mm = pe.transpose(ps[:, k * P:(k + 1) * P],
                                                  XN[:, t, (4 * b + k) * P:(4 * b + k + 1) * P], ident)
                            mm.then_inc(*cpe.mark("filled", "normT", i, t, b))

                def attention(u0, heads, scores, outs):
                    for s in range(heads + 2):
                        if s < heads:
                            u = u0 + s
                            if u >= 2:
                                pe.wait_ge(*after("scores_read", u - 2))
                            scores(s, SC_BANK[u % 2]).then_inc(*cpe.mark("scores", u))
                        if 1 <= s <= heads:
                            u = u0 + s - 1
                            pe.wait_ge(*after("probs", u))
                            if u >= 2:
                                pe.wait_ge(*after("pt_copied", u - 2))
                            ps = PT_BANK[u % 2]
                            for kt in range(TT):
                                for qt in range(TT):
                                    mm = pe.transpose(ps[:, kt * S + qt * P:kt * S + (qt + 1) * P],
                                                      PR[:, u % 3, qt, kt * P:(kt + 1) * P], ident)
                            mm.then_inc(*cpe.mark("pt", u))
                        if s >= 2:
                            u = u0 + s - 2
                            pe.wait_ge(*after("pt_copied", u))
                            outs(s - 2, PT[:, u % 2], u)

                def pair_outs(stage, tag, v):
                    def outs(h, pt, u):
                        if h % 2 == 0:
                            ps = open_bank(stage, *tag, h // 2)
                        else:
                            ps = bank_of[(stage, *tag, h // 2)]
                        o = 64 * (h % 2)
                        for kt in range(TT):
                            mm = pe.matmul(ps[o:o + HD, 0:S], v[:, kt, h * HD:(h + 1) * HD], pt[:, kt, :],
                                           start=(kt == 0), stop=(kt == TT - 1))
                        mm.then_inc(*cpe.mark("o", u))
                        if h % 2:
                            cpe.also("filled", stage, *tag, h // 2)
                    return outs

                pe.wait_ge(rows_in, 16 * 12)
                pe.wait_ge(ident_in, 16)
                ps = open_bank("cols")
                at = 0
                for i, n in enumerate((64, 124, 88)):
                    mm = pe.transpose(ps[:, at:at + n], GR[0:n, i, :], ident[0:n, 0:n])
                    at += n
                mm.then_inc(*cpe.mark("filled", "cols"))

                turn_norm(0)
                pe.wait_ge(*after("ht", 0))
                features_out("g", HT, 512)
                features_out("a", HT, 512)
                tokens_out("q", HT, 512)
                tokens_out("k", HT, 512)
                tokens_out("v", HT, 512)
                turn_norm(1)
                pe.wait_ge(*after("ht", 1))
                for i in range(2):
                    features_out("xk", MT, 512, i)
                pe.wait_ge(*after("rotated"))
                for b in range(4):
                    ps = open_bank("qkT", b)
                    for c in range(2):
                        for t in range(TT):
                            mm = pe.transpose(ps[:, c * S + t * P:c * S + (t + 1) * P],
                                              QK[:, t, (2 * b + c) * P:(2 * b + c + 1) * P], ident)
                    mm.then_inc(*cpe.mark("filled", "qkT", b))
                pe.wait_ge(*after("read", "qkT", 3))
                pe.wait_ge(*after("read", "v", 0, 1))

                def scores1(h, ps):
                    o = 64 * (h % 2)
                    for t in range(TT):
                        mm = pe.matmul(ps[:, t * S:(t + 1) * S], QKT[o:o + HD, h // 2, t * P:(t + 1) * P],
                                       QKT[o:o + HD, 4 + h // 2, :], start=True, stop=True)
                    return mm

                attention(0, AH, scores1, pair_outs("att_o", (), V))
                for i in range(2):
                    tokens_out("xv", MT, 512, i)
                for name, need in (("cmean", "conv"), ("cvar", "csq")):
                    pe.wait_ge(*after(need))
                    src = C if name == "cmean" else SIG
                    ps = open_bank(name)
                    for k in range(4):
                        mm = pe.matmul(ps[:, 0:S], mean_w, src[:, k, :], start=(k == 0), stop=(k == 3))
                    mm.then_inc(*cpe.mark("filled", name))
                pe.wait_ge(*after("convT"))
                pe.wait_ge(*after("read", "att_o", 3))
                for i in range(2):
                    tokens_out("wout", CAT, 512, i)

                turn_norm(2)
                pe.wait_ge(*after("ht", 2))
                for i in range(2):
                    features_out("xq", HT, 512, i)
                pe.wait_ge(*after("read", "xq", 1, 1))
                pe.wait_ge(*after("read", "xv", 1, 1))

                def scoresx(h, ps):
                    for t in range(TT):
                        for c in range(2):
                            mm = pe.matmul(ps[:, t * S:(t + 1) * S], XQT[:, 2 * h + c, t * P:(t + 1) * P],
                                           XKT[:, 2 * h + c, :], start=(c == 0), stop=(c == 1))
                    return mm

                def outsx(h, pt, u):
                    ps = open_bank("xatt_o", h)
                    for c in range(2):
                        for kt in range(TT):
                            mm = pe.matmul(ps[:, c * S:(c + 1) * S],
                                           XV[:, kt, h * 256 + c * P:h * 256 + (c + 1) * P], pt[:, kt, :],
                                           start=(kt == 0), stop=(kt == TT - 1))
                    mm.then_inc(*cpe.mark("o", u))
                    cpe.also("filled", "xatt_o", h)

                attention(AH, XH, scoresx, outsx)
                pe.wait_ge(*after("read", "xatt_o", 3))
                for i in range(2):
                    tokens_out("xo", CAT, 512, i)

                def down(j, w, hbuf, n, first, last, *done):
                    for k in range(n):
                        for t in range(TT):
                            for c in range(2):
                                mm = pe.matmul(banks[2 * t + c][:, :], hbuf[:, k, t * P:(t + 1) * P],
                                               w[:, k, c * 512:(c + 1) * 512],
                                               start=(first and k == 0), stop=(last and k == n - 1))
                    mm.then_inc(*cpe.mark(*done))

                turn_norm(3)
                pe.wait_ge(*after("ht", 3))
                for i in range(MLP_SLOTS + 1):
                    if i < MLP_SLOTS:
                        features_out("up", HT, 512, i)
                    if i >= 1:
                        j, w = weights("down", 1024, 4)
                        if i == 1:
                            pe.wait_ge(*after("scores_read", AH + XH - 1))
                            pe.wait_ge(*after("pt_copied", AH + XH - 1))
                        pe.wait_ge(*after("hidden", "mlp", i - 1, 1))
                        down(j, w, UH[:, (i - 1) % 3], 4, i == 1, i == MLP_SLOTS, "down", "mlp", i - 1)
                        cpe.also("slot", j)

                if stop == 1:
                    return

                for l in range(LAYERS):
                    turn_norm(5 + 2 * l)
                    pe.wait_ge(*after("ht", 5 + 2 * l))
                    for i in range(3):
                        features_out("cqkv", HT, HW, i, (l,))
                    features_out("pool", HT, 256, 0, (l,))
                    tokens_out("zab", HT, HW + 12, 0, (l,))
                    for name, n in (("fq", HW), ("fk", HW), ("fv", HW + 6)):
                        tokens_out(name, HT, n, 0, (l,))
                    pe.wait_ge(*after("pooled", l))
                    if l == 0:
                        pe.wait_ge(poolw_in, 16 * 8)
                        pe.wait_ge(*after("poolw_zero"))
                    ps = open_bank("poolw", l)
                    for i in range(2):
                        mm = pe.matmul(ps[:, i * S:(i + 1) * S], PW[:, l, i, :], YP[:, i, :], start=True, stop=True)
                    mm.then_inc(*cpe.mark("filled", "poolw", l))
                    for b in range(5):
                        ps = open_bank("dnT", l, b)
                        for c in range(2 * b, min(2 * b + 2, 9)):
                            pe.wait_ge(*after("conv2", l, c))
                            for t in range(TT):
                                mm = pe.transpose(ps[:, t * S + (c % 2) * P:t * S + (c % 2 + 1) * P],
                                                  CO[:, c, t * P:(t + 1) * P], ident)
                        mm.then_inc(*cpe.mark("filled", "dnT", l, b))
                    pe.wait_ge(*after("gates", l))
                    ps = open_bank("cum", l)
                    g, nf = SM[:, 0, 0:12], SM[:, 1, 0:12]
                    for t in range(TT):
                        pe.matmul(ps[:, 6 * t:6 * t + 6], upper, g[:, 6 * t:6 * t + 6], start=True, stop=True)
                        pe.matmul(ps[0:NH, 128 + t * P:128 + (t + 1) * P], g[:, 6 * t:6 * t + 6], upper,
                                  start=True, stop=True)
                        mm = pe.matmul(ps[:, 16 + 6 * t:22 + 6 * t], ones, g[:, 6 * t:6 * t + 6],
                                       start=True, stop=True)
                    mm.then_inc(*cpe.mark("filled", "cum", l))
                    ps = open_bank("ncum", l)
                    pe.matmul(ps[0:NH, 0:S], nf[:, 0:6], upper_ones, start=True, stop=False)
                    pe.matmul(ps[0:NH, P:S], nf[:, 6:12], upper, start=False, stop=True)\
                      .then_inc(*cpe.mark("filled", "ncum", l))
                    pe.wait_ge(*after("fx_normed", l))
                    for b in range(3):
                        ps = open_bank("fT", l, b)
                        for c in range(2):
                            for t in range(TT):
                                mm = pe.transpose(ps[:, c * S + t * P:c * S + (t + 1) * P],
                                                  FQ[:, t, (2 * b + c) * P:(2 * b + c + 1) * P], ident)
                        mm.then_inc(*cpe.mark("filled", "fT", l, b))
                    for p in range(3):
                        pe.wait_ge(*after("dn_ready", l))
                        ps = open_bank("kqT", l, p)
                        for t in range(TT):
                            pe.transpose(ps[:, (2 * t) * P:(2 * t + 1) * P], KB[:, t, p * P:(p + 1) * P], ident)
                            mm = pe.transpose(ps[:, (2 * t + 1) * P:(2 * t + 2) * P],
                                              QT3[:, t, p * P:(p + 1) * P], ident)
                        mm.then_inc(*cpe.mark("filled", "kqT", l, p))
                    for p in range(3):
                        ps = open_bank("kT", l, p)
                        for t in range(TT):
                            mm = pe.transpose(ps[:, t * P:(t + 1) * P],
                                              QT3[:, t, HW + p * P:HW + (p + 1) * P], ident)
                        mm.then_inc(*cpe.mark("filled", "kT", l, p))
                    pe.wait_ge(*after("read", "cum", l))
                    for b in range(4):
                        ps = open_bank("grow", l, b)
                        for c in range(3):
                            t, h = chunk_head(3 * b + c)
                            mm = pe.matmul(ps[:, c * P:(c + 1) * P], sel[:, h, :], GT[:, t * P:(t + 1) * P],
                                           start=True, stop=True)
                        mm.then_inc(*cpe.mark("filled", "grow", l, b))
                    pe.wait_ge(*after("read", "kT", l, 2))
                    for b in range(6):
                        ps = open_bank("aq", l, b)
                        for c in range(2):
                            t, h = chunk_head(2 * b + c)
                            o = 64 * (h % 2)
                            mm = pe.matmul(ps[:, c * S:(c + 1) * S], KT[o:o + HD, h // 2, t, :],
                                           KQ[o:o + HD, h // 2, t, :, :].rearrange("p a b -> p (a b)"),
                                           start=True, stop=True)
                        mm.then_inc(*cpe.mark("filled", "aq", l, b))

                    pe.wait_ge(*after("read", "fT", l, 2))
                    pe.wait_ge(*after("read", "ncum", l))

                    def scores2(h, ps):
                        o = 64 * (h % 2)
                        for t in range(TT):
                            pe.matmul(ps[:, t * S:(t + 1) * S], FT[o:o + HD, h // 2, t * P:(t + 1) * P],
                                      FT[o:o + HD, 3 + h // 2, :], start=True, stop=False)
                            mm = pe.matmul(ps[:, t * S:(t + 1) * S], sel[:, h, :], NCT, start=False, stop=True)
                        return mm

                    if l == 0:
                        pe.wait_ge(*after("x", "mlp"))
                    else:
                        pe.wait_ge(*after("x", "ffn"))
                    attention(AH + XH + NH * l, NH, scores2, pair_outs("fx_o", (l,), FV))

                    for lev in range(LEVELS):
                        for gi in range(3):
                            sy = range(4 * gi, 4 * gi + 4)
                            pe.wait_ge(*after("level", l, lev, gi))
                            if lev == 0:
                                ps = open_bank("inv0", l, gi)
                                for i, s in enumerate(sy):
                                    mm = pe.transpose(ps[:, i * P:(i + 1) * P], LT[:, s, :], ident)
                                mm.then_inc(*cpe.mark("filled", "inv0", l, gi))
                                continue
                            pe.wait_ge(*after("inv", l, lev - 1, gi))
                            ps = open_bank("invp", l, lev, gi)
                            for i, s in enumerate(sy):
                                mm = pe.matmul(ps[:, i * P:(i + 1) * P], LT[:, s, :], DI[:, s, :],
                                               start=True, stop=True)
                            mm.then_inc(*cpe.mark("filled", "invp", l, lev, gi))
                        if lev == 0:
                            continue
                        for gi in range(3):
                            sy = range(4 * gi, 4 * gi + 4)
                            pe.wait_ge(*after("read", "invp", l, lev, gi))
                            if lev < LEVELS - 1:
                                ps = open_bank("invd", l, lev, gi)
                                for i, s in enumerate(sy):
                                    mm = pe.matmul(ps[:, i * P:(i + 1) * P], DIT[:, s, :], PM[:, s, :],
                                                   start=True, stop=True)
                                mm.then_inc(*cpe.mark("filled", "invd", l, lev, gi))
                            ps = open_bank("invt", l, lev, gi)
                            for i, s in enumerate(sy):
                                mm = pe.matmul(ps[:, i * P:(i + 1) * P], PM[:, s, :], DIT[:, s, :],
                                               start=True, stop=True)
                            mm.then_inc(*cpe.mark("filled", "invt", l, lev, gi))
                    pe.wait_ge(*after("inv", l, LEVELS - 1, 2))

                    def per_head(name, lhs, rhs):
                        ps = open_bank(name, l)
                        for h in range(NH):
                            mm = pe.matmul(ps[:, h * HD:(h + 1) * HD], lhs(h), rhs(h), start=True, stop=True)
                        mm.then_inc(*cpe.mark("filled", name, l))

                    def hs(h):
                        return slice(h * HD, (h + 1) * HD)

                    pe.wait_ge(*after("bv", l))
                    per_head("vn0", lambda h: DIT[:, system(0, h), :], lambda h: BV[:, 0, hs(h)])
                    pe.wait_ge(*after("read", "vn0", l))
                    ps = open_bank("state", l)
                    for h in range(NH):
                        o = 64 * (h % 2)
                        mm = pe.matmul(ps[o:o + HD, (h // 2) * HD:(h // 2 + 1) * HD], KDC[:, hs(h)],
                                       VN[:, 0, hs(h)], start=True, stop=True)
                    mm.then_inc(*cpe.mark("filled", "state", l))
                    per_head("o0", lambda h: AQ[:, system(0, h), 1, :], lambda h: VN[:, 0, hs(h)])
                    pe.wait_ge(*after("read", "state", l))

                    def half(h):
                        return slice(64 * (h % 2), 64 * (h % 2) + HD)

                    for par in range(2):
                        ps = open_bank("ks", l, par)
                        for p in range(3):
                            for a in range(2):
                                at = (3 * a + p) * HD
                                mm = pe.matmul(ps[:, at:at + HD], KQ[half(par), p, 1, a, :], SST[half(par), p, :],
                                               start=True, stop=True)
                        mm.then_inc(*cpe.mark("filled", "ks", l, par))
                    pe.wait_ge(*after("bv1", l))
                    per_head("vn1", lambda h: DIT[:, system(1, h), :], lambda h: BV[:, 1, hs(h)])
                    pe.wait_ge(*after("read", "vn1", l))
                    per_head("o1", lambda h: AQ[:, system(1, h), 1, :], lambda h: VN[:, 1, hs(h)])
                    pe.wait_ge(*after("dn_out", l))
                    for b in range(2):
                        ps = open_bank("dnoT", l, b)
                        for c in range(2 * b, min(2 * b + 2, 3)):
                            for t in range(TT):
                                mm = pe.transpose(ps[:, (c % 2) * S + t * P:(c % 2) * S + (t + 1) * P],
                                                  O[:, t, c * P:(c + 1) * P], ident)
                        mm.then_inc(*cpe.mark("filled", "dnoT", l, b))
                    pe.wait_ge(*after("read", "dnoT", l, 1))
                    pe.wait_ge(*after("read", "fx_o", l, 2))
                    pe.wait_ge(*after("read", "poolw", l))
                    for i in range(2):
                        tokens_out("wout2", CAT, 512, i, (l,))

                    turn_norm(6 + 2 * l)
                    pe.wait_ge(*after("ht", 6 + 2 * l))

                    def gate_up(w, *name):
                        for c in range(2):
                            ps = open_bank(*name, c)
                            for m in range(2):
                                for k in range(KD_):
                                    mm = pe.matmul(ps[:, m * S:(m + 1) * S],
                                                   w[:, k, m * 256 + c * P:m * 256 + (c + 1) * P], HT[:, k, :],
                                                   start=(k == 0), stop=(k == KD_ - 1))
                            mm.then_inc(*cpe.mark("filled", *name, c))

                    if l == 0:
                        gu = dn = 0
                        pe.wait_ge(*after("scores_read", AH + XH + NH - 1))
                        pe.wait_ge(*after("pt_copied", AH + XH + NH - 1))
                        while nslot[0] < len(slots) and slots[nslot[0]][0] in ("gu", "dn"):
                            if slots[nslot[0]][0] == "gu":
                                j, w = weights("gu", 512)
                                gate_up(w, "gu", gu)
                                gu += 1
                            else:
                                n = min(4, FF2 // P - 4 * dn)
                                j, w = weights("dn", 1024, 4)
                                pe.wait_ge(*after("hidden", "ffn", min(2 * dn + 1, GU2 - 1), 1))
                                down(j, w, UH[:, dn % 3], n, dn == 0, dn == DN2 - 1, "down", "ffn", dn)
                                dn += 1
                            cpe.also("slot", j)
                        continue

                    ps = open_bank("router")
                    for t in range(TT):
                        for k in range(KD_):
                            mm = pe.matmul(ps[:, t * NE:(t + 1) * NE], HT[:, k, t * P:(t + 1) * P], RT[:, k, :],
                                           start=(k == 0), stop=(k == KD_ - 1))
                    mm.then_inc(*cpe.mark("filled", "router"))
                    pe.wait_ge(*after("hot"))
                    hot = SM[:, 4, :].rearrange("p (t e) -> p t e", t=TT)
                    ps = open_bank("ranks")
                    pe.matmul(ps[:, 0:NE], upper, hot[:, 0, :], start=True, stop=True)
                    pe.matmul(ps[:, NE:2 * NE], upper, hot[:, 1, :], start=True, stop=False)
                    pe.matmul(ps[:, NE:2 * NE], ones, hot[:, 0, :], start=False, stop=True)
                    pe.matmul(ps[:, 2 * NE:3 * NE], ones, hot[:, 0, :], start=True, stop=False)
                    pe.matmul(ps[:, 2 * NE:3 * NE], ones, hot[:, 1, :], start=False, stop=True)\
                      .then_inc(*cpe.mark("filled", "ranks"))
                    pe.wait_ge(*after("scores_read", AH + XH + 2 * NH - 1))
                    pe.wait_ge(*after("pt_copied", AH + XH + 2 * NH - 1))
                    for b in range(4):
                        pe.matmul(banks[b][:, :], ident, X[:, b // 2, (b % 2) * 512:(b % 2 + 1) * 512],
                                  start=True, stop=True)

                    def gather(part, ps, *name):
                        for k in range(4):
                            f = 4 * part + k
                            for t in range(TT):
                                mm = pe.matmul(ps[:, k * P:(k + 1) * P], XN[:, t, f * P:(f + 1) * P], GSEL[:, t, :],
                                               start=(t == 0), stop=(t == TT - 1))
                        mm.then_inc(*cpe.mark(*name))

                    pe.wait_ge(*after("select0"))
                    for part in range(2):
                        gather(part, open_bank("gather", part), "filled", "gather", part)
                    for b in range(1, 5):
                        pe.wait_ge(*after("read", *order[-b]))
                    items = pe.value_load(ITEM[0:1, 15:16], min_val=NE, max_val=NE + MORE)
                    base = cpe.n
                    with pe.Fori(0, items) as i:
                        def item_open(name):
                            prev, before = item_reader_before(name)
                            key = points.get(("item_read", prev), ("dve", 1))[0]
                            pe.wait_ge(*in_loop(i, key, "item_read", prev, before=before))
                            return item_bank(name)

                        def item_weights(s):
                            r = (EXPERT0 + s) % RING
                            pe.wait_ge(w_in[r], i * expert_total[r] + expert_loads[s])
                            return slot_view(EXPERT0 + s, 512) if s < 6 else slot_view(EXPERT0 + s, 1024, 4)

                        def wide(name, s):
                            w = item_weights(s)
                            ps = item_open(name)
                            for k in range(KD_):
                                mm = pe.matmul(ps[:, :], HG[:, k, :], w[:, k, :], start=(k == 0), stop=(k == KD_ - 1))
                            mm.then_inc(*cpe.mark("item", name))
                            cpe.also("expert_slot", s)

                        def turn(n):
                            pe.wait_ge(*in_loop(i, "dve", "hh", n))
                            ps = item_open(f"hT{n}")
                            for k in range(4):
                                mm = pe.transpose(ps[:, k * P:(k + 1) * P], HH[:, n, k * P:(k + 1) * P], ident)
                            mm.then_inc(*cpe.mark("item", f"hT{n}"))

                        def down_slot(n):
                            w = item_weights(6 + n)
                            if n == 0:
                                item_open("down0")
                                item_open("down1")
                            pe.wait_ge(*in_loop(i, "act", "item_read", f"hT{n}"))
                            for k in range(4):
                                for c in range(2):
                                    mm = pe.matmul(item_bank(f"down{c}")[:, :], HHT[:, 4 * n + k, :],
                                                   w[:, k, c * 512:(c + 1) * 512], start=(n == 0 and k == 0),
                                                   stop=(n == 2 and k == 3))
                            mm.then_inc(*cpe.mark("expert_slot", 6 + n))

                        pe.wait_ge(*in_loop(i, "dve", "gathered", before=True))
                        wide("gate0", 0)
                        wide("up0", 1)
                        pe.wait_ge(*in_loop(i, "dve", "gate_rows"))
                        ps = item_open("scatterT")
                        for t in range(TT):
                            mm = pe.transpose(ps[:, t * P:(t + 1) * P], GGATE[:, t, :], ident)
                        mm.then_inc(*cpe.mark("item", "scatterT"))
                        wide("gate1", 2)
                        wide("up1", 3)
                        turn(0)
                        wide("gate2", 4)
                        wide("up2", 5)
                        turn(1)
                        down_slot(0)
                        turn(2)
                        down_slot(1)
                        down_slot(2)
                        cpe.also("item", "down0")
                        cpe.also("item", "down1")
                        pe.wait_ge(*in_loop(i, "dve", "select"))
                        for part in range(2):
                            gather(part, item_open(f"gather{part}"), "item", f"gather{part}")
                        pe.wait_ge(*in_loop(i, "act", "item_read", "scatterT"))
                        for c in range(2):
                            pe.wait_ge(*in_loop(i, "act", "item_read", f"down{c}"))
                            for t in range(TT):
                                mm = pe.matmul(banks[2 * t + c][:, :], GST[:, t, :], Y[:, c, :], start=False,
                                               stop=True, skip_group_check=True)
                        mm.then_inc(*cpe.mark("item", "scatter"))
                    points[("per", "pe")] = ("pe", cpe.n - base)

            @block.sync
            def _(sp):
                xv = A["x"][0].rearrange("(t p) n -> p t n", p=P)
                for t in range(TT):
                    sp.dma_start(X[:, t, :], xv[:, t, :]).then_inc(x_in, 16)
                sp.dma_start(T_[:, 0:P], A["table"][:, 0:P]).then_inc(ident_in, 16)

                def load(j):
                    if j >= RING:
                        sp.wait_ge(*after("slot", j - RING))
                    for (a, b, n), src in slots[j][1]:
                        k = src.shape[1]
                        sp.dma_start(slot_view(j, n, k)[:, :, a:b], src).then_inc(w_in[j % RING], 16)

                for j in range(RING):
                    load(j)
                for t in range(TT):
                    sp.dma_start(MEM[:, t, :], A["mem"][0].rearrange("(t p) n -> p t n", p=P)[:, t, :])\
                      .then_inc(mem_in, 16)
                sp.dma_start(T_[:, P:], A["table"][:, P:]).then_inc(table_in, 16)
                for name in WIDE:
                    at, n = WIDE[name]
                    src = A[name].rearrange("a b -> (a b)") if len(A[name].shape) == 2 else A[name]
                    sp.dma_start(WD[:, at:at + n], src.partition_broadcast(P)).then_inc(wide_in, 16)
                sp.dma_start(RT[:, :, :], A["router_2"][0].rearrange("(k p) n -> p k n", p=P)).then_inc(wide_in, 16)
                sp.wait_ge(*after("poolw_zero"))
                for l in range(LAYERS):
                    for g in range(4):
                        o = 64 * (g % 2)
                        sp.dma_start(PW[o:o + 64, l, g // 2, o:o + 64], A["pool_w_2"][l, g]).then_inc(poolw_in, 16)
                for j in range(RING, len(slots) if stop == 0 else N1):
                    load(j)
                if stop == 1:
                    sp.wait_ge(*after("x_final"))
                else:
                    def load_item(i, e):
                        for s, kind in enumerate(EXPERT):
                            j = EXPERT0 + s
                            sp.wait_ge(*in_loop(i, "pe", "expert_slot", (s - RING) % len(EXPERT), before=s < RING))
                            if kind == "down":
                                n = s - 6
                                dst = slot_view(j, 1024, 4)
                                src = A["moe_down_2"][0, bass.ds(e, 1), n * 512:(n + 1) * 512, :]
                            else:
                                n = s // 2
                                dst = slot_view(j, 512)
                                src = A[f"moe_{kind}_2"][0, bass.ds(e, 1), :, n * 512:(n + 1) * 512]
                            sp.dma_start(dst, src.rearrange("e (k p) n -> p (e k) n", p=P)).then_inc(w_in[j % RING], 16)

                    with sp.Fori(0, NE) as i:
                        load_item(i, i)
                    sp.wait_ge(*after("items"))
                    items = sp.value_load(ITEM[0:1, 15:16], min_val=NE, max_val=NE + MORE)
                    with sp.If(items > NE):
                        with sp.Fori(NE, items) as i:
                            load_item(i, sp.value_load(ITEM[0:1, bass.ds(i, 1)], min_val=0, max_val=NE - 1))
                    sp.wait_ge(moe_out, 4)
                sp.dma_start(out[0].rearrange("(t p) n -> p t n", p=P), X[:, :, :]).then_inc(out_written, 16)
                sp.wait_ge(out_written, 16)

            @block.scalar
            def _(act):
                for i, tile in enumerate(ROWS):
                    at = 0
                    for name, n in tile:
                        src = A[name]
                        if len(src.shape) == 3:
                            src = src.rearrange("a b (r p) -> (a b r) p", p=P)
                        else:
                            src = src.rearrange("a (r p) -> (a r) p", p=P)
                        act.dma_start(GR[at:at + n, i, :], src).then_inc(rows_in, 16)
                        at += n

                def do(ins, *name):
                    ins.then_inc(*cact.mark(*name))

                def own():
                    act.wait_ge(*cact.last())

                def sumsq(i, src):
                    for t in range(TT):
                        do(act.activation(XN[:, t, :], src[:, t, :], ACT.Square, accum_out=SS[:, t:t + 1]),
                           "ss", i, t)

                def copy_out(dst, src, *name):
                    act.wait_ge(*after("filled", *name))
                    do(act.activation(dst, src, ACT.Copy), "read", *name)

                def exps(u):
                    act.wait_ge(*after("negmax", u))
                    for t in range(TT):
                        do(act.activation(PR[:, u % 3, t, :], PR[:, u % 3, t, :], ACT.Exp,
                                          bias=NM[:, u % 3, t:t + 1], accum_out=DEN[:, u % 3, t:t + 1]),
                           "exp", u, t)

                def attention(u0, heads, outs):
                    for s in range(heads + 3):
                        if s < heads:
                            exps(u0 + s)
                        if 1 <= s <= heads:
                            u = u0 + s - 1
                            act.wait_ge(*after("pt", u))
                            if u >= 2:
                                act.wait_ge(*after("o", u - 2))
                            do(act.activation(PT[:, u % 2], PT_BANK[u % 2][:, :].rearrange("p (a b) -> p a b", a=2),
                                              ACT.Copy), "pt_copied", u)
                        if s >= 3:
                            outs(s - 3)

                def psum(*name):
                    return bank_of[name]

                def two(ps):
                    return ps[:, :].rearrange("p (a b) -> p a b", a=2)

                act.wait_ge(x_in, 32)
                sumsq(0, X)
                for b in range(2):
                    act.wait_ge(*after("filled", "g", 0, b))
                    do(act.activation(SIG[:, 2 * b:2 * b + 2, :], two(psum("g", 0, b)), ACT.Sigmoid),
                       "read", "g", 0, b)
                for t in range(TT):
                    copy_out(QK[:, t, 0:512], psum("q", 0, t)[:, :], "q", 0, t)
                for t in range(TT):
                    copy_out(QK[:, t, 512:1024], psum("k", 0, t)[:, :], "k", 0, t)
                act.wait_ge(mem_in, 32)
                act.wait_ge(*after("filled", "normT", 0, 1, 1))
                sumsq(1, MEM)
                for t in range(TT):
                    copy_out(V[:, t, :], psum("v", 0, t)[:, :], "v", 0, t)
                for i in range(2):
                    for b in range(2):
                        copy_out(XKT[:, 4 * i + 2 * b:4 * i + 2 * b + 2, :], two(psum("xk", i, b)), "xk", i, b)
                for b in range(4):
                    copy_out(QKT[:, 2 * b:2 * b + 2, :], two(psum("qkT", b)), "qkT", b)

                def outs1(h):
                    if h % 2:
                        copy_out(CAT[:, h // 2, :], psum("att_o", h // 2)[:, 0:S], "att_o", h // 2)

                attention(0, AH, outs1)
                for i in range(2):
                    for t in range(TT):
                        copy_out(XV[:, t, i * 512:(i + 1) * 512], psum("xv", i, t)[:, :], "xv", i, t)
                act.wait_ge(*after("read", "cmean"))
                do(act.activation(SIG[:, :, :], C[:, :, :], ACT.Square), "csq")
                act.wait_ge(*after("read", "cvar"))
                do(act.activation(U[:, 0, 0:S], U[:, 0, 0:S], ACT.Sqrt), "csd")
                act.wait_ge(*after("cnormed"))
                for i in range(4):
                    do(act.activation(CAT[:, 4 + i, :], C[:, i, :], ACT.Silu, bias=col("conv_ln_b", i),
                                      scale=col("conv_ln_g", i)), "convT")
                act.wait_ge(*after("read", "wout", 1, 1))
                sumsq(2, X)
                for i in range(2):
                    for b in range(2):
                        copy_out(XQT[:, 4 * i + 2 * b:4 * i + 2 * b + 2, :], two(psum("xq", i, b)), "xq", i, b)

                def outsx(h):
                    copy_out(CAT[:, 2 * h:2 * h + 2, :], two(psum("xatt_o", h)), "xatt_o", h)

                attention(AH, XH, outsx)
                act.wait_ge(*after("read", "xo", 1, 1))
                sumsq(3, X)
                n = 0
                for i in range(MLP_SLOTS):
                    for b in range(2):
                        act.wait_ge(*after("filled", "up", i, b))
                        if n >= 2:
                            act.wait_ge(*after("hidden", "mlp", (n - 2) // 2, n % 2))
                        do(act.activation(SG[:, n % 2, :], psum("up", i, b)[:, :], ACT.Relu), "read", "up", i, b)
                        n += 1
                act.wait_ge(*after("x", "mlp"))
                sumsq(4, X)
                if stop == 1:
                    return
                for l in range(LAYERS):
                    i0 = 5 + 2 * l
                    act.wait_ge(*after("x_final1") if l == 0 else after("x", "ffn"))
                    sumsq(i0, X)
                    for i in range(3):
                        copy_out(CI[:, 3 * i:3 * i + 2, 3:3 + S], two(psum("cqkv", l, i, 0)), "cqkv", l, i, 0)
                        copy_out(CI[:, 3 * i + 2, 3:3 + S], psum("cqkv", l, i, 1)[:, 0:S], "cqkv", l, i, 1)
                    copy_out(XP[:, :, 16:], two(psum("pool", l, 0, 0)), "pool", l, 0, 0)
                    for t in range(TT):
                        copy_out(ZAB[:, t, :], psum("zab", l, 0, t)[:, 0:HW + 12], "zab", l, 0, t)
                    for t in range(TT):
                        copy_out(FQ[:, t, 0:HW], psum("fq", l, 0, t)[:, 0:HW], "fq", l, 0, t)
                    for t in range(TT):
                        copy_out(FQ[:, t, HW:], psum("fk", l, 0, t)[:, 0:HW], "fk", l, 0, t)
                    for t in range(TT):
                        copy_out(FV[:, t, :], psum("fv", l, 0, t)[:, 0:HW + 6], "fv", l, 0, t)
                    for i in range(9):
                        act.wait_ge(*after("taps", l, i))
                        do(act.activation(CO[:, i, :], CO[:, i, :], ACT.Silu), "conv2", l, i)
                    own()
                    do(act.activation(ZAB[:, :, 0:HW], ZAB[:, :, 0:HW], ACT.Silu), "silu_z", l)
                    do(act.activation(SM[:, 2, 0:12].rearrange("p (t h) -> p t h", t=2), ZAB[:, :, HW + 6:],
                                      ACT.Sigmoid), "beta", l)
                    act.wait_ge(*after("absneg", l))
                    do(act.activation(SM[:, 5:7, 0:12], SM[:, 5:7, 0:12], ACT.Exp))
                    do(act.activation(SM[:, 7, 0:6], wide("dn_a_log_2", l, NH), ACT.Exp))
                    own()
                    do(act.activation(SM[:, 5:7, 0:12], SM[:, 5:7, 0:12], ACT.Ln, bias=1.0), "softlog", l)
                    act.wait_ge(*after("filled", "normT", i0, 1, 1))
                    do(act.activation(SQ[:, :, :], FQ[:, :, :], ACT.Square), "fx_sq", l)
                    for b in range(5):
                        n = 256 if b < 4 else P
                        copy_out(QT3[:, :, b * 256:b * 256 + n], two(psum("dnT", l, b))[:, :, 0:n], "dnT", l, b)
                    own()
                    act.wait_ge(*after("fx_ssum", l))
                    do(act.activation(SQ[:, :, :], QT3[:, :, 0:2 * HW], ACT.Square), "dn_sq", l)
                    act.wait_ge(*after("read", "cum", l))
                    do(act.activation(SM[:, 9, 0:12], SM[:, 8, 0:12], ACT.Exp))
                    do(act.activation(SM[:, 10, 0:6], SM[:, 11, 0:6], ACT.Exp), "expg", l)
                    for b in range(3):
                        copy_out(FT[:, 2 * b:2 * b + 2, :], two(psum("fT", l, b)), "fT", l, b)
                    for p in range(3):
                        copy_out(KQ[:, p].rearrange("p a b c -> p (a b c)"), psum("kqT", l, p)[:, :], "kqT", l, p)
                    for p in range(3):
                        copy_out(KT[:, p].rearrange("p a b -> p (a b)"), psum("kT", l, p)[:, 0:S], "kT", l, p)
                    act.wait_ge(*after("read", "grow", l, 3))
                    do(act.activation(DD[:, :, :], DD[:, :, :], ACT.Exp), "decay", l)

                    def outs2(h):
                        if h % 2:
                            copy_out(CAT[:, 3 + h // 2, :], psum("fx_o", l, h // 2)[:, 0:S], "fx_o", l, h // 2)

                    attention(AH + XH + NH * l, NH, outs2)
                    for lev in range(1, LEVELS):
                        for gi in range(3):
                            copy_out(PM[:, 4 * gi:4 * gi + 4, :],
                                     psum("invp", l, lev, gi)[:, :].rearrange("p (a b) -> p a b", a=4),
                                     "invp", l, lev, gi)
                    copy_out(VN[:, 0, :], psum("vn0", l)[:, 0:HW], "vn0", l)
                    copy_out(SST[:, :, :], psum("state", l)[:, 0:3 * HD].rearrange("p (a b) -> p a b", a=3), "state", l)
                    copy_out(O[:, 0, :], psum("o0", l)[:, 0:HW], "o0", l)
                    copy_out(VN[:, 1, :], psum("vn1", l)[:, 0:HW], "vn1", l)
                    act.wait_ge(*after("read", "o1", l))
                    do(act.activation(SQ[:, :, 0:HW], O[:, :, :], ACT.Square), "o_sq", l)
                    copy_out(CAT[:, 0:2, :], two(psum("dnoT", l, 0)), "dnoT", l, 0)
                    copy_out(CAT[:, 2, :], psum("dnoT", l, 1)[:, 0:S], "dnoT", l, 1)
                    act.wait_ge(*after("read", "wout2", l, 1, 1))
                    sumsq(i0 + 1, X)
                    if l == 0:
                        n = 0
                        for i in range(GU2):
                            for c in range(2):
                                act.wait_ge(*after("filled", "gu", i, c))
                                if n >= 2:
                                    act.wait_ge(*after("hidden", "ffn", (n - 2) // 2, n % 2))
                                do(act.activation(SG[:, n % 2, 0:S], psum("gu", i, c)[:, 0:S], ACT.Silu),
                                   "silu", "ffn", i, c)
                                n += 1
                        continue
                    act.wait_ge(*after("logit_shift"))
                    do(act.activation(SM[:, 3, :], SM[:, 2, :], ACT.Exp), "gate_exp")
                    act.wait_ge(*after("items"))
                    items = act.value_load(ITEM[0:1, 15:16], min_val=NE, max_val=NE + MORE)
                    base = cact.n
                    with act.Fori(0, items) as i:
                        def silu(n):
                            act.wait_ge(*in_loop(i, "pe", "item", f"gate{n}"))
                            act.wait_ge(*in_loop(i, "dve", "hh", n, before=True))
                            do(act.activation(SGE[:, n, :], item_bank(f"gate{n}")[:, :], ACT.Silu),
                               "item_read", f"gate{n}")

                        def copy(dst, name, free, key="pe", before=True):
                            act.wait_ge(*in_loop(i, "pe", "item", name))
                            act.wait_ge(*in_loop(i, "pe", *free, before=True))
                            do(act.activation(dst, item_bank(name)[:, 0:dst.shape[1]], ACT.Copy), "item_read", name)

                        def copy_hT(n):
                            copy(HHT[:, 4 * n:4 * n + 4, :].rearrange("p a b -> p (a b)"), f"hT{n}", ("expert_slot", 8))

                        silu(0)
                        copy(GST.rearrange("p a b -> p (a b)"), "scatterT", ("item", "scatter"))
                        silu(1)
                        copy_hT(0)
                        silu(2)
                        copy_hT(1)
                        copy_hT(2)
                        for c in range(2):
                            copy(Y[:, c, :], f"down{c}", ("item", "scatter"))
                    points[("per", "act")] = ("act", cact.n - base)

            @block.gpsimd
            def _(pool):
                def do(ins, *name):
                    ins.then_inc(*cpool.mark(*name))

                do(pool.memset(NHALF[:, :], -0.5), "nhalf")
                do(pool.memset(U[:, :, 0:PAD], 0.0))
                do(pool.memset(U[:, :, PAD + S:], 0.0), "u_padded")
                do(pool.memset(PW[:, :, :, :], 0.0), "poolw_zero")
                pool.wait_ge(*cpool.last())

                def power(n, need, *name):
                    pool.wait_ge(*after(*need))
                    do(pool.tensor_tensor(RS[:, 0:n], MS[:, 0:n], NHALF[:, 0:n], ALU.pow), *name)

                for i in range(5):
                    power(2, ("ms", i), "rstd", i)
                if stop == 1:
                    return
                for l in range(LAYERS):
                    power(2, ("ms", 5 + 2 * l), "rstd", 5 + 2 * l)
                    pool.wait_ge(*after("read", "pool", l, 0, 0))
                    do(pool.memset(XP[:, :, 0:16], 0.0))
                    do(pool.memset(SA[:, :, 0:16], 0.0))
                    do(pool.memset(SBf[:, :, 0:16], 0.0))
                    do(pool.memset(SC[:, :, 0:16], 0.0))
                    last = XP
                    for n, nxt in ((1, SA), (2, SBf), (4, SC)):
                        pool.wait_ge(*cpool.last())
                        do(pool.tensor_tensor(nxt[:, :, 16:], last[:, :, 16:], last[:, :, 16 - n:16 + S - n], ALU.add))
                        last = nxt
                    pool.wait_ge(*cpool.last())
                    for i, (half_, src) in enumerate(((slice(0, 64), SA), (slice(64, 128), SBf))):
                        do(pool.tensor_tensor(YP[half_, 0, :], src[half_, 0, 16:], poolinv[half_, 0, :], ALU.mult))
                    do(pool.tensor_tensor(YP[0:64, 1, :], SC[0:64, 1, 16:], poolinv[0:64, 1, :], ALU.mult))
                    pool.wait_ge(*cpool.last())
                    do(pool.tensor_tensor(SA[64:128, 1, 16:], SC[64:128, 1, 16:], SC[64:128, 1, 8:8 + S], ALU.add))
                    pool.wait_ge(*cpool.last())
                    do(pool.tensor_tensor(YP[64:128, 1, :], SA[64:128, 1, 16:], poolinv[64:128, 1, :], ALU.mult))
                    pool.wait_ge(*cpool.last())
                    do(pool.tensor_tensor(YP[:, :, :], YP[:, :, :], XP[:, :, 16:], ALU.subtract), "pooled", l)
                    power(24, ("fx_ms", l), "fx_rstd", l)
                    power(24, ("dn_ms", l), "dn_rstd", l)
                    power(12, ("o_ms", l), "o_rstd", l)
                    power(2, ("ms", 6 + 2 * l), "rstd", 6 + 2 * l)

            @block.vector
            def _(dve):
                def do(ins, *name):
                    ins.then_inc(*cdve.mark(*name))

                def own(back=0):
                    dve.wait_ge(*cdve.last(back))

                def psum(*name):
                    return bank_of[name]

                def norm(i, src, gain, gi, dst):
                    rows_norm(i, src)
                    for t in range(TT):
                        for b in range(2):
                            dve.wait_ge(*after("filled", "normT", i, t, b))
                            do(dve.tensor_tensor(dst[:, 4 * b:4 * b + 4, t * P:(t + 1) * P],
                                                 psum("normT", i, t, b)[:, :].rearrange("p (k n) -> p k n", k=4),
                                                 cols(gain, gi + 4 * b, 4).unsqueeze(2).broadcast_to([P, 4, P]),
                                                 ALU.mult), "read", "normT", i, t, b)
                    cdve.also("ht", i)

                def rows_norm(i, src, final=False):
                    dve.wait_ge(*after("ss", i, 1))
                    do(dve.tensor_scalar(MS[:, 0:TT], SS[:, 0:TT], 1.0 / D, EPS, ALU.mult, ALU.add), "ms", i)
                    dve.wait_ge(*after("rstd", i))
                    for t in range(TT):
                        if final:
                            do(dve.scalar_tensor_tensor(src[:, t, :], src[:, t, :], RS[:, t:t + 1],
                                                        wide("norm_final_g", 0, D), ALU.mult, ALU.mult), "xn", i, t)
                        else:
                            do(dve.tensor_scalar(XN[:, t, :], src[:, t, :], RS[:, t:t + 1], None, ALU.mult),
                               "xn", i, t)

                def add_residual(*name):
                    for i in range(2):
                        for t in range(TT):
                            dve.wait_ge(*after("filled", *name, i, t))
                            part = X[:, t, i * 512:(i + 1) * 512]
                            do(dve.tensor_tensor(part, psum(*name, i, t)[:, :], part, ALU.add), "read", *name, i, t)

                def add_banks(*name):
                    for b in range(4):
                        part = X[:, b // 2, (b % 2) * 512:(b % 2 + 1) * 512]
                        do(dve.tensor_tensor(part, banks[b][:, :], part, ALU.add))
                    cdve.also(*name)

                def attention(u0, heads, scale, mask):
                    for s in range(heads + 1):
                        if s < heads:
                            u = u0 + s
                            dve.wait_ge(*after("scores", u))
                            if u >= 3:
                                dve.wait_ge(*after("pt", u - 3))
                            ps = SC_BANK[u % 2][:, :]
                            pr = PR[:, u % 3].rearrange("p a b -> p (a b)")
                            if mask is None:
                                do(dve.tensor_scalar(pr, ps, scale, None, ALU.mult), "scores_read", u)
                            else:
                                do(dve.scalar_tensor_tensor(pr, ps, scale, mask.rearrange("p a b -> p (a b)"),
                                                            ALU.mult, ALU.add), "scores_read", u)
                            own()
                            do(dve.tensor_reduce(NM[:, u % 3, :], PR[:, u % 3], AX.X, ALU.max, negate=True),
                               "negmax", u)
                        if s >= 1:
                            u = u0 + s - 1
                            dve.wait_ge(*after("exp", u, 1))
                            do(dve.reciprocal(RDEN[:, u % 3, :], DEN[:, u % 3, :]))
                            own()
                            for t in range(TT):
                                do(dve.tensor_scalar(PR[:, u % 3, t, :], PR[:, u % 3, t, :],
                                                     RDEN[:, u % 3, t:t + 1], None, ALU.mult), "probs", u)

                dve.wait_ge(*after("filled", "cols"))
                do(dve.tensor_copy(COL[:, :], psum("cols")[:, 0:NCOLS]), "read", "cols")
                own()
                dve.wait_ge(*after("nhalf"))
                norm(0, X, "norm_mix_g", 0, HT)
                dve.wait_ge(*after("u_padded"))
                for b in range(2):
                    dve.wait_ge(*after("filled", "a", 0, b))
                    dve.wait_ge(*after("read", "g", 0, b))
                    do(dve.tensor_tensor(U[:, 2 * b:2 * b + 2, PAD:PAD + S],
                                         psum("a", 0, b)[:, :].rearrange("p (a b) -> p a b", a=2),
                                         SIG[:, 2 * b:2 * b + 2, :], ALU.mult), "read", "a", 0, b)
                own()
                def conv_taps(lo, hi):
                    for k in range(lo, hi):
                        for i in range(4):
                            w = col("conv_w", 4 * k + i)
                            if k == 0:
                                do(dve.tensor_scalar(C[:, i, :], U[:, i, 0:S], w, col("conv_b", i), ALU.mult, ALU.add))
                            else:
                                own(3)
                                do(dve.scalar_tensor_tensor(C[:, i, :], U[:, i, k:k + S], w, C[:, i, :],
                                                            ALU.mult, ALU.add))

                conv_taps(0, 20)
                rows_norm(1, MEM)
                for n in (0, 1):
                    dve.wait_ge(*after("read", "q" if n == 0 else "k", 0, 1))
                dve.wait_ge(table_in, 16)
                own()
                heads = QK.rearrange("p t (h c) -> p t h c", c=HD)
                x1, x2 = heads[:, :, :, 0:8], heads[:, :, :, 8:16]
                cb = cos.unsqueeze(2).broadcast_to([P, TT, 16, 8])
                sbr = sin.unsqueeze(2).broadcast_to([P, TT, 16, 8])
                r = [RT1[:, i, :].rearrange("p (t h c) -> p t h c", t=TT, h=16) for i in range(4)]
                do(dve.tensor_tensor(r[0], x1, cb, ALU.mult))
                do(dve.tensor_tensor(r[1], x2, sbr, ALU.mult))
                do(dve.tensor_tensor(r[2], x2, cb, ALU.mult))
                do(dve.tensor_tensor(r[3], x1, sbr, ALU.mult))
                own()
                do(dve.tensor_tensor(x1, r[0], r[1], ALU.subtract))
                do(dve.tensor_tensor(x2, r[2], r[3], ALU.add), "rotated")
                for t in range(TT):
                    for b in range(2):
                        dve.wait_ge(*after("filled", "normT", 1, t, b))
                        do(dve.tensor_tensor(MT[:, 4 * b:4 * b + 4, t * P:(t + 1) * P],
                                             psum("normT", 1, t, b)[:, :].rearrange("p (k n) -> p k n", k=4),
                                             cols("norm_mem_g", 4 * b, 4).unsqueeze(2).broadcast_to([P, 4, P]),
                                             ALU.mult), "read", "normT", 1, t, b)
                cdve.also("ht", 1)
                conv_taps(20, TAPS)
                cdve.also("conv")
                attention(0, AH, 0.125, logc)
                dve.wait_ge(*after("filled", "cmean"))
                do(dve.tensor_tensor(C[:, :, :], C[:, :, :],
                                     psum("cmean")[:, 0:S].unsqueeze(1).broadcast_to([P, 4, S]), ALU.subtract),
                   "read", "cmean")
                dve.wait_ge(*after("filled", "cvar"))
                do(dve.tensor_scalar(U[:, 0, 0:S], psum("cvar")[:, 0:S], EPS, None, ALU.add), "read", "cvar")
                dve.wait_ge(*after("csd"))
                do(dve.reciprocal(U[:, 1, 0:S], U[:, 0, 0:S]))
                own()
                do(dve.tensor_tensor(C[:, :, :], C[:, :, :],
                                     U[:, 1, 0:S].unsqueeze(1).broadcast_to([P, 4, S]), ALU.mult), "cnormed")
                add_residual("wout")
                norm(2, X, "norm_x_g", 0, HT)
                attention(AH, XH, 0.0625, None)
                add_residual("xo")
                norm(3, X, "norm_mlp_g", 0, HT)
                for i in range(MLP_SLOTS):
                    for b in range(2):
                        n = 2 * i + b
                        dve.wait_ge(*after("read", "up", i, b))
                        if i >= 3:
                            dve.wait_ge(*after("down", "mlp", i - 3))
                        sg = SG[:, n % 2, :].rearrange("p (a b) -> p a b", a=2)
                        do(dve.tensor_tensor(UH[:, i % 3, 2 * b:2 * b + 2, :], sg, sg, ALU.mult),
                           "hidden", "mlp", i, b)
                dve.wait_ge(*after("down", "mlp", MLP_SLOTS - 1))
                add_banks("x", "mlp")
                dve.wait_ge(wide_in, 16 * 8)
                rows_norm(4, X, final=True)
                cdve.also("x_final1")
                if stop == 1:
                    cdve.also("x_final")
                    return

                for l in range(LAYERS):
                    i0 = 5 + 2 * l
                    norm(i0, X, "norm1_2", 8 * l, HT)
                    do(dve.memset(CI[:, :, 0:3], 0.0))
                    own()
                    for i in range(9):
                        dve.wait_ge(*after("read", "cqkv", l, i // 3, (i % 3) // 2))
                        for k in range(DTAPS):
                            w = col("dn_conv_2", 36 * l + 9 * k + i)
                            if k == 0:
                                do(dve.tensor_scalar(CO[:, i, :], CI[:, i, 0:S], w, None, ALU.mult))
                            else:
                                own()
                                do(dve.scalar_tensor_tensor(CO[:, i, :], CI[:, i, k:k + S], w, CO[:, i, :],
                                                            ALU.mult, ALU.add), "taps", l, i)
                    dve.wait_ge(*after("read", "fv", l, 0, 1))
                    dve.wait_ge(*after("beta", l))

                    def six(v):
                        return v.rearrange("p (t h) -> p t h", t=TT)

                    def bc6(v):
                        return v.unsqueeze(1).broadcast_to([P, TT, NH])

                    do(dve.tensor_tensor(six(SM[:, 3, 0:12]), ZAB[:, :, HW:HW + 6], bc6(wide("dn_dt_bias_2", l, NH)),
                                         ALU.add))
                    do(dve.tensor_tensor(six(SM[:, 4, 0:12]), FV[:, :, HW:HW + 6], bc6(wide("fx_f_bias_2", l, NH)),
                                         ALU.add))
                    own()
                    do(dve.tensor_scalar(SM[:, 4, 0:12], SM[:, 4, 0:12], -1.0, None, ALU.mult))
                    own()
                    do(dve.tensor_scalar(SM[:, 12:14, 0:12], SM[:, 3:5, 0:12], -1.0, None, ALU.mult))
                    own()
                    do(dve.tensor_tensor(SM[:, 5:7, 0:12], SM[:, 3:5, 0:12], SM[:, 12:14, 0:12], ALU.min), "absneg", l)
                    dve.wait_ge(*after("softlog", l))
                    do(dve.scalar_tensor_tensor(SM[:, 0:2, 0:12], SM[:, 3:5, 0:12], 0.0, SM[:, 5:7, 0:12],
                                                ALU.max, ALU.add))
                    own()
                    do(dve.scalar_tensor_tensor(six(SM[:, 0, 0:12]), six(SM[:, 0, 0:12]), -1.0, bc6(SM[:, 7, 0:6]),
                                                ALU.mult, ALU.mult), "gates", l)
                    dve.wait_ge(*after("filled", "poolw", l))
                    for i in range(2):
                        do(dve.tensor_scalar(CAT[:, 6 + i, :], psum("poolw", l)[:, i * S:(i + 1) * S],
                                             col("pool_scale_2", 2 * l + i), None, ALU.mult), "read", "poolw", l)

                    def head_norm(name, src, scale_q, width, sq_done, div, last_name):
                        n = TT * width
                        dve.wait_ge(*after(*sq_done))
                        sq = SQ[:, :, 0:width * HD].rearrange("p t (h c) -> p t h c", c=HD)
                        do(dve.tensor_reduce(SS[:, 0:n].rearrange("p (t h) -> p t h", t=TT), sq, AX.X, ALU.add),
                           name + "_ssum", l)
                        own()
                        do(dve.tensor_scalar(MS[:, 0:n], SS[:, 0:n], 1.0 / div, EPS, ALU.mult, ALU.add),
                           name + "_ms", l)
                        dve.wait_ge(*after(name + "_rstd", l))
                        rs = RS[:, 0:n].rearrange("p (t h) -> p t h", t=TT)
                        if scale_q != 1.0:
                            do(dve.tensor_scalar(rs[:, :, 0:NH], rs[:, :, 0:NH], scale_q, None, ALU.mult))
                            own()
                        v = src.rearrange("p t (h c) -> p t h c", c=HD)
                        do(dve.tensor_tensor(v, v, rs.unsqueeze(3).broadcast_to([P, TT, width, HD]), ALU.mult),
                           last_name, l)

                    head_norm("fx", FQ, 1.0, 12, ("fx_sq", l), HD, "fx_scaled")
                    own()
                    for i, name in enumerate(("fx_qnorm_2", "fx_knorm_2")):
                        for t in range(TT):
                            v = FQ[:, t, i * HW:(i + 1) * HW].rearrange("p (h c) -> p h c", c=HD)
                            do(dve.tensor_tensor(v, v, wide(name, l, HD).unsqueeze(1).broadcast_to([P, NH, HD]),
                                                 ALU.mult), "fx_normed", l)
                    dve.wait_ge(*after("filled", "cum", l))
                    ps = psum("cum", l)
                    do(dve.tensor_copy(GT, ps[0:NH, 128:128 + S]))
                    do(dve.tensor_copy(SM[:, 8, 0:12], ps[:, 0:12]))
                    own()
                    do(dve.scalar_tensor_tensor(SM[:, 11, 0:6], SM[:, 8, 0:6], -1.0, ps[:, 16:22], ALU.mult, ALU.add),
                       "read", "cum", l)
                    dve.wait_ge(*after("filled", "ncum", l))
                    do(dve.tensor_scalar(NCT, psum("ncum", l)[0:NH, 0:S], 8.0, None, ALU.mult), "read", "ncum", l)
                    head_norm("dn", QT3[:, :, 0:2 * HW], HD ** -0.5, 12, ("dn_sq", l), 1.0, "dn_scaled")
                    own()
                    beta = six(SM[:, 2, 0:12])

                    def heads3(v):
                        return v.rearrange("p t (h c) -> p t h c", c=HD)

                    bb = beta.unsqueeze(3).broadcast_to([P, TT, NH, HD])
                    do(dve.tensor_tensor(heads3(KB), heads3(QT3[:, :, HW:2 * HW]), bb, ALU.mult), "dn_ready", l)
                    do(dve.tensor_tensor(heads3(BV), heads3(QT3[:, :, 2 * HW:]), bb, ALU.mult), "bv", l)
                    dve.wait_ge(*after("expg", l))
                    do(dve.tensor_tensor(KDC.rearrange("p (h c) -> p h c", c=HD),
                                         QT3[:, 0, HW:2 * HW].rearrange("p (h c) -> p h c", c=HD),
                                         SM[:, 10, 0:6].unsqueeze(2).broadcast_to([P, NH, HD]), ALU.mult), "kdc", l)
                    for b in range(4):
                        dve.wait_ge(*after("filled", "grow", l, b))
                        for c in range(3):
                            s = 3 * b + c
                            t, h = chunk_head(s)
                            do(dve.tensor_scalar(DD[:, s, :], psum("grow", l, b)[:, c * P:(c + 1) * P],
                                                 SM[:, 8, NH * t + h:NH * t + h + 1], 0.0, ALU.subtract, ALU.min), "read", "grow", l, b)
                    dve.wait_ge(*after("decay", l))
                    do(dve.tensor_tensor(DD[:, :, :], DD[:, :, :], upper.unsqueeze(1).broadcast_to([P, 12, P]),
                                         ALU.mult))
                    own()
                    for b in range(6):
                        dve.wait_ge(*after("filled", "aq", l, b))
                        do(dve.tensor_tensor(AQ[:, 2 * b:2 * b + 2],
                                             psum("aq", l, b)[:, :].rearrange("p (a b c) -> p a b c", a=2, b=2),
                                             DD[:, 2 * b:2 * b + 2, :].unsqueeze(2).broadcast_to([P, 2, 2, P]),
                                             ALU.mult), "read", "aq", l, b)
                    attention(AH + XH + NH * l, NH, 0.125, causal)

                    def level_mask(lev, gi):
                        do(dve.tensor_tensor(LT[:, 4 * gi:4 * gi + 4, :], AQ[:, 4 * gi:4 * gi + 4, 0, :],
                                             levels[:, lev, :].unsqueeze(1).broadcast_to([P, 4, P]), ALU.mult),
                           "level", l, lev, gi)

                    idb = ident.unsqueeze(1).broadcast_to([P, 4, P])
                    for gi in range(3):
                        level_mask(0, gi)
                    own()
                    for gi in range(3):
                        do(dve.tensor_tensor(DIT[:, 4 * gi:4 * gi + 4, :], idb, LT[:, 4 * gi:4 * gi + 4, :],
                                             ALU.subtract))
                    for gi in range(3):
                        g4 = slice(4 * gi, 4 * gi + 4)
                        dve.wait_ge(*after("filled", "inv0", l, gi))
                        do(dve.tensor_tensor(DI[:, g4, :], idb,
                                             psum("inv0", l, gi)[:, :].rearrange("p (a b) -> p a b", a=4),
                                             ALU.subtract), "read", "inv0", l, gi)
                        cdve.also("inv", l, 0, gi)
                        own()
                        level_mask(1, gi)
                    for lev in range(1, LEVELS):
                        for gi in range(3):
                            g4 = slice(4 * gi, 4 * gi + 4)
                            names = (("invd", DI), ("invt", DIT)) if lev < LEVELS - 1 else (("invt", DIT),)
                            for name, dst in names:
                                dve.wait_ge(*after("filled", "invt", l, lev, gi))
                                do(dve.tensor_tensor(dst[:, g4, :], dst[:, g4, :],
                                                     psum(name, l, lev, gi)[:, :].rearrange("p (a b) -> p a b", a=4),
                                                     ALU.subtract), "read", name, l, lev, gi)
                            cdve.also("inv", l, lev, gi)
                            if lev < LEVELS - 1:
                                level_mask(lev + 1, gi)
                    def h6(v):
                        return v.rearrange("p (h c) -> p h c", c=HD)

                    def parity(v, par):
                        return v.rearrange("p (g two c) -> p g two c", two=2, c=HD)[:, :, par, :]

                    for par in range(2):
                        eg = SM[:, 9, 6:12].rearrange("p (g two) -> p g two", two=2)[:, :, par].unsqueeze(2)\
                            .broadcast_to([P, 3, HD])
                        dve.wait_ge(*after("filled", "ks", l, par))
                        ps = psum("ks", l, par)
                        do(dve.tensor_tensor(parity(VN[:, 1, :], par), h6(ps[:, 0:3 * HD]), eg, ALU.mult))
                        do(dve.tensor_tensor(parity(O[:, 1, :], par), h6(ps[:, 3 * HD:6 * HD]), eg, ALU.mult),
                           "read", "ks", l, par)
                    own()
                    do(dve.tensor_tensor(BV[:, 1, :], BV[:, 1, :], VN[:, 1, :], ALU.subtract), "bv1", l)
                    dve.wait_ge(*after("filled", "o1", l))
                    do(dve.tensor_tensor(O[:, 1, :], psum("o1", l)[:, 0:HW], O[:, 1, :], ALU.add), "read", "o1", l)
                    dve.wait_ge(*after("silu_z", l))
                    head_norm("o", O, 1.0, NH, ("o_sq", l), HD, "o_scaled")
                    own()
                    for t in range(TT):
                        v = h6(O[:, t, :])
                        do(dve.tensor_tensor(v, v, wide("dn_onorm_2", l, HD).unsqueeze(1).broadcast_to([P, NH, HD]),
                                             ALU.mult))
                    own()
                    do(dve.tensor_tensor(O[:, :, :], O[:, :, :], ZAB[:, :, 0:HW], ALU.mult), "dn_out", l)
                    add_residual("wout2", l)
                    norm(i0 + 1, X, "norm2_2", 8 * l, HT)
                    if l == 0:
                        for i in range(GU2):
                            for c in range(2):
                                n = 2 * i + c
                                dve.wait_ge(*after("silu", "ffn", i, c))
                                if i // 2 >= 3:
                                    dve.wait_ge(*after("down", "ffn", i // 2 - 3))
                                do(dve.tensor_tensor(UH[:, i // 2 % 3, 2 * (i % 2) + c, :], SG[:, n % 2, 0:S],
                                                     psum("gu", i, c)[:, S:2 * S], ALU.mult), "hidden", "ffn", i, c)
                                cdve.also("read", "gu", i, c)
                        dve.wait_ge(*after("down", "ffn", DN2 - 1))
                        add_banks("x", "ffn")
                        continue

                    LG = GATE
                    dve.wait_ge(*after("filled", "router"))
                    do(dve.tensor_copy(LG[:, :, :], psum("router")[:, 0:TT * NE].rearrange("p (t e) -> p t e", t=TT)),
                       "read", "router")
                    own()
                    RKs = SM[:, 0, :].rearrange("p (t e) -> p t e", t=TT)
                    lane = SM[:, 1, 0:NE]
                    hot = SM[:, 4, :].rearrange("p (t e) -> p t e", t=TT)
                    hot2 = SM[:, 5, :].rearrange("p (t e) -> p t e", t=TT)
                    cur = SM[:, 6, :].rearrange("p (t e) -> p t e", t=TT)
                    m1, m2, mr = SM[:, 7, 0:2], SM[:, 7, 2:4], SM[:, 7, 4:6]
                    for k in range(NE):
                        do(dve.memset(lane[:, k:k + 1], float(NE - k)))
                    own()

                    def bce(v):
                        return v.unsqueeze(2).broadcast_to([P, TT, NE])

                    def one_hot(src, m, dst):
                        do(dve.tensor_reduce(m, src, AX.X, ALU.max))
                        own()
                        do(dve.tensor_tensor(RKs, src, bce(m), ALU.is_equal))
                        own()
                        do(dve.tensor_tensor(RKs, RKs, lane.unsqueeze(1).broadcast_to([P, TT, NE]), ALU.mult))
                        own()
                        do(dve.tensor_reduce(mr, RKs, AX.X, ALU.max))
                        own()
                        do(dve.tensor_tensor(dst, RKs, bce(mr), ALU.is_equal))
                        own()

                    one_hot(LG, m1, hot)
                    do(dve.scalar_tensor_tensor(cur, hot, NEG, LG, ALU.mult, ALU.add))
                    own()
                    one_hot(cur, m2, hot2)
                    do(dve.tensor_tensor(hot, hot, hot2, ALU.add), "hot")
                    do(dve.tensor_tensor(SM[:, 2, :].rearrange("p (t e) -> p t e", t=TT), LG, bce(m1), ALU.subtract),
                       "logit_shift")
                    dve.wait_ge(*after("gate_exp"))
                    own()
                    ex = SM[:, 3, :].rearrange("p (t e) -> p t e", t=TT)
                    do(dve.tensor_tensor(ex, ex, hot, ALU.mult))
                    own()
                    do(dve.tensor_reduce(mr, ex, AX.X, ALU.add))
                    own()
                    do(dve.reciprocal(m2, mr))
                    own()
                    do(dve.tensor_tensor(GATE[:, :, :], ex, bce(m2), ALU.mult))
                    rank = SM[:, 9, :].rearrange("p (t e) -> p t e", t=TT)
                    picked = SM[:, 10, :].rearrange("p (t e) -> p t e", t=TT)
                    over, nth, which = SM[:, 11, 0:NE], SM[:, 12, 0:NE], SM[:, 13, 0:NE]
                    wsum = SM[:, 14, 0:NE]
                    do(dve.memset(PG[:, :, :], -1.0))
                    for e in range(NE):
                        do(dve.memset(ITEM[0:1, e:e + 1], e))
                    do(dve.memset(ITEM[0:1, NE:16], 0))
                    dve.wait_ge(*after("filled", "ranks"))
                    ps = psum("ranks")
                    do(dve.tensor_tensor(rank, ps[:, 0:2 * NE].rearrange("p (t e) -> p t e", t=TT), hot, ALU.mult))
                    do(dve.tensor_scalar(over, ps[:, 2 * NE:3 * NE], float(P), None, ALU.is_gt), "read", "ranks")
                    own()
                    do(dve.tensor_scalar(PG[:, 0:NE, 0:2], rank.rearrange("p t e -> p e t"), -1.0, None, ALU.add))
                    do(dve.tensor_copy(PG[:, 0:NE, 2:4], GATE.rearrange("p t e -> p e t")))
                    own()
                    for t in range(TT):
                        do(dve.tensor_scalar(GSEL[:, t, :], iota, PG[:, 0, t:t + 1], None, ALU.is_equal), "select0")
                    do(dve.tensor_copy(nth[:, 0:1], over[:, 0:1]))
                    for e in range(1, NE):
                        own()
                        do(dve.tensor_tensor(nth[:, e:e + 1], nth[:, e - 1:e], over[:, e:e + 1], ALU.add))
                    own()
                    for j in range(MORE):
                        do(dve.scalar_tensor_tensor(which, nth, float(j + 1), over, ALU.is_equal, ALU.mult))
                        own()
                        wb = which.unsqueeze(1).broadcast_to([P, TT, NE])
                        do(dve.tensor_tensor(picked, rank, wb, ALU.mult))
                        own()
                        do(dve.tensor_reduce(mr, picked, AX.X, ALU.add))
                        own()
                        do(dve.tensor_scalar(PG[:, NE + j, 0:2], mr, -1.0 - P, None, ALU.add))
                        do(dve.tensor_tensor(picked, GATE, wb, ALU.mult))
                        own()
                        do(dve.tensor_reduce(PG[:, NE + j, 2:4], picked, AX.X, ALU.add))
                        do(dve.tensor_tensor(wsum, which, lane, ALU.mult))
                        own()
                        do(dve.tensor_reduce(m1[:, 0:1], wsum, AX.X, ALU.add))
                        own()
                        do(dve.tensor_scalar(m1[:, 0:1], m1[:, 0:1], -1.0, float(NE), ALU.mult, ALU.add))
                        own()
                        do(dve.tensor_scalar(ITEM[0:1, NE + j:NE + j + 1], m1[0:1, 0:1], float(NE - 1), None, ALU.min))
                    do(dve.tensor_scalar(ITEM[0:1, 15:16], nth[0:1, NE - 1:NE], float(NE), None, ALU.add), "items")
                    gain = [cols("norm2_2", 8 + 4 * part, 4).unsqueeze(2).broadcast_to([P, 4, P]) for part in range(2)]

                    def four(ps):
                        return ps[:, :].rearrange("p (k n) -> p k n", k=4)

                    for part in range(2):
                        dve.wait_ge(*after("filled", "gather", part))
                        do(dve.tensor_tensor(HG[:, 4 * part:4 * part + 4, :], four(psum("gather", part)), gain[part],
                                             ALU.mult), "read", "gather", part)
                    dve.wait_ge(*after("items"))
                    items = dve.value_load(ITEM[0:1, 15:16], min_val=NE, max_val=NE + MORE)
                    base = cdve.n
                    with dve.Fori(0, items) as i:
                        dve.wait_ge(*in_loop(i, "dve", "gathered", before=True))
                        do(dve.tensor_copy(PC[:, 0:4].unsqueeze(1), PG[:, bass.ds(i, 1), :]))
                        do(dve.tensor_copy(PC[:, 4:6].unsqueeze(1), PG[:, bass.ds(i + 1, 1), 0:2]), "item_row")
                        dve.wait_ge(*in_loop(i, "dve", "item_row"))
                        dve.wait_ge(*in_loop(i, "pe", "item", "scatterT", before=True))
                        for t in range(TT):
                            do(dve.tensor_scalar(GGATE[:, t, :], iota, PC[:, t:t + 1], PC[:, 2 + t:3 + t],
                                                 ALU.is_equal, ALU.mult), "gate_rows")
                        for n in range(3):
                            dve.wait_ge(*in_loop(i, "act", "item_read", f"gate{n}"))
                            dve.wait_ge(*in_loop(i, "pe", "item", f"up{n}"))
                            dve.wait_ge(*in_loop(i, "pe", "item", f"hT{n}", before=True))
                            do(dve.tensor_tensor(HH[:, n, :], SGE[:, n, :], item_bank(f"up{n}")[:, :], ALU.mult),
                               "hh", n)
                            cdve.also("item_read", f"up{n}")
                            if n == 1:
                                dve.wait_ge(*in_loop(i, "pe", "item", "gather1", before=True))
                                for t in range(TT):
                                    do(dve.tensor_scalar(GSEL[:, t, :], iota, PC[:, 4 + t:5 + t], None, ALU.is_equal),
                                       "select")
                        for part in range(2):
                            dve.wait_ge(*in_loop(i, "pe", "item", f"gather{part}"))
                            do(dve.tensor_tensor(HG[:, 4 * part:4 * part + 4, :], four(item_bank(f"gather{part}")),
                                                 gain[part], ALU.mult), "item_read", f"gather{part}")
                        cdve.also("gathered")
                    points[("per", "dve")] = ("dve", cdve.n - base)
                    dve.wait_ge(*in_loop(items - 1, "pe", "item", "scatter"))
                    for b in range(4):
                        dve.tensor_copy(X[:, b // 2, (b % 2) * 512:(b % 2 + 1) * 512], banks[b][:, :])\
                           .then_inc(moe_out, 1)


_INS = ['x', 'mem', 'norm_mix_g', 'w_in', 'conv_w', 'conv_b', 'conv_ln_g', 'conv_ln_b', 'w_out', 'norm_x_g',
        'norm_mem_g', 'w_xq', 'w_xk', 'w_xv', 'w_xo', 'norm_mlp_g', 'w_up', 'w_down', 'norm_final_g', 'norm1_2',
        'w_in_2', 'dn_conv_2', 'dn_a_log_2', 'dn_dt_bias_2', 'dn_onorm_2', 'fx_qnorm_2', 'fx_knorm_2',
        'fx_f_bias_2', 'pool_w_2', 'pool_scale_2', 'w_out_2', 'norm2_2', 'ffn_gate_2', 'ffn_up_2', 'ffn_down_2',
        'router_2', 'moe_gate_2', 'moe_up_2', 'moe_down_2']
_OUTS = [((1, S, D), 'float32')]
STOP = 0


def kernel(**inputs):
    import numpy as _np
    import concourse.bacc as _bacc
    from concourse import mybir as _mybir
    from concourse.bass_utils import run_bass_kernel_spmd as _run

    arrays = {f"in_{name}_dram": _np.ascontiguousarray(inputs[name]) for name in _INS}
    arrays["in_table_dram"] = table()
    points = {}
    for _ in range(2):
        nc = _bacc.Bacc("TRN2", target_bir_lowering=False, num_devices=1)
        args = {name[3:-5]: nc.dram_tensor(name, a.shape, _mybir.dt.from_np(a.dtype), kind="ExternalInput").ap()
                for name, a in arrays.items()}
        outs = [nc.dram_tensor(f"out_{i}_dram", shape, _mybir.dt.from_np(_np.dtype(dtype)), kind="ExternalOutput").ap()
                for i, (shape, dtype) in enumerate(_OUTS)]
        program(nc, args, outs[0], points, STOP)
    r = _run(nc, [arrays], core_ids=[0])
    return r.results[0]["out_0_dram"]
```

```python
import numpy as np
import concourse.bass as bass
from concourse import mybir
from contextlib import ExitStack

F32 = mybir.dt.float32
F32R = mybir.dt.float32r
ACT = mybir.ActivationFunctionType
ALU = mybir.AluOpType
AX = mybir.AxisListType

P = 128
S = 256
TT = S // P
D = 1024
KD_ = D // P
HD = 64
EPS = 1e-6
NEG = -1e30
ATT = 512
AH = ATT // HD
TAPS = 31
PAD = TAPS // 2
XH = 4
MLP_SLOTS = 8
LAYERS = 2
NH = 6
HW = NH * HD
DTAPS = 4
FF2 = 2816
FFE = 1536
NE = 8
TOP = 2
MORE = (TOP * S - 1) // (P + 1) if TOP * S < NE * (P + 1) else NE
RING = 3
SPLIT = 2
SLOT = 2048
LEVELS = 7

TABLE = {}
TABLE_COLS = 0
for _name, _n in (("ident", P), ("logc", TT * S), ("causal", TT * S), ("upper", P), ("ones", P),
                  ("levels", LEVELS * P), ("poolinv", TT * S), ("cos", TT * 8), ("sin", TT * 8),
                  ("iota", P), ("sel", NH * P)):
    TABLE[_name] = (TABLE_COLS, _n)
    TABLE_COLS += _n


def table():
    t = np.zeros((P, TABLE_COLS), np.float32)

    def put(name, a):
        at, n = TABLE[name]
        t[:a.shape[0], at:at + n] = a.reshape(a.shape[0], n)

    p = np.arange(P)
    put("ident", np.eye(P))
    q = (np.arange(TT)[None, :, None] * P + p[:, None, None])
    k = np.arange(S)[None, None, :]
    count = (np.abs(q - k) <= 64).astype(int) + ((q - k) % 4 == 0) + ((q - k) % 16 == 0)
    put("logc", np.where(count > 0, np.log(np.maximum(count, 1)), NEG))
    put("causal", np.where(k <= q, 0.0, NEG))
    put("upper", p[:, None] <= p[None, :])
    put("ones", np.ones((P, P)))
    lev = []
    for n in range(LEVELS):
        b = 1 << n
        j, i = p[:, None], p[None, :]
        lev.append((j // (2 * b) == i // (2 * b)) & (j // b % 2 == 0) & (i // b % 2 == 1))
    put("levels", np.stack(lev, 1))
    win = np.array([[2, 4], [8, 16]])[:, p // 64].T
    put("poolinv", 1.0 / np.minimum(np.arange(S)[None, None, :] + 1, win[:, :, None]))
    freqs = (np.float32(500000.0) ** (-np.arange(0, 16, 2, dtype=np.float32) / np.float32(16))).astype(np.float32)
    ang = (np.arange(S, dtype=np.float32)[:, None] * freqs[None, :]).astype(np.float32)
    ang = ang.reshape(TT, P, 8).transpose(1, 0, 2)
    put("cos", np.cos(ang))
    put("sin", np.sin(ang))
    put("iota", np.tile(np.arange(P), (P, 1)))
    sel = np.zeros((NH, NH, P))
    sel[np.arange(NH), np.arange(NH)] = 1.0
    put("sel", sel)
    return t


ROWS = [
    [("norm_mix_g", 8), ("norm_x_g", 8), ("norm_mem_g", 8), ("norm_mlp_g", 8), ("norm1_2", 16), ("norm2_2", 16)],
    [("conv_w", 124)],
    [("conv_b", 4), ("conv_ln_g", 4), ("conv_ln_b", 4), ("pool_scale_2", 4), ("dn_conv_2", 72)],
]
COLS = {}
_at = 0
for _tile in ROWS:
    for _name, _n in _tile:
        COLS[_name] = _at
        _at += _n
NCOLS = _at

WIDE = {}
_at = 0
for _name, _n in (("norm_final_g", D), ("fx_qnorm_2", LAYERS * HD), ("fx_knorm_2", LAYERS * HD),
                  ("dn_onorm_2", LAYERS * HD), ("dn_a_log_2", LAYERS * NH), ("dn_dt_bias_2", LAYERS * NH),
                  ("fx_f_bias_2", LAYERS * NH)):
    WIDE[_name] = (_at, _n)
    _at += _n
NWIDE = _at


class Counter:

    def __init__(self, sem, key, points):
        self.sem, self.key, self.points, self.n = sem, key, points, 0

    def mark(self, *name):
        self.n += 1
        if name:
            self.points[name] = (self.key, self.n)
        return self.sem, 1

    def also(self, *name):
        self.points[name] = (self.key, self.n)

    def last(self, back=0):
        return self.sem, self.n - back


def program(nc, A, out, points, stop):
    ctx = ExitStack()
    with ctx:
        def sb(name, shape, dt=F32):
            return ctx.enter_context(nc.sbuf_tensor(name, shape, dt))

        def sem(name):
            return ctx.enter_context(nc.semaphore(name))

        T_ = sb("shape_table", [P, TABLE_COLS])
        X = sb("residual", [P, TT, D])
        XN = sb("normed", [P, TT, D])
        AB = sb("features_split", [P, 2, KD_, S], F32R)
        HB = sb("hidden_split", [P, 2, 2048], F32R)
        W = sb("weights", [P, RING, SLOT])
        WS = sb("weights_split", [P, SPLIT, 2, SLOT], F32R)
        COL = sb("vector_cols", [P, NCOLS])
        WD = sb("vector_wide", [P, NWIDE])
        PR = sb("probs", [P, 3, TT, S])
        PT = sb("probsT", [P, 2, TT, S])
        PW = sb("pool_weights", [P, LAYERS, 2, P])
        RT = sb("router", [P, KD_, NE])
        NHALF = sb("minus_half", [P, 24])
        SS = sb("sumsq", [P, 48])
        MS = sb("meansq", [P, 48])
        RS = sb("rstd", [P, 48])
        NM = sb("negmax", [P, 3, TT])
        DEN = sb("den", [P, 3, TT])
        RDEN = sb("rden", [P, 3, TT])
        SM = sb("small", [P, 16, 16])
        ARENA = sb("arena", [P, 17400])
        ITEM = sb("items", [1, 16], mybir.dt.int32)

        def ar(at, *shape):
            n = int(np.prod(shape))
            v = ARENA[:, at:at + n]
            if len(shape) == 2:
                v = v.rearrange("p (a b) -> p a b", a=shape[0])
            elif len(shape) == 3:
                v = v.rearrange("p (a b c) -> p a b c", a=shape[0], b=shape[1])
            elif len(shape) == 4:
                v = v.rearrange("p (a b c d) -> p a b c d", a=shape[0], b=shape[1], c=shape[2])
            return v

        QK = ar(0, TT, 1024)
        QKT = ar(2048, 8, S)
        V = ar(4096, TT, ATT)
        U = ar(5120, 4, S + 2 * PAD)
        C = ar(6264, 4, S)
        SIG = ar(7288, 4, S)
        XKT = ar(8312, 8, S)
        XV = ar(10360, TT, 1024)
        MEM = ar(10360, TT, 1024)
        XQT = ar(12408, 8, S)
        T1 = ar(12408, KD_, S)
        GR = ar(14456, 3, P)
        RT1 = ar(14840, 4, 256)
        SG = ar(0, 2, 2 * S)
        PRD = ar(1024, 2, 2 * S)
        CI = ar(0, 9, S + 4)
        CO = ar(2340, 9, S)
        KB = ar(0, TT, HW)
        DI = ar(0, 12, P)
        DIT = ar(1536, 12, P)
        PM = ar(3072, 12, P)
        DD = ar(3072, 12, P)
        QT3 = ar(4644, TT, 3 * HW)
        O = ar(4644, TT, HW)
        VN = ar(5412, TT, HW)
        ZAB = ar(6948, TT, HW + 12)
        FQ = ar(7740, TT, 2 * HW)
        KQ = ar(7740, 3, TT, 2, P)
        FV = ar(9276, TT, HW + 6)
        KT = ar(10056, 3, TT, P)
        AQ = ar(10824, 12, 2, P)
        XP = ar(10824, 2, 16 + S)
        SA = ar(10824 + 544, 2, 16 + S)
        SBf = ar(10824 + 1088, 2, 16 + S)
        SC = ar(10824 + 1632, 2, 16 + S)
        YP = ar(10824 + 2176, 2, S)
        LT = XN[:, :, :].rearrange("p t n -> p (t n)")[:, 0:12 * P].rearrange("p (b c) -> p b c", c=P)
        BV = ar(13896, TT, HW)
        KDC = ar(14664, HW)
        FT = ar(15048, 6, S)
        NCT = ARENA[0:NH, 16584:16584 + S]
        GT = ARENA[0:NH, 16840:16840 + S]
        SST = ar(17096, 3, HD)
        GATE = ar(17288, TT, NE)
        T2 = ar(9276, KD_, S)
        GSEL = ar(0, TT, P)
        GGATE = ar(256, TT, P)
        HGT = ar(512, KD_, P)
        GST = ar(1536, TT, P)
        SGE = ar(1792, 3, 512)
        HH = ar(3328, 3, 512)
        Y = ar(6400, 2, 512)
        HG = AB[:, :, :, 0:P]
        HHT = HB[:, :, 0:12 * P].rearrange("p z (k n) -> p z k n", k=12)
        HT = CAT = AB
        MT = HB[:, :, :].rearrange("p z (k n) -> p z k n", k=KD_)
        UH = HB[:, :, :].rearrange("p z (b k n) -> p z b k n", b=2, k=4)
        PG = ar(7424, NE + MORE + 1, 4)
        PC = ar(7500, 8)
        SQ = XN[:, :, 0:2 * HW]

        def system(t, h):
            return (h % 2) * NH + t * (NH // 2) + h // 2

        def chunk_head(s):
            return s % NH // (NH // 2), 2 * (s % (NH // 2)) + s // NH

        ident = T_[:, 0:P]

        def tab(name, n=P):
            return T_[0:n, TABLE[name][0]:TABLE[name][0] + TABLE[name][1]]

        logc = tab("logc").rearrange("p (t k) -> p t k", t=TT)
        causal = tab("causal").rearrange("p (t k) -> p t k", t=TT)
        upper, ones, iota = tab("upper"), tab("ones"), tab("iota")
        upper_ones = T_[:, TABLE["upper"][0]:TABLE["upper"][0] + 2 * P]
        levels = tab("levels").rearrange("p (n k) -> p n k", n=LEVELS)
        poolinv = tab("poolinv").rearrange("p (t k) -> p t k", t=2)
        cos = tab("cos").rearrange("p (t k) -> p t k", t=TT)
        sin = tab("sin").rearrange("p (t k) -> p t k", t=TT)
        sel = tab("sel", NH).rearrange("p (h k) -> p h k", h=NH)

        def col(name, i=0):
            return COL[:, COLS[name] + i:COLS[name] + i + 1]

        def cols(name, i, n):
            return COL[:, COLS[name] + i:COLS[name] + i + n]

        def wide(name, l, n):
            at = WIDE[name][0] + l * n
            return WD[:, at:at + n]

        banks = [ctx.enter_context(nc.psum_tensor(f"bank{i}", [P, 512], F32)) for i in range(8)]
        SC_BANK, PT_BANK, RING_BANK = banks[0:2], banks[2:4], banks[4:8]

        matmul_done, scalar_done = sem("matmul_done"), sem("scalar_done")
        vector_done, pool_done = sem("vector_done"), sem("pool_done")
        x_in, mem_in, rows_in, table_in = sem("x_in"), sem("mem_in"), sem("rows_in"), sem("table_in")
        ident_in, moe_out = sem("ident_in"), sem("moe_out")
        wide_in, poolw_in, out_written = sem("wide_in"), sem("poolw_in"), sem("out_written")
        w_in = [sem(f"weights_in{i}") for i in range(RING)]
        sems = {"pe": matmul_done, "act": scalar_done, "dve": vector_done, "pool": pool_done}
        cpe = Counter(matmul_done, "pe", points)
        cact = Counter(scalar_done, "act", points)
        cdve = Counter(vector_done, "dve", points)
        cpool = Counter(pool_done, "pool", points)

        def after(*name):
            key, n = points.get(name, ("pe", 1))
            return sems[key], n

        def in_loop(e, key, *name, before=False):
            n = points.get(name, (key, 1))[1]
            per = points.get(("per", key), (key, 1))[1]
            return sems[key], e * per + max(1, n - per if before else n)

        slots = []

        def kview(w, a, b):
            return w[:, a:b].rearrange("(k p) n -> p k n", p=P)

        def slot_f(stage, w, a, b):
            for c in range(a, b, 256):
                slots.append((stage, kview(w, c, min(c + 256, b))))

        def slot_t(stage, w, a, b):
            for r in range(2):
                slots.append((stage, kview(w[r * 512:(r + 1) * 512], a, b)))

        def slot_d(stage, w, r, n):
            for k in range(0, n, 2):
                slots.append((stage, kview(w[r + k * P:r + (k + 2) * P], 0, D)))

        w1 = A["w_in"][0]
        for name, at in (("g", 4), ("a", 3), ("q", 0), ("k", 1), ("v", 2)):
            (slot_f if name in "ga" else slot_t)(name, w1, at * ATT, (at + 1) * ATT)
        for i in range(2):
            slot_f("xk", A["w_xk"][0], i * 512, i * 512 + 512)
        for i in range(2):
            slot_t("xv", A["w_xv"][0], i * 512, i * 512 + 512)
        for i in range(2):
            slot_t("wout", A["w_out"][0], i * 512, i * 512 + 512)
        for i in range(2):
            slot_f("xq", A["w_xq"][0], i * 512, i * 512 + 512)
        for i in range(2):
            slot_t("xo", A["w_xo"][0], i * 512, i * 512 + 512)
        for i in range(MLP_SLOTS + 1):
            if i < MLP_SLOTS:
                slot_f("up", A["w_up"][0], i * 512, i * 512 + 512)
            if i >= 1:
                slot_d("down", A["w_down"][0], (i - 1) * 512, 4)
        N1 = len(slots)
        GU2 = FF2 // 256
        DN2 = (GU2 + 1) // 2
        for l in range(LAYERS):
            w2 = A["w_in_2"][l]
            slot_f("cqkv", w2, 0, 3 * HW)
            slot_f("pool", w2, 2706, 2962)
            slot_t("zab", w2, 1152, 1548)
            slot_t("fq", w2, 1548, 1932)
            slot_t("fk", w2, 1932, 2316)
            slot_t("fv", w2, 2316, 2706)
            for i in range(2):
                slot_t("wout2", A["w_out_2"][l], i * 512, i * 512 + 512)
            if l == 0:
                for i in range(GU2):
                    slot_f("gate", A["ffn_gate_2"][0], i * 256, i * 256 + 256)
                    slot_f("gate", A["ffn_up_2"][0], i * 256, i * 256 + 256)
                    if i >= 2 and i % 2 == 0:
                        slot_d("dn", A["ffn_down_2"][0], (i - 2) * 256, 4)
                slot_d("dn", A["ffn_down_2"][0], (DN2 - 1) * 512, FF2 // P - 4 * (DN2 - 1))
        EXPERT0 = len(slots)
        EXPERT = ["gate"] * 2 + ["up"] * 2
        EXPERT = EXPERT * 3 + ["down"] * 6

        def expert_src(s, e):
            if s >= 12:
                src = A["moe_down_2"][0, bass.ds(e, 1), (s - 12) * 2 * P:(s - 11) * 2 * P, :]
            else:
                n, r = s // 4, s % 2
                src = A[f"moe_{EXPERT[s]}_2"][0, bass.ds(e, 1), r * 512:(r + 1) * 512, n * 512:(n + 1) * 512]
            return src.rearrange("e (k p) n -> p (e k) n", p=P)

        for s in range(SPLIT):
            slots.append(("expert", expert_src(s, 0)))
        loads = []
        total = [0] * RING
        for j in range(len(slots)):
            total[j % RING] += 16
            loads.append(total[j % RING])
        NX = len(EXPERT)
        PER_RING = 16 * NX // RING
        expert_loads = [16 * ((EXPERT0 + s) // RING + 1) for s in range(NX + SPLIT)]

        def shape_of(j):
            return slots[j][1].shape[1], slots[j][1].shape[2]

        def raw(j, k, n):
            return W[:, j % RING, 0:k * n].rearrange("p (k n) -> p k n", k=k)

        def split_view(j, k, n):
            return WS[:, j % SPLIT, :, 0:k * n].rearrange("p z (k n) -> p z k n", k=k)

        ITEM_JOBS = ["gate0", "up0", "scatterT", "gate1", "up1", "hT0", "gate2", "up2", "hT1", "down0", "down1",
                     "hT2", "gather0", "gather1"]

        ITEM_BANKS = [0, 1, 2, 3, 0, 1, 2, 3, 0, 1, 2, 3, 0, 3]

        def item_bank(name):
            return RING_BANK[ITEM_BANKS[ITEM_JOBS.index(name)]]

        def item_reader_before(name):
            n = ITEM_JOBS.index(name)
            same = [m for m in range(len(ITEM_JOBS)) if ITEM_BANKS[m] == ITEM_BANKS[n]]
            at = same.index(n)
            return ITEM_JOBS[same[at - 1]], at == 0

        bank_of = {}
        order = []

        with nc.Block() as block:

            @block.tensor
            def _(pe):
                nslot = [0]

                def weights(stage):
                    j = nslot[0]
                    assert slots[j][0] == stage, (j, slots[j][0], stage)
                    nslot[0] += 1
                    pe.wait_ge(*after("lo", j))
                    return j, split_view(j, *shape_of(j))

                def matmul3(ps, lhs, rhs, start, stop):
                    pe.matmul(ps, lhs(0), rhs(0), start=start, stop=False)
                    pe.matmul(ps, lhs(0), rhs(1), start=False, stop=False)
                    return pe.matmul(ps, lhs(1), rhs(0), start=False, stop=stop)

                def open_bank(*name):
                    k = len(order)
                    if k >= 4:
                        pe.wait_ge(*after("read", *order[k - 4]))
                    order.append(name)
                    bank_of[name] = RING_BANK[k % 4]
                    return RING_BANK[k % 4]

                def tokens_out(stage, actT, n, i=0, tag=()):
                    ps = []
                    for r in range(2):
                        j, w = weights(stage)
                        for t in range(TT):
                            if r == 0:
                                ps.append(open_bank(stage, *tag, i, t))
                            for k in range(4):
                                mm = matmul3(ps[t][:, 0:n], lambda z: actT[:, z, 4 * r + k, t * P:(t + 1) * P],
                                             lambda z: w[:, z, k, :], r == 0 and k == 0, r == 1 and k == 3)
                            if r == 1:
                                mm.then_inc(*cpe.mark("filled", stage, *tag, i, t))
                            elif t == 1:
                                mm.then_inc(*cpe.mark("slot", j))
                    cpe.also("slot", j)

                def features_out(stage, actT, *name):
                    j, w = weights(stage)
                    ps = open_bank(*name)
                    for c in range(0, shape_of(j)[1], P):
                        for k in range(KD_):
                            mm = matmul3(ps[:, 2 * c:2 * c + S], lambda z: w[:, z, k, c:c + P],
                                         lambda z: actT[:, z, k, :], k == 0, k == KD_ - 1)
                    mm.then_inc(*cpe.mark("filled", *name))
                    cpe.also("slot", j)

                def turn_norm(i):
                    for t in range(TT):
                        pe.wait_ge(*after("xn", i, t))
                        for b in range(2):
                            ps = open_bank("normT", i, t, b)
                            for k in range(4):
                                mm = pe.transpose(ps[:, k * P:(k + 1) * P],
                                                  XN[:, t, (4 * b + k) * P:(4 * b + k + 1) * P], ident)
                            mm.then_inc(*cpe.mark("filled", "normT", i, t, b))

                def attention(u0, heads, scores, outs, paired=False, between=lambda s: None):
                    for s in range(heads + 2):
                        if s < heads:
                            u = u0 + s
                            if u >= 2:
                                pe.wait_ge(*after("scores_read", u - 2))
                            scores(s, SC_BANK[u % 2]).then_inc(*cpe.mark("scores", u))
                        if 1 <= s <= heads:
                            u = u0 + s - 1
                            pe.wait_ge(*after("probs", u))
                            if u >= 2:
                                pe.wait_ge(*after("pt_copied", u - 2))
                            ps = PT_BANK[u % 2]
                            for kt in range(TT):
                                for qt in range(TT):
                                    mm = pe.transpose(ps[:, kt * S + qt * P:kt * S + (qt + 1) * P],
                                                      PR[:, u % 3, qt, kt * P:(kt + 1) * P], ident)
                            mm.then_inc(*cpe.mark("pt", u))
                        if s >= 2 and not (paired and s % 2 == 0):
                            for h in (s - 3, s - 2) if paired else (s - 2,):
                                u = u0 + h
                                pe.wait_ge(*after("pt_copied", u))
                                outs(h, PT[:, u % 2], u)
                        between(s)

                def pair_outs(stage, tag, v):
                    def outs(h, pt, u):
                        if h % 2 == 0:
                            ps = open_bank(stage, *tag, h // 2)
                        else:
                            ps = bank_of[(stage, *tag, h // 2)]
                        o = 64 * (h % 2)
                        for kt in range(TT):
                            mm = pe.matmul(ps[o:o + HD, 0:S], v[:, kt, h * HD:(h + 1) * HD], pt[:, kt, :],
                                           start=(kt == 0), stop=(kt == TT - 1))
                        mm.then_inc(*cpe.mark("o", u))
                        if h % 2:
                            cpe.also("filled", stage, *tag, h // 2)
                    return outs

                pe.wait_ge(rows_in, 16 * 12)
                pe.wait_ge(ident_in, 16)
                ps = open_bank("cols")
                at = 0
                for i, n in enumerate((64, 124, 88)):
                    mm = pe.transpose(ps[:, at:at + n], GR[0:n, i, :], ident[0:n, 0:n])
                    at += n
                mm.then_inc(*cpe.mark("filled", "cols"))

                turn_norm(0)
                pe.wait_ge(*after("ht", 0))
                for b in range(2):
                    features_out("g", HT, "g", b)
                for b in range(2):
                    features_out("a", HT, "a", b)
                tokens_out("q", HT, 512)
                tokens_out("k", HT, 512)
                turn_norm(1)
                tokens_out("v", HT, 512)
                pe.wait_ge(*after("ht", 1))
                for i in range(4):
                    features_out("xk", MT, "xk", i)
                for i in range(2):
                    tokens_out("xv", MT, 512, i)
                pe.wait_ge(*after("rotated"))
                for b in range(4):
                    ps = open_bank("qkT", b)
                    for c in range(2):
                        for t in range(TT):
                            mm = pe.transpose(ps[:, c * S + t * P:c * S + (t + 1) * P],
                                              QK[:, t, (2 * b + c) * P:(2 * b + c + 1) * P], ident)
                    mm.then_inc(*cpe.mark("filled", "qkT", b))
                pe.wait_ge(*after("read", "qkT", 3))
                pe.wait_ge(*after("read", "v", 0, 1))

                def scores1(h, ps):
                    o = 64 * (h % 2)
                    for t in range(TT):
                        mm = pe.matmul(ps[:, t * S:(t + 1) * S], QKT[o:o + HD, h // 2, t * P:(t + 1) * P],
                                       QKT[o:o + HD, 4 + h // 2, :], start=True, stop=True)
                    return mm

                attention(0, AH, scores1, pair_outs("att_o", (), V))
                for name, need in (("cmean", "conv"), ("cvar", "csq")):
                    pe.wait_ge(*after(need))
                    src = C if name == "cmean" else SIG
                    ps = open_bank(name)
                    for k in range(4):
                        mm = pe.matmul(ps[:, 0:S], ones, src[:, k, :], start=(k == 0), stop=(k == 3))
                    mm.then_inc(*cpe.mark("filled", name))
                pe.wait_ge(*after("convT"))
                pe.wait_ge(*after("read", "att_o", 3))
                for i in range(2):
                    tokens_out("wout", CAT, 512, i)

                turn_norm(2)
                pe.wait_ge(*after("ht", 2))
                for i in range(4):
                    features_out("xq", HT, "xq", i)
                pe.wait_ge(*after("read", "xq", 3))
                pe.wait_ge(*after("read", "xv", 1, 1))

                def scoresx(h, ps):
                    for t in range(TT):
                        for c in range(2):
                            mm = pe.matmul(ps[:, t * S:(t + 1) * S], XQT[:, 2 * h + c, t * P:(t + 1) * P],
                                           XKT[:, 2 * h + c, :], start=(c == 0), stop=(c == 1))
                    return mm

                def outsx(h, pt, u):
                    ps = open_bank("xatt_o", h)
                    for c in range(2):
                        for kt in range(TT):
                            mm = pe.matmul(ps[:, c * S:(c + 1) * S],
                                           XV[:, kt, h * 256 + c * P:h * 256 + (c + 1) * P], pt[:, kt, :],
                                           start=(kt == 0), stop=(kt == TT - 1))
                    mm.then_inc(*cpe.mark("o", u))
                    cpe.also("filled", "xatt_o", h)

                attention(AH, XH, scoresx, outsx)
                pe.wait_ge(*after("read", "xatt_o", 3))
                for i in range(2):
                    tokens_out("xo", CAT, 512, i)

                def down(stage, hbuf, n, first, last, *done):
                    for r in range(0, n, 2):
                        j, w = weights(stage)
                        for k in range(2):
                            for t in range(TT):
                                for c in range(2):
                                    mm = matmul3(banks[2 * t + c][:, :],
                                                 lambda z: HB_[:, z, hbuf, r + k, t * P:(t + 1) * P],
                                                 lambda z: w[:, z, k, c * 512:(c + 1) * 512],
                                                 first and r == 0 and k == 0, last and r == n - 2 and k == 1)
                        mm.then_inc(*cpe.mark("slot", j))
                    cpe.also(*done)

                HB_ = UH
                turn_norm(3)
                pe.wait_ge(*after("ht", 3))
                for i in range(MLP_SLOTS + 1):
                    if i < MLP_SLOTS:
                        for b in range(2):
                            features_out("up", HT, "up", i, b)
                    if i >= 1:
                        if i == 1:
                            pe.wait_ge(*after("scores_read", AH + XH - 1))
                            pe.wait_ge(*after("pt_copied", AH + XH - 1))
                        pe.wait_ge(*after("hidden", "mlp", i - 1, 1))
                        down("down", (i - 1) % 2, 4, i == 1, i == MLP_SLOTS, "down", "mlp", i - 1)

                if stop == 1:
                    return

                for l in range(LAYERS):
                    turn_norm(5 + 2 * l)
                    pe.wait_ge(*after("ht", 5 + 2 * l))
                    for i in range(5):
                        features_out("cqkv", HT, "cqkv", l, i)
                    features_out("pool", HT, "pool", l)
                    tokens_out("zab", HT, HW + 12, 0, (l,))
                    for name, n in (("fq", HW), ("fk", HW), ("fv", HW + 6)):
                        tokens_out(name, HT, n, 0, (l,))
                    pe.wait_ge(*after("pooled", l))
                    if l == 0:
                        pe.wait_ge(poolw_in, 16 * 8)
                        pe.wait_ge(*after("poolw_zero"))
                    ps = open_bank("poolw", l)
                    for i in range(2):
                        mm = pe.matmul(ps[:, i * S:(i + 1) * S], PW[:, l, i, :], YP[:, i, :], start=True, stop=True)
                    mm.then_inc(*cpe.mark("filled", "poolw", l))
                    for b in range(5):
                        ps = open_bank("dnT", l, b)
                        for c in range(2 * b, min(2 * b + 2, 9)):
                            pe.wait_ge(*after("conv2", l, c))
                            for t in range(TT):
                                mm = pe.transpose(ps[:, t * S + (c % 2) * P:t * S + (c % 2 + 1) * P],
                                                  CO[:, c, t * P:(t + 1) * P], ident)
                        mm.then_inc(*cpe.mark("filled", "dnT", l, b))
                    pe.wait_ge(*after("gates", l))
                    ps = open_bank("cum", l)
                    g, nf = SM[:, 0, 0:12], SM[:, 1, 0:12]
                    for t in range(TT):
                        pe.matmul(ps[:, 6 * t:6 * t + 6], upper, g[:, 6 * t:6 * t + 6], start=True, stop=True)
                        pe.matmul(ps[0:NH, 128 + t * P:128 + (t + 1) * P], g[:, 6 * t:6 * t + 6], upper,
                                  start=True, stop=True)
                        mm = pe.matmul(ps[:, 16 + 6 * t:22 + 6 * t], ones, g[:, 6 * t:6 * t + 6],
                                       start=True, stop=True)
                    mm.then_inc(*cpe.mark("filled", "cum", l))
                    ps = open_bank("ncum", l)
                    pe.matmul(ps[0:NH, 0:S], nf[:, 0:6], upper_ones, start=True, stop=False)
                    pe.matmul(ps[0:NH, P:S], nf[:, 6:12], upper, start=False, stop=True)\
                      .then_inc(*cpe.mark("filled", "ncum", l))
                    pe.wait_ge(*after("fx_normed", l))
                    for b in range(3):
                        ps = open_bank("fT", l, b)
                        for c in range(2):
                            for t in range(TT):
                                mm = pe.transpose(ps[:, c * S + t * P:c * S + (t + 1) * P],
                                                  FQ[:, t, (2 * b + c) * P:(2 * b + c + 1) * P], ident)
                        mm.then_inc(*cpe.mark("filled", "fT", l, b))
                    for p in range(3):
                        pe.wait_ge(*after("dn_ready", l))
                        ps = open_bank("kqT", l, p)
                        for t in range(TT):
                            pe.transpose(ps[:, (2 * t) * P:(2 * t + 1) * P], KB[:, t, p * P:(p + 1) * P], ident)
                            mm = pe.transpose(ps[:, (2 * t + 1) * P:(2 * t + 2) * P],
                                              QT3[:, t, p * P:(p + 1) * P], ident)
                        mm.then_inc(*cpe.mark("filled", "kqT", l, p))
                    for p in range(3):
                        ps = open_bank("kT", l, p)
                        for t in range(TT):
                            mm = pe.transpose(ps[:, t * P:(t + 1) * P],
                                              QT3[:, t, HW + p * P:HW + (p + 1) * P], ident)
                        mm.then_inc(*cpe.mark("filled", "kT", l, p))
                    pe.wait_ge(*after("read", "cum", l))
                    for b in range(4):
                        ps = open_bank("grow", l, b)
                        for c in range(3):
                            t, h = chunk_head(3 * b + c)
                            mm = pe.matmul(ps[:, c * P:(c + 1) * P], sel[:, h, :], GT[:, t * P:(t + 1) * P],
                                           start=True, stop=True)
                        mm.then_inc(*cpe.mark("filled", "grow", l, b))
                    pe.wait_ge(*after("read", "kT", l, 2))
                    for b in range(6):
                        ps = open_bank("aq", l, b)
                        for c in range(2):
                            t, h = chunk_head(2 * b + c)
                            o = 64 * (h % 2)
                            mm = pe.matmul(ps[:, c * S:(c + 1) * S], KT[o:o + HD, h // 2, t, :],
                                           KQ[o:o + HD, h // 2, t, :, :].rearrange("p a b -> p (a b)"),
                                           start=True, stop=True)
                        mm.then_inc(*cpe.mark("filled", "aq", l, b))

                    pe.wait_ge(*after("read", "fT", l, 2))
                    pe.wait_ge(*after("read", "ncum", l))

                    def scores2(h, ps):
                        o = 64 * (h % 2)
                        for t in range(TT):
                            pe.matmul(ps[:, t * S:(t + 1) * S], FT[o:o + HD, h // 2, t * P:(t + 1) * P],
                                      FT[o:o + HD, 3 + h // 2, :], start=True, stop=False)
                            mm = pe.matmul(ps[:, t * S:(t + 1) * S], sel[:, h, :], NCT, start=False, stop=True)
                        return mm

                    if l == 0:
                        pe.wait_ge(*after("x", "mlp"))
                    else:
                        pe.wait_ge(*after("x", "ffn"))
                    def inverse_level(lev):
                        if lev >= LEVELS:
                            return
                        for gi in range(3):
                            sy = range(4 * gi, 4 * gi + 4)
                            pe.wait_ge(*after("level", l, lev, gi))
                            if lev == 0:
                                ps = open_bank("inv0", l, gi)
                                for i, s in enumerate(sy):
                                    mm = pe.transpose(ps[:, i * P:(i + 1) * P], LT[:, s, :], ident)
                                mm.then_inc(*cpe.mark("filled", "inv0", l, gi))
                                continue
                            pe.wait_ge(*after("inv", l, lev - 1, gi))
                            ps = open_bank("invp", l, lev, gi)
                            for i, s in enumerate(sy):
                                mm = pe.matmul(ps[:, i * P:(i + 1) * P], LT[:, s, :], DI[:, s, :],
                                               start=True, stop=True)
                            mm.then_inc(*cpe.mark("filled", "invp", l, lev, gi))
                        if lev == 0:
                            return
                        for gi in range(3):
                            sy = range(4 * gi, 4 * gi + 4)
                            pe.wait_ge(*after("read", "invp", l, lev, gi))
                            if lev < LEVELS - 1:
                                ps = open_bank("invd", l, lev, gi)
                                for i, s in enumerate(sy):
                                    mm = pe.matmul(ps[:, i * P:(i + 1) * P], DIT[:, s, :], PM[:, s, :],
                                                   start=True, stop=True)
                                mm.then_inc(*cpe.mark("filled", "invd", l, lev, gi))
                            ps = open_bank("invt", l, lev, gi)
                            for i, s in enumerate(sy):
                                mm = pe.matmul(ps[:, i * P:(i + 1) * P], PM[:, s, :], DIT[:, s, :],
                                               start=True, stop=True)
                            mm.then_inc(*cpe.mark("filled", "invt", l, lev, gi))

                    attention(AH + XH + NH * l, NH, scores2, pair_outs("fx_o", (l,), FV), True, inverse_level)
                    pe.wait_ge(*after("inv", l, LEVELS - 1, 2))

                    def per_head(name, lhs, rhs):
                        ps = open_bank(name, l)
                        for h in range(NH):
                            mm = pe.matmul(ps[:, h * HD:(h + 1) * HD], lhs(h), rhs(h), start=True, stop=True)
                        mm.then_inc(*cpe.mark("filled", name, l))

                    def hs(h):
                        return slice(h * HD, (h + 1) * HD)

                    pe.wait_ge(*after("bv", l))
                    per_head("vn0", lambda h: DIT[:, system(0, h), :], lambda h: BV[:, 0, hs(h)])
                    pe.wait_ge(*after("read", "vn0", l))
                    ps = open_bank("state", l)
                    for h in range(NH):
                        o = 64 * (h % 2)
                        mm = pe.matmul(ps[o:o + HD, (h // 2) * HD:(h // 2 + 1) * HD], KDC[:, hs(h)],
                                       VN[:, 0, hs(h)], start=True, stop=True)
                    mm.then_inc(*cpe.mark("filled", "state", l))
                    per_head("o0", lambda h: AQ[:, system(0, h), 1, :], lambda h: VN[:, 0, hs(h)])
                    pe.wait_ge(*after("read", "state", l))

                    def half(h):
                        return slice(64 * (h % 2), 64 * (h % 2) + HD)

                    for par in range(2):
                        ps = open_bank("ks", l, par)
                        for p in range(3):
                            for a in range(2):
                                at = (3 * a + p) * HD
                                mm = pe.matmul(ps[:, at:at + HD], KQ[half(par), p, 1, a, :], SST[half(par), p, :],
                                               start=True, stop=True)
                        mm.then_inc(*cpe.mark("filled", "ks", l, par))
                    pe.wait_ge(*after("bv1", l))
                    per_head("vn1", lambda h: DIT[:, system(1, h), :], lambda h: BV[:, 1, hs(h)])
                    pe.wait_ge(*after("read", "vn1", l))
                    per_head("o1", lambda h: AQ[:, system(1, h), 1, :], lambda h: VN[:, 1, hs(h)])
                    pe.wait_ge(*after("dn_out", l))
                    for b in range(2):
                        ps = open_bank("dnoT", l, b)
                        for c in range(2 * b, min(2 * b + 2, 3)):
                            for t in range(TT):
                                mm = pe.transpose(ps[:, (c % 2) * S + t * P:(c % 2) * S + (t + 1) * P],
                                                  O[:, t, c * P:(c + 1) * P], ident)
                        mm.then_inc(*cpe.mark("filled", "dnoT", l, b))
                    pe.wait_ge(*after("read", "dnoT", l, 1))
                    pe.wait_ge(*after("read", "fx_o", l, 2))
                    pe.wait_ge(*after("read", "poolw", l))
                    for i in range(2):
                        tokens_out("wout2", CAT, 512, i, (l,))

                    turn_norm(6 + 2 * l)
                    pe.wait_ge(*after("ht", 6 + 2 * l))

                    if l == 0:
                        pe.wait_ge(*after("scores_read", AH + XH + NH - 1))
                        pe.wait_ge(*after("pt_copied", AH + XH + NH - 1))
                        dn = 0
                        for i in range(GU2 + 1):
                            if i < GU2:
                                features_out("gate", HT, "gate", i)
                                features_out("gate", HT, "up2", i)
                            if i >= 2 and i % 2 == 0 or i == GU2:
                                n = min(4, FF2 // P - 4 * dn)
                                pe.wait_ge(*after("hidden", "ffn", min(2 * dn + 1, GU2 - 1)))
                                down("dn", dn % 2, n, dn == 0, dn == DN2 - 1, "down", "ffn", dn)
                                dn += 1
                        continue

                    ps = open_bank("router")
                    for t in range(TT):
                        for k in range(KD_):
                            mm = pe.matmul(ps[:, t * NE:(t + 1) * NE], T2[:, k, t * P:(t + 1) * P], RT[:, k, :],
                                           start=(k == 0), stop=(k == KD_ - 1))
                    mm.then_inc(*cpe.mark("filled", "router"))
                    pe.wait_ge(*after("hot"))
                    hot = SM[:, 4, :].rearrange("p (t e) -> p t e", t=TT)
                    ps = open_bank("ranks")
                    pe.matmul(ps[:, 0:NE], upper, hot[:, 0, :], start=True, stop=True)
                    pe.matmul(ps[:, NE:2 * NE], upper, hot[:, 1, :], start=True, stop=False)
                    pe.matmul(ps[:, NE:2 * NE], ones, hot[:, 0, :], start=False, stop=True)
                    pe.matmul(ps[:, 2 * NE:3 * NE], ones, hot[:, 0, :], start=True, stop=False)
                    pe.matmul(ps[:, 2 * NE:3 * NE], ones, hot[:, 1, :], start=False, stop=True)\
                      .then_inc(*cpe.mark("filled", "ranks"))
                    pe.wait_ge(*after("scores_read", AH + XH + 2 * NH - 1))
                    pe.wait_ge(*after("pt_copied", AH + XH + 2 * NH - 1))
                    for b in range(4):
                        pe.matmul(banks[b][:, :], ident, X[:, b // 2, (b % 2) * 512:(b % 2 + 1) * 512],
                                  start=True, stop=True)

                    def gather(part, ps, *name):
                        for k in range(4):
                            f = 4 * part + k
                            for t in range(TT):
                                mm = pe.matmul(ps[:, k * P:(k + 1) * P], XN[:, t, f * P:(f + 1) * P], GSEL[:, t, :],
                                               start=(t == 0), stop=(t == TT - 1))
                        mm.then_inc(*cpe.mark(*name))

                    pe.wait_ge(*after("select0"))
                    for part in range(2):
                        gather(part, open_bank("gather", part), "filled", "gather", part)
                    for b in range(1, 5):
                        pe.wait_ge(*after("read", *order[-b]))
                    pe.wait_ge(*after("lo", EXPERT0 + SPLIT - 1))
                    pe.wait_ge(*after("first_gathered"))
                    items = pe.value_load(ITEM[0:1, 15:16], min_val=NE, max_val=NE + MORE)
                    base = cpe.n
                    with pe.Fori(0, items) as i:
                        def item_open(name):
                            prev, before = item_reader_before(name)
                            key = points.get(("item_read", prev), ("dve", 1))[0]
                            pe.wait_ge(*in_loop(i, key, "item_read", prev, before=before))
                            return item_bank(name)

                        def item_weights(s, b):
                            if s < SPLIT:
                                pe.wait_ge(*in_loop(i, "dve", "lo_item", s + NX, b, before=True))
                            else:
                                pe.wait_ge(*in_loop(i, "dve", "lo_item", s, b))
                            return split_view(EXPERT0 + s, *((4, 512) if s < 12 else (2, 1024)))

                        def wide(name, s):
                            for r in range(2):
                                if r == 0:
                                    ps = item_open(name)
                                for k in range(4):
                                    if k % 2 == 0:
                                        w = item_weights(s + r, k // 2)
                                    mm = matmul3(ps[:, :], lambda z: HG[:, z, 4 * r + k, :], lambda z: w[:, z, k, :],
                                                 r == 0 and k == 0, r == 1 and k == 3)
                                    if k % 2:
                                        mm.then_inc(*cpe.mark("expert_slot", s + r, k // 2))
                            cpe.also("item", name)

                        def turn(n):
                            pe.wait_ge(*in_loop(i, "dve", "hh", n))
                            ps = item_open(f"hT{n}")
                            for k in range(4):
                                mm = pe.transpose(ps[:, k * P:(k + 1) * P], HH[:, n, k * P:(k + 1) * P], ident)
                            mm.then_inc(*cpe.mark("item", f"hT{n}"))

                        def down_slot(n):
                            if n == 0:
                                item_open("down0")
                                item_open("down1")
                            pe.wait_ge(*in_loop(i, "dve", "item_read", f"hT{n}"))
                            for r in range(2):
                                for k in range(2):
                                    w = item_weights(12 + 2 * n + r, k)
                                    for c in range(2):
                                        mm = matmul3(item_bank(f"down{c}")[:, :],
                                                     lambda z: HHT[:, z, 4 * n + 2 * r + k, :],
                                                     lambda z: w[:, z, k, c * 512:(c + 1) * 512],
                                                     n == 0 and r == 0 and k == 0, n == 2 and r == 1 and k == 1)
                                    mm.then_inc(*cpe.mark("expert_slot", 12 + 2 * n + r, k))

                        pe.wait_ge(*in_loop(i, "dve", "gathered", before=True))
                        wide("gate0", 0)
                        wide("up0", 2)
                        pe.wait_ge(*in_loop(i, "dve", "gate_rows"))
                        ps = item_open("scatterT")
                        for t in range(TT):
                            mm = pe.transpose(ps[:, t * P:(t + 1) * P], GGATE[:, t, :], ident)
                        mm.then_inc(*cpe.mark("item", "scatterT"))
                        wide("gate1", 4)
                        wide("up1", 6)
                        turn(0)
                        wide("gate2", 8)
                        wide("up2", 10)
                        turn(1)
                        down_slot(0)
                        turn(2)
                        down_slot(1)
                        pe.wait_ge(*in_loop(i, "dve", "select"))
                        for part in range(2):
                            gather(part, item_open(f"gather{part}"), "item", f"gather{part}")
                        down_slot(2)
                        cpe.also("item", "down0")
                        cpe.also("item", "down1")
                        pe.wait_ge(*in_loop(i, "act", "item_read", "scatterT"))
                        for c in range(2):
                            pe.wait_ge(*in_loop(i, "act", "item_read", f"down{c}"))
                            for t in range(TT):
                                mm = pe.matmul(banks[2 * t + c][:, :], GST[:, t, :], Y[:, c, :], start=False,
                                               stop=True, skip_group_check=True)
                        mm.then_inc(*cpe.mark("item", "scatter"))
                    points[("per", "pe")] = ("pe", cpe.n - base)

            @block.sync
            def _(sp):
                xv = A["x"][0].rearrange("(t p) n -> p t n", p=P)
                for t in range(TT):
                    sp.dma_start(X[:, t, :], xv[:, t, :]).then_inc(x_in, 16)
                sp.dma_start(T_[:, 0:P], A["table"][:, 0:P]).then_inc(ident_in, 16)

                def load(j):
                    if j >= RING:
                        sp.wait_ge(*after("lo", j - RING))
                    sp.dma_start(raw(j, *shape_of(j)), slots[j][1]).then_inc(w_in[j % RING], 16)

                for j in range(RING):
                    load(j)
                for t in range(TT):
                    sp.dma_start(MEM[:, t, :], A["mem"][0].rearrange("(t p) n -> p t n", p=P)[:, t, :])\
                      .then_inc(mem_in, 16)
                sp.dma_start(T_[:, P:], A["table"][:, P:]).then_inc(table_in, 16)
                for name in WIDE:
                    at, n = WIDE[name]
                    src = A[name].rearrange("a b -> (a b)") if len(A[name].shape) == 2 else A[name]
                    sp.dma_start(WD[:, at:at + n], src.partition_broadcast(P)).then_inc(wide_in, 16)
                sp.dma_start(RT[:, :, :], A["router_2"][0].rearrange("(k p) n -> p k n", p=P)).then_inc(wide_in, 16)
                sp.wait_ge(*after("poolw_zero"))
                for l in range(LAYERS):
                    for g in range(4):
                        o = 64 * (g % 2)
                        sp.dma_start(PW[o:o + 64, l, g // 2, o:o + 64], A["pool_w_2"][l, g]).then_inc(poolw_in, 16)
                for j in range(RING, len(slots) if stop == 0 else N1):
                    load(j)
                if stop == 1:
                    sp.wait_ge(*after("x_final"))
                else:
                    def load_item(i, lo, hi, e):
                        for s in range(lo, hi):
                            if s - RING >= SPLIT:
                                sp.wait_ge(*in_loop(i, "dve", "lo_item", s - RING, 1))
                            else:
                                sp.wait_ge(*in_loop(i, "dve", "lo_item", s - RING + NX, 1, before=True))
                            j = EXPERT0 + s
                            sp.dma_start(raw(j, *((4, 512) if s % NX < 12 else (2, 1024))), expert_src(s % NX, e))\
                              .then_inc(w_in[j % RING], 16)

                    sp.wait_ge(*after("lo", EXPERT0 + SPLIT - 1))
                    with sp.Fori(0, NE - 1) as i:
                        load_item(i, SPLIT, NX, i)
                        load_item(i, NX, NX + SPLIT, i + 1)
                    sp.wait_ge(*after("items"))
                    items = sp.value_load(ITEM[0:1, 15:16], min_val=NE, max_val=NE + MORE)
                    with sp.Fori(NE - 1, items) as i:
                        load_item(i, SPLIT, NX, sp.value_load(ITEM[0:1, bass.ds(i, 1)], min_val=0, max_val=NE - 1))
                        load_item(i, NX, NX + SPLIT,
                                  sp.value_load(ITEM[0:1, bass.ds(i + 1, 1)], min_val=0, max_val=NE - 1))
                    sp.wait_ge(moe_out, 4)
                sp.dma_start(out[0].rearrange("(t p) n -> p t n", p=P), X[:, :, :]).then_inc(out_written, 16)
                sp.wait_ge(out_written, 16)

            @block.scalar
            def _(act):
                for i, tile in enumerate(ROWS):
                    at = 0
                    for name, n in tile:
                        src = A[name]
                        if len(src.shape) == 3:
                            src = src.rearrange("a b (r p) -> (a b r) p", p=P)
                        else:
                            src = src.rearrange("a (r p) -> (a r) p", p=P)
                        act.dma_start(GR[at:at + n, i, :], src).then_inc(rows_in, 16)
                        at += n

                def do(ins, *name):
                    ins.then_inc(*cact.mark(*name))

                def own():
                    act.wait_ge(*cact.last())

                nsplit = [0]
                HALF = SLOT // 2

                def high(n):
                    for _ in range(n):
                        j = nsplit[0]
                        nsplit[0] += 1
                        k, m = shape_of(j)
                        act.wait_ge(w_in[j % RING], loads[j])
                        if j >= SPLIT:
                            act.wait_ge(*after("slot", j - SPLIT))
                        for b in range(2):
                            part = slice(b * k * m // 2, (b + 1) * k * m // 2)
                            do(act.activation(WS[:, j % SPLIT, 0, part], W[:, j % RING, part], ACT.Copy), "hi", j, b)

                def sumsq(i, src):
                    for t in range(TT):
                        do(act.activation(XN[:, t, :], src[:, t, :], ACT.Square, accum_out=SS[:, t:t + 1]),
                           "ss", i, t)

                def features_high(i, dst, tmp):
                    for t in range(TT):
                        act.wait_ge(*after("scaled", i, t))
                        part = slice(t * P, (t + 1) * P)
                        do(act.activation(dst[:, 0, :, part], tmp[:, :, part], ACT.Copy), "features_high", i, t)

                def copy_out(dst, src, *name):
                    act.wait_ge(*after("filled", *name))
                    do(act.activation(dst, src, ACT.Copy), "read", *name)

                def exps(u):
                    act.wait_ge(*after("negmax", u))
                    for t in range(TT):
                        do(act.activation(PR[:, u % 3, t, :], PR[:, u % 3, t, :], ACT.Exp,
                                          bias=NM[:, u % 3, t:t + 1], accum_out=DEN[:, u % 3, t:t + 1]),
                           "exp", u, t)

                def attention(u0, heads, between=lambda s: None):
                    for s in range(heads + 1):
                        if s < heads:
                            exps(u0 + s)
                        if s >= 1:
                            u = u0 + s - 1
                            act.wait_ge(*after("pt", u))
                            if u >= 2:
                                act.wait_ge(*after("o", u - 2))
                            do(act.activation(PT[:, u % 2], PT_BANK[u % 2][:, :].rearrange("p (a b) -> p a b", a=2),
                                              ACT.Copy), "pt_copied", u)
                        between(s)

                def psum(*name):
                    return bank_of[name]

                def two(ps):
                    return ps[:, :].rearrange("p (a b) -> p a b", a=2)

                act.wait_ge(x_in, 32)
                sumsq(0, X)
                high(2)
                features_high(0, HT, T1)
                for b in range(2):
                    high(1)
                    act.wait_ge(*after("filled", "g", b))
                    do(act.activation(SIG[:, 2 * b:2 * b + 2, :], two(psum("g", b)), ACT.Sigmoid), "read", "g", b)
                high(4)
                act.wait_ge(mem_in, 32)
                act.wait_ge(*after("filled", "normT", 0, 1, 1))
                sumsq(1, MEM)
                for t in range(TT):
                    copy_out(QK[:, t, 0:512], psum("q", 0, t)[:, :], "q", 0, t)
                high(2)
                for t in range(TT):
                    copy_out(QK[:, t, 512:1024], psum("k", 0, t)[:, :], "k", 0, t)
                features_high(1, MT, T1)
                high(2)
                for t in range(TT):
                    copy_out(V[:, t, :], psum("v", 0, t)[:, :], "v", 0, t)
                for i in range(4):
                    high(1)
                    copy_out(XKT[:, 2 * i:2 * i + 2, :], two(psum("xk", i)), "xk", i)
                for i in range(2):
                    high(2)
                    for t in range(TT):
                        copy_out(XV[:, t, i * 512:(i + 1) * 512], psum("xv", i, t)[:, :], "xv", i, t)
                for b in range(4):
                    copy_out(QKT[:, 2 * b:2 * b + 2, :], two(psum("qkT", b)), "qkT", b)
                attention(0, AH)
                act.wait_ge(*after("read", "cmean"))
                do(act.activation(SIG[:, :, :], C[:, :, :], ACT.Square), "csq")
                act.wait_ge(*after("read", "cvar"))
                do(act.activation(U[:, 0, 0:S], U[:, 0, 0:S], ACT.Sqrt), "csd")
                act.wait_ge(*after("cnormed"))
                for i in range(4):
                    do(act.activation(C[:, i, :], C[:, i, :], ACT.Silu, bias=col("conv_ln_b", i),
                                      scale=col("conv_ln_g", i)), "csilu")
                high(4)
                act.wait_ge(*after("read", "wout", 1, 1))
                sumsq(2, X)
                features_high(2, HT, T1)
                for i in range(4):
                    high(1)
                    copy_out(XQT[:, 2 * i:2 * i + 2, :], two(psum("xq", i)), "xq", i)
                attention(AH, XH)
                high(4)
                act.wait_ge(*after("read", "xo", 1, 1))
                sumsq(3, X)
                features_high(3, HT, T1)
                for i in range(MLP_SLOTS):
                    for b in range(2):
                        n = 2 * i + b
                        high(1)
                        act.wait_ge(*after("filled", "up", i, b))
                        if n >= 2:
                            act.wait_ge(*after("squared", n - 2))
                        do(act.activation(SG[:, n % 2, :], psum("up", i, b)[:, :], ACT.Relu), "read", "up", i, b)
                    if i >= 1:
                        high(2)
                high(2)
                act.wait_ge(*after("x", "mlp"))
                sumsq(4, X)
                if stop == 1:
                    return
                for l in range(LAYERS):
                    i0 = 5 + 2 * l
                    act.wait_ge(*after("x_final1") if l == 0 else after("x", "ffn"))
                    sumsq(i0, X)
                    features_high(i0, HT, T2)
                    for i in range(5):
                        high(1)
                        if i < 4:
                            copy_out(CI[:, 2 * i:2 * i + 2, 3:3 + S], two(psum("cqkv", l, i)), "cqkv", l, i)
                        else:
                            copy_out(CI[:, 8, 3:3 + S], psum("cqkv", l, i)[:, 0:S], "cqkv", l, i)
                    high(1)
                    copy_out(XP[:, :, 16:], two(psum("pool", l)), "pool", l)
                    for name, dst, n in (("zab", ZAB, HW + 12), ("fq", FQ[:, :, 0:HW], HW), ("fk", FQ[:, :, HW:], HW),
                                         ("fv", FV, HW + 6)):
                        high(2)
                        for t in range(TT):
                            copy_out(dst[:, t, :], psum(name, l, 0, t)[:, 0:n], name, l, 0, t)
                    for i in range(9):
                        act.wait_ge(*after("taps", l, i))
                        do(act.activation(CO[:, i, :], CO[:, i, :], ACT.Silu), "conv2", l, i)
                    own()
                    do(act.activation(ZAB[:, :, 0:HW], ZAB[:, :, 0:HW], ACT.Silu), "silu_z", l)
                    do(act.activation(SM[:, 2, 0:12].rearrange("p (t h) -> p t h", t=2), ZAB[:, :, HW + 6:],
                                      ACT.Sigmoid), "beta", l)
                    act.wait_ge(*after("absneg", l))
                    do(act.activation(SM[:, 5:7, 0:12], SM[:, 5:7, 0:12], ACT.Exp))
                    do(act.activation(SM[:, 7, 0:6], wide("dn_a_log_2", l, NH), ACT.Exp))
                    own()
                    do(act.activation(SM[:, 5:7, 0:12], SM[:, 5:7, 0:12], ACT.Ln, bias=1.0), "softlog", l)
                    act.wait_ge(*after("filled", "normT", i0, 1, 1))
                    do(act.activation(SQ[:, :, :], FQ[:, :, :], ACT.Square), "fx_sq", l)
                    for b in range(5):
                        n = 256 if b < 4 else P
                        copy_out(QT3[:, :, b * 256:b * 256 + n], two(psum("dnT", l, b))[:, :, 0:n], "dnT", l, b)
                    own()
                    act.wait_ge(*after("fx_ssum", l))
                    do(act.activation(SQ[:, :, :], QT3[:, :, 0:2 * HW], ACT.Square), "dn_sq", l)
                    act.wait_ge(*after("read", "cum", l))
                    do(act.activation(SM[:, 9, 0:12], SM[:, 8, 0:12], ACT.Exp))
                    do(act.activation(SM[:, 10, 0:6], SM[:, 11, 0:6], ACT.Exp), "expg", l)
                    for b in range(3):
                        copy_out(FT[:, 2 * b:2 * b + 2, :], two(psum("fT", l, b)), "fT", l, b)
                    for p in range(3):
                        copy_out(KQ[:, p].rearrange("p a b c -> p (a b c)"), psum("kqT", l, p)[:, :], "kqT", l, p)
                    for p in range(3):
                        copy_out(KT[:, p].rearrange("p a b -> p (a b)"), psum("kT", l, p)[:, 0:S], "kT", l, p)
                    act.wait_ge(*after("read", "grow", l, 3))
                    do(act.activation(DD[:, :, :], DD[:, :, :], ACT.Exp), "decay", l)

                    def inverse_level(lev):
                        for gi in range(3 if lev >= 1 else 0):
                            copy_out(PM[:, 4 * gi:4 * gi + 4, :],
                                     psum("invp", l, lev, gi)[:, :].rearrange("p (a b) -> p a b", a=4),
                                     "invp", l, lev, gi)

                    attention(AH + XH + NH * l, NH, inverse_level)
                    copy_out(VN[:, 0, :], psum("vn0", l)[:, 0:HW], "vn0", l)
                    copy_out(SST[:, :, :], psum("state", l)[:, 0:3 * HD].rearrange("p (a b) -> p a b", a=3), "state", l)
                    copy_out(O[:, 0, :], psum("o0", l)[:, 0:HW], "o0", l)
                    copy_out(VN[:, 1, :], psum("vn1", l)[:, 0:HW], "vn1", l)
                    act.wait_ge(*after("read", "o1", l))
                    do(act.activation(SQ[:, :, 0:HW], O[:, :, :], ACT.Square), "o_sq", l)
                    high(4)
                    act.wait_ge(*after("read", "wout2", l, 1, 1))
                    sumsq(i0 + 1, X)
                    if l == 0:
                        features_high(i0 + 1, HT, T2)
                        for i in range(GU2):
                            high(1)
                            act.wait_ge(*after("filled", "gate", i))
                            if i >= 2:
                                act.wait_ge(*after("hidden", "ffn", i - 2))
                            do(act.activation(SG[:, i % 2, :], psum("gate", i)[:, :], ACT.Silu), "read", "gate", i)
                            high(1)
                            if i >= 2 and i % 2 == 0:
                                high(2)
                        high(1)
                        continue
                    act.wait_ge(*after("logit_shift"))
                    do(act.activation(SM[:, 3, :], SM[:, 2, :], ACT.Exp), "gate_exp")
                    act.wait_ge(*after("items"))
                    items = act.value_load(ITEM[0:1, 15:16], min_val=NE, max_val=NE + MORE)
                    base = cact.n
                    with act.Fori(0, items) as i:
                        def silu(n):
                            act.wait_ge(*in_loop(i, "pe", "item", f"gate{n}"))
                            act.wait_ge(*in_loop(i, "dve", "hh", n, before=True))
                            do(act.activation(SGE[:, n, :], item_bank(f"gate{n}")[:, :], ACT.Silu),
                               "item_read", f"gate{n}")

                        def copy(dst, name, free, key="pe", before=True):
                            act.wait_ge(*in_loop(i, "pe", "item", name))
                            act.wait_ge(*in_loop(i, "pe", *free, before=True))
                            do(act.activation(dst, item_bank(name)[:, 0:dst.shape[1]], ACT.Copy), "item_read", name)

                        def high_item(*ss):
                            for s in ss:
                                j = EXPERT0 + s
                                act.wait_ge(w_in[j % RING], i * PER_RING + expert_loads[s])
                                for b in range(2):
                                    act.wait_ge(*in_loop(i, "pe", "expert_slot", s - SPLIT, b))
                                    part = slice(b * HALF, (b + 1) * HALF)
                                    do(act.activation(WS[:, j % SPLIT, 0, part], W[:, j % RING, part], ACT.Copy),
                                       "hi_item", s, b)

                        def hidden_high(n):
                            act.wait_ge(*in_loop(i, "pe", "item", f"hT{n}"))
                            act.wait_ge(*in_loop(i, "pe", "expert_slot", NX - 1, 1, before=True))
                            do(act.activation(HHT[:, 0, 4 * n:4 * n + 4, :],
                                              item_bank(f"hT{n}")[:, :].rearrange("p (k n) -> p k n", k=4), ACT.Copy),
                               "hhi", n)

                        high_item(2, 3)
                        silu(0)
                        high_item(4, 5)
                        copy(GST.rearrange("p a b -> p (a b)"), "scatterT", ("item", "scatter"))
                        high_item(6, 7)
                        silu(1)
                        high_item(8, 9)
                        hidden_high(0)
                        high_item(10, 11)
                        silu(2)
                        high_item(12, 13)
                        hidden_high(1)
                        high_item(14, 15)
                        hidden_high(2)
                        high_item(16, 17)
                        act.wait_ge(*in_loop(i, "dve", "item_read", "gather1"))
                        do(act.activation(HG[:, 0], HGT[:, :, :], ACT.Copy), "ghi")
                        high_item(18, 19)
                        for c in range(2):
                            copy(Y[:, c, :], f"down{c}", ("item", "scatter"))
                    points[("per", "act")] = ("act", cact.n - base)

            @block.gpsimd
            def _(pool):
                def do(ins, *name):
                    ins.then_inc(*cpool.mark(*name))

                do(pool.memset(NHALF[:, :], -0.5), "nhalf")
                do(pool.memset(U[:, :, 0:PAD], 0.0))
                do(pool.memset(U[:, :, PAD + S:], 0.0), "u_padded")
                do(pool.memset(PW[:, :, :, :], 0.0), "poolw_zero")
                pool.wait_ge(*cpool.last())

                def power(n, need, *name, at=0):
                    pool.wait_ge(*after(*need))
                    do(pool.tensor_tensor(RS[:, at:at + n], MS[:, at:at + n], NHALF[:, 0:n], ALU.pow), *name)

                for i in range(5):
                    power(2, ("ms", i), "rstd", i)
                if stop == 1:
                    return
                for l in range(LAYERS):
                    power(2, ("ms", 5 + 2 * l), "rstd", 5 + 2 * l)
                    pool.wait_ge(*after("read", "pool", l))
                    do(pool.memset(XP[:, :, 0:16], 0.0))
                    do(pool.memset(SA[:, :, 0:16], 0.0))
                    do(pool.memset(SBf[:, :, 0:16], 0.0))
                    do(pool.memset(SC[:, :, 0:16], 0.0))
                    last = XP
                    for n, nxt in ((1, SA), (2, SBf), (4, SC)):
                        pool.wait_ge(*cpool.last())
                        do(pool.tensor_tensor(nxt[:, :, 16:], last[:, :, 16:], last[:, :, 16 - n:16 + S - n], ALU.add))
                        last = nxt
                    pool.wait_ge(*cpool.last())
                    for i, (half_, src) in enumerate(((slice(0, 64), SA), (slice(64, 128), SBf))):
                        do(pool.tensor_tensor(YP[half_, 0, :], src[half_, 0, 16:], poolinv[half_, 0, :], ALU.mult))
                    do(pool.tensor_tensor(YP[0:64, 1, :], SC[0:64, 1, 16:], poolinv[0:64, 1, :], ALU.mult))
                    pool.wait_ge(*cpool.last())
                    do(pool.tensor_tensor(SA[64:128, 1, 16:], SC[64:128, 1, 16:], SC[64:128, 1, 8:8 + S], ALU.add))
                    pool.wait_ge(*cpool.last())
                    do(pool.tensor_tensor(YP[64:128, 1, :], SA[64:128, 1, 16:], poolinv[64:128, 1, :], ALU.mult))
                    pool.wait_ge(*cpool.last())
                    do(pool.tensor_tensor(YP[:, :, :], YP[:, :, :], XP[:, :, 16:], ALU.subtract), "pooled", l)
                    power(24, ("fx_ms", l), "fx_rstd", l)
                    power(24, ("dn_ms", l), "dn_rstd", l, at=24)
                    power(12, ("o_ms", l), "o_rstd", l)
                    power(2, ("ms", 6 + 2 * l), "rstd", 6 + 2 * l)

            @block.vector
            def _(dve):
                def do(ins, *name):
                    ins.then_inc(*cdve.mark(*name))

                def own(back=0):
                    dve.wait_ge(*cdve.last(back))

                def psum(*name):
                    return bank_of[name]

                nsplit = [0]
                HALF = SLOT // 2

                def low(n):
                    for _ in range(n):
                        j = nsplit[0]
                        nsplit[0] += 1
                        k, m = shape_of(j)
                        for b in range(2):
                            part = slice(b * k * m // 2, (b + 1) * k * m // 2)
                            dve.wait_ge(*after("hi", j, b))
                            do(dve.tensor_tensor(WS[:, j % SPLIT, 1, part], W[:, j % RING, part],
                                                 WS[:, j % SPLIT, 0, part].bitcast(F32), ALU.subtract), "lo", j)

                def split(dst, src, *name):
                    do(dve.tensor_copy(dst(0), src))
                    own()
                    do(dve.tensor_tensor(dst(1), src, dst(0).bitcast(F32), ALU.subtract), *name)

                def norm(i, src, gain, gi, dst, tmp):
                    rows_norm(i, src)
                    turned(i, gain, gi, dst, tmp)

                def turned(i, gain, gi, dst, tmp):
                    for t in range(TT):
                        for b in range(2):
                            dve.wait_ge(*after("filled", "normT", i, t, b))
                            do(dve.tensor_tensor(tmp[:, 4 * b:4 * b + 4, t * P:(t + 1) * P],
                                                 psum("normT", i, t, b)[:, :].rearrange("p (k n) -> p k n", k=4),
                                                 cols(gain, gi + 4 * b, 4).unsqueeze(2).broadcast_to([P, 4, P]),
                                                 ALU.mult), "read", "normT", i, t, b)
                        cdve.also("scaled", i, t)
                    if dst is not None:
                        for t in range(TT):
                            part = slice(t * P, (t + 1) * P)
                            dve.wait_ge(*after("features_high", i, t))
                            do(dve.tensor_tensor(dst[:, 1, :, part], tmp[:, :, part],
                                                 dst[:, 0, :, part].bitcast(F32), ALU.subtract))
                    cdve.also("ht", i)

                def rows_norm(i, src, final=False):
                    dve.wait_ge(*after("ss", i, 1))
                    do(dve.tensor_scalar(MS[:, 0:TT], SS[:, 0:TT], 1.0 / D, EPS, ALU.mult, ALU.add), "ms", i)
                    dve.wait_ge(*after("rstd", i))
                    for t in range(TT):
                        if final:
                            do(dve.scalar_tensor_tensor(src[:, t, :], src[:, t, :], RS[:, t:t + 1],
                                                        wide("norm_final_g", 0, D), ALU.mult, ALU.mult), "xn", i, t)
                        else:
                            do(dve.tensor_scalar(XN[:, t, :], src[:, t, :], RS[:, t:t + 1], None, ALU.mult),
                               "xn", i, t)

                def add_residual(*name):
                    for i in range(2):
                        for t in range(TT):
                            dve.wait_ge(*after("filled", *name, i, t))
                            part = X[:, t, i * 512:(i + 1) * 512]
                            do(dve.tensor_tensor(part, psum(*name, i, t)[:, :], part, ALU.add), "read", *name, i, t)

                def add_banks(*name):
                    for b in range(4):
                        part = X[:, b // 2, (b % 2) * 512:(b % 2 + 1) * 512]
                        do(dve.tensor_tensor(part, banks[b][:, :], part, ALU.add))
                    cdve.also(*name)

                def attention(u0, heads, scale, mask, outs, lag=4, between=lambda s: None):
                    for s in range(heads + lag):
                        if 1 <= s <= heads:
                            u = u0 + s - 1
                            dve.wait_ge(*after("exp", u, 1))
                            do(dve.reciprocal(RDEN[:, u % 3, :], DEN[:, u % 3, :]))
                            own()
                            for t in range(TT):
                                do(dve.tensor_scalar(PR[:, u % 3, t, :], PR[:, u % 3, t, :],
                                                     RDEN[:, u % 3, t:t + 1], None, ALU.mult), "probs", u)
                        if s < heads:
                            u = u0 + s
                            dve.wait_ge(*after("scores", u))
                            if u >= 3:
                                dve.wait_ge(*after("pt", u - 3))
                            ps = SC_BANK[u % 2][:, :]
                            pr = PR[:, u % 3].rearrange("p a b -> p (a b)")
                            if mask is None:
                                do(dve.tensor_scalar(pr, ps, scale, None, ALU.mult), "scores_read", u)
                            else:
                                do(dve.scalar_tensor_tensor(pr, ps, scale, mask.rearrange("p a b -> p (a b)"),
                                                            ALU.mult, ALU.add), "scores_read", u)
                            own()
                            do(dve.tensor_reduce(NM[:, u % 3, :], PR[:, u % 3], AX.X, ALU.max, negate=True),
                               "negmax", u)
                        if s >= lag:
                            outs(s - lag)
                        between(s)

                dve.wait_ge(*after("nhalf"))
                rows_norm(0, X)
                low(2)
                dve.wait_ge(*after("filled", "cols"))
                do(dve.tensor_copy(COL[:, :], psum("cols")[:, 0:NCOLS]), "read", "cols")
                own()
                turned(0, "norm_mix_g", 0, HT, T1)
                low(2)
                dve.wait_ge(*after("u_padded"))
                for b in range(2):
                    low(1)
                    dve.wait_ge(*after("filled", "a", b))
                    dve.wait_ge(*after("read", "g", b))
                    do(dve.tensor_tensor(U[:, 2 * b:2 * b + 2, PAD:PAD + S],
                                         psum("a", b)[:, :].rearrange("p (a b) -> p a b", a=2),
                                         SIG[:, 2 * b:2 * b + 2, :], ALU.mult), "read", "a", b)
                own()
                tap = [0]

                def conv_taps(n):
                    for k in range(tap[0], min(tap[0] + n, TAPS)):
                        for i in range(4):
                            w = col("conv_w", 4 * k + i)
                            if k == 0:
                                do(dve.tensor_scalar(C[:, i, :], U[:, i, 0:S], w, col("conv_b", i), ALU.mult, ALU.add))
                            else:
                                own(3)
                                do(dve.scalar_tensor_tensor(C[:, i, :], U[:, i, k:k + S], w, C[:, i, :],
                                                            ALU.mult, ALU.add))
                    tap[0] += n

                for i in range(4):
                    if i == 2:
                        rows_norm(1, MEM)
                    conv_taps(1)
                    low(1)
                turned(1, "norm_mem_g", 0, MT, T1)
                for _ in range(2):
                    low(1)
                    conv_taps(1)
                for n in (0, 1):
                    dve.wait_ge(*after("read", "q" if n == 0 else "k", 0, 1))
                dve.wait_ge(table_in, 16)
                heads = QK.rearrange("p t (h c) -> p t h c", c=HD)
                x1, x2 = heads[:, :, :, 0:8], heads[:, :, :, 8:16]
                cb = cos.unsqueeze(2).broadcast_to([P, TT, 16, 8])
                sbr = sin.unsqueeze(2).broadcast_to([P, TT, 16, 8])
                r = [RT1[:, i, :].rearrange("p (t h c) -> p t h c", t=TT, h=16) for i in range(4)]
                do(dve.tensor_tensor(r[0], x1, cb, ALU.mult))
                do(dve.tensor_tensor(r[1], x2, sbr, ALU.mult))
                do(dve.tensor_tensor(r[2], x2, cb, ALU.mult))
                do(dve.tensor_tensor(r[3], x1, sbr, ALU.mult))
                own()
                do(dve.tensor_tensor(x1, r[0], r[1], ALU.subtract))
                do(dve.tensor_tensor(x2, r[2], r[3], ALU.add), "rotated")
                for _ in range(8):
                    low(1)
                    conv_taps(2)

                def outs1(h):
                    if h % 2:
                        dve.wait_ge(*after("filled", "att_o", h // 2))
                        split(lambda z: CAT[:, z, h // 2, :], psum("att_o", h // 2)[:, 0:S], "read", "att_o", h // 2)

                attention(0, AH, 0.125, logc, outs1, between=lambda s: conv_taps(1))
                assert tap[0] >= TAPS
                cdve.also("conv")
                dve.wait_ge(*after("filled", "cmean"))
                do(dve.scalar_tensor_tensor(C[:, :, :], psum("cmean")[:, 0:S].unsqueeze(1).broadcast_to([P, 4, S]),
                                            -1.0 / ATT, C[:, :, :], ALU.mult, ALU.add), "read", "cmean")
                dve.wait_ge(*after("filled", "cvar"))
                do(dve.tensor_scalar(U[:, 0, 0:S], psum("cvar")[:, 0:S], 1.0 / ATT, EPS, ALU.mult, ALU.add),
                   "read", "cvar")
                dve.wait_ge(*after("csd"))
                do(dve.reciprocal(U[:, 1, 0:S], U[:, 0, 0:S]))
                own()
                do(dve.tensor_tensor(C[:, :, :], C[:, :, :],
                                     U[:, 1, 0:S].unsqueeze(1).broadcast_to([P, 4, S]), ALU.mult), "cnormed")
                dve.wait_ge(*after("csilu"))
                split(lambda z: CAT[:, z, 4:8, :], C[:, :, :], "convT")
                low(4)
                add_residual("wout")
                norm(2, X, "norm_x_g", 0, HT, T1)
                low(4)

                def outsx(h):
                    dve.wait_ge(*after("filled", "xatt_o", h))
                    split(lambda z: CAT[:, z, 2 * h:2 * h + 2, :],
                          psum("xatt_o", h)[:, :].rearrange("p (a b) -> p a b", a=2), "read", "xatt_o", h)

                attention(AH, XH, 0.0625, None, outsx)
                low(4)
                add_residual("xo")
                norm(3, X, "norm_mlp_g", 0, HT, T1)
                for i in range(MLP_SLOTS):
                    for b in range(2):
                        n = 2 * i + b
                        low(1)
                        dve.wait_ge(*after("read", "up", i, b))
                        if i >= 2:
                            dve.wait_ge(*after("down", "mlp", i - 2))
                        do(dve.tensor_tensor(PRD[:, n % 2, :], SG[:, n % 2, :], SG[:, n % 2, :], ALU.mult),
                           "squared", n)
                        own()
                        split(lambda z: UH[:, z, i % 2, 2 * b:2 * b + 2, :],
                              PRD[:, n % 2, :].rearrange("p (a b) -> p a b", a=2), "hidden", "mlp", i, b)
                    if i >= 1:
                        low(2)
                low(2)
                dve.wait_ge(*after("down", "mlp", MLP_SLOTS - 1))
                add_banks("x", "mlp")
                dve.wait_ge(wide_in, 16 * 8)
                rows_norm(4, X, final=True)
                cdve.also("x_final1")
                if stop == 1:
                    cdve.also("x_final")
                    return

                for l in range(LAYERS):
                    i0 = 5 + 2 * l
                    norm(i0, X, "norm1_2", 8 * l, HT, T2)
                    do(dve.memset(CI[:, :, 0:3], 0.0))
                    own()
                    for i in range(9):
                        if i % 2 == 0:
                            low(1)
                        dve.wait_ge(*after("read", "cqkv", l, i // 2))
                        for k in range(DTAPS):
                            w = col("dn_conv_2", 36 * l + 9 * k + i)
                            if k == 0:
                                do(dve.tensor_scalar(CO[:, i, :], CI[:, i, 0:S], w, None, ALU.mult))
                            else:
                                own()
                                do(dve.scalar_tensor_tensor(CO[:, i, :], CI[:, i, k:k + S], w, CO[:, i, :],
                                                            ALU.mult, ALU.add), "taps", l, i)
                    low(9)
                    dve.wait_ge(*after("read", "fv", l, 0, 1))
                    dve.wait_ge(*after("beta", l))

                    def six(v):
                        return v.rearrange("p (t h) -> p t h", t=TT)

                    def bc6(v):
                        return v.unsqueeze(1).broadcast_to([P, TT, NH])

                    do(dve.tensor_tensor(six(SM[:, 3, 0:12]), ZAB[:, :, HW:HW + 6], bc6(wide("dn_dt_bias_2", l, NH)),
                                         ALU.add))
                    do(dve.tensor_tensor(six(SM[:, 4, 0:12]), FV[:, :, HW:HW + 6], bc6(wide("fx_f_bias_2", l, NH)),
                                         ALU.add))
                    own()
                    do(dve.tensor_scalar(SM[:, 4, 0:12], SM[:, 4, 0:12], -1.0, None, ALU.mult))
                    own()
                    do(dve.tensor_scalar(SM[:, 12:14, 0:12], SM[:, 3:5, 0:12], -1.0, None, ALU.mult))
                    own()
                    do(dve.tensor_tensor(SM[:, 5:7, 0:12], SM[:, 3:5, 0:12], SM[:, 12:14, 0:12], ALU.min), "absneg", l)
                    dve.wait_ge(*after("softlog", l))
                    do(dve.scalar_tensor_tensor(SM[:, 0:2, 0:12], SM[:, 3:5, 0:12], 0.0, SM[:, 5:7, 0:12],
                                                ALU.max, ALU.add))
                    own()
                    do(dve.scalar_tensor_tensor(six(SM[:, 0, 0:12]), six(SM[:, 0, 0:12]), -1.0, bc6(SM[:, 7, 0:6]),
                                                ALU.mult, ALU.mult), "gates", l)
                    dve.wait_ge(*after("filled", "poolw", l))
                    for i in range(2):
                        do(dve.tensor_scalar(YP[:, i, :], psum("poolw", l)[:, i * S:(i + 1) * S],
                                             col("pool_scale_2", 2 * l + i), None, ALU.mult))
                    own()
                    cdve.also("read", "poolw", l)
                    split(lambda z: CAT[:, z, 6:8, :], YP[:, :, :], "pool_split", l)

                    def head_squares(name, width, div, at=0):
                        n = TT * width
                        dve.wait_ge(*after(name + "_sq", l))
                        sq = SQ[:, :, 0:width * HD].rearrange("p t (h c) -> p t h c", c=HD)
                        do(dve.tensor_reduce(SS[:, at:at + n].rearrange("p (t h) -> p t h", t=TT), sq, AX.X, ALU.add),
                           name + "_ssum", l)
                        own()
                        do(dve.tensor_scalar(MS[:, at:at + n], SS[:, at:at + n], 1.0 / div, EPS, ALU.mult, ALU.add),
                           name + "_ms", l)

                    def head_scale(name, src, scale_q, width, at=0):
                        dve.wait_ge(*after(name + "_rstd", l))
                        rs = RS[:, at:at + TT * width].rearrange("p (t h) -> p t h", t=TT)
                        if scale_q != 1.0:
                            do(dve.tensor_scalar(rs[:, :, 0:NH], rs[:, :, 0:NH], scale_q, None, ALU.mult))
                            own()
                        v = src.rearrange("p t (h c) -> p t h c", c=HD)
                        do(dve.tensor_tensor(v, v, rs.unsqueeze(3).broadcast_to([P, TT, width, HD]), ALU.mult))

                    head_squares("fx", 12, HD)
                    head_squares("dn", 12, 1.0, 24)
                    head_scale("fx", FQ, 1.0, 12)
                    own()
                    for i, name in enumerate(("fx_qnorm_2", "fx_knorm_2")):
                        for t in range(TT):
                            v = FQ[:, t, i * HW:(i + 1) * HW].rearrange("p (h c) -> p h c", c=HD)
                            do(dve.tensor_tensor(v, v, wide(name, l, HD).unsqueeze(1).broadcast_to([P, NH, HD]),
                                                 ALU.mult), "fx_normed", l)
                    dve.wait_ge(*after("filled", "cum", l))
                    ps = psum("cum", l)
                    do(dve.tensor_copy(GT, ps[0:NH, 128:128 + S]))
                    do(dve.tensor_copy(SM[:, 8, 0:12], ps[:, 0:12]))
                    own()
                    do(dve.scalar_tensor_tensor(SM[:, 11, 0:6], SM[:, 8, 0:6], -1.0, ps[:, 16:22], ALU.mult, ALU.add),
                       "read", "cum", l)
                    dve.wait_ge(*after("filled", "ncum", l))
                    do(dve.tensor_scalar(NCT, psum("ncum", l)[0:NH, 0:S], 8.0, None, ALU.mult), "read", "ncum", l)
                    head_scale("dn", QT3[:, :, 0:2 * HW], HD ** -0.5, 12, 24)
                    own()
                    beta = six(SM[:, 2, 0:12])

                    def heads3(v):
                        return v.rearrange("p t (h c) -> p t h c", c=HD)

                    bb = beta.unsqueeze(3).broadcast_to([P, TT, NH, HD])
                    do(dve.tensor_tensor(heads3(KB), heads3(QT3[:, :, HW:2 * HW]), bb, ALU.mult), "dn_ready", l)
                    do(dve.tensor_tensor(heads3(BV), heads3(QT3[:, :, 2 * HW:]), bb, ALU.mult), "bv", l)
                    dve.wait_ge(*after("expg", l))
                    do(dve.tensor_tensor(KDC.rearrange("p (h c) -> p h c", c=HD),
                                         QT3[:, 0, HW:2 * HW].rearrange("p (h c) -> p h c", c=HD),
                                         SM[:, 10, 0:6].unsqueeze(2).broadcast_to([P, NH, HD]), ALU.mult), "kdc", l)
                    for b in range(4):
                        dve.wait_ge(*after("filled", "grow", l, b))
                        for c in range(3):
                            s = 3 * b + c
                            t, h = chunk_head(s)
                            do(dve.tensor_scalar(DD[:, s, :], psum("grow", l, b)[:, c * P:(c + 1) * P],
                                                 SM[:, 8, NH * t + h:NH * t + h + 1], 0.0, ALU.subtract, ALU.min), "read", "grow", l, b)
                    dve.wait_ge(*after("decay", l))
                    do(dve.tensor_tensor(DD[:, :, :], DD[:, :, :], upper.unsqueeze(1).broadcast_to([P, 12, P]),
                                         ALU.mult))
                    own()
                    for b in range(6):
                        dve.wait_ge(*after("filled", "aq", l, b))
                        do(dve.tensor_tensor(AQ[:, 2 * b:2 * b + 2],
                                             psum("aq", l, b)[:, :].rearrange("p (a b c) -> p a b c", a=2, b=2),
                                             DD[:, 2 * b:2 * b + 2, :].unsqueeze(2).broadcast_to([P, 2, 2, P]),
                                             ALU.mult), "read", "aq", l, b)

                    def outs2(h):
                        if h % 2:
                            dve.wait_ge(*after("filled", "fx_o", l, h // 2))
                            split(lambda z: CAT[:, z, 3 + h // 2, :], psum("fx_o", l, h // 2)[:, 0:S],
                                  "read", "fx_o", l, h // 2)

                    def level_mask(lev, gi):
                        do(dve.tensor_tensor(LT[:, 4 * gi:4 * gi + 4, :], AQ[:, 4 * gi:4 * gi + 4, 0, :],
                                             levels[:, lev, :].unsqueeze(1).broadcast_to([P, 4, P]), ALU.mult),
                           "level", l, lev, gi)

                    idb = ident.unsqueeze(1).broadcast_to([P, 4, P])

                    def first_level():
                        for gi in range(3):
                            level_mask(0, gi)
                        own()
                        for gi in range(3):
                            do(dve.tensor_tensor(DIT[:, 4 * gi:4 * gi + 4, :], idb, LT[:, 4 * gi:4 * gi + 4, :],
                                                 ALU.subtract))
                        for gi in range(3):
                            g4 = slice(4 * gi, 4 * gi + 4)
                            dve.wait_ge(*after("filled", "inv0", l, gi))
                            do(dve.tensor_tensor(DI[:, g4, :], idb,
                                                 psum("inv0", l, gi)[:, :].rearrange("p (a b) -> p a b", a=4),
                                                 ALU.subtract), "read", "inv0", l, gi)
                            cdve.also("inv", l, 0, gi)
                            own()
                            level_mask(1, gi)

                    def inverse_level(lev):
                        if lev == 0:
                            first_level()
                        if lev == 0 or lev >= LEVELS:
                            return
                        for gi in range(3):
                            g4 = slice(4 * gi, 4 * gi + 4)
                            names = (("invd", DI), ("invt", DIT)) if lev < LEVELS - 1 else (("invt", DIT),)
                            for name, dst in names:
                                dve.wait_ge(*after("filled", "invt", l, lev, gi))
                                do(dve.tensor_tensor(dst[:, g4, :], dst[:, g4, :],
                                                     psum(name, l, lev, gi)[:, :].rearrange("p (a b) -> p a b", a=4),
                                                     ALU.subtract), "read", name, l, lev, gi)
                            cdve.also("inv", l, lev, gi)
                            if lev < LEVELS - 1:
                                level_mask(lev + 1, gi)

                    attention(AH + XH + NH * l, NH, 0.125, causal, outs2, 2, inverse_level)
                    def h6(v):
                        return v.rearrange("p (h c) -> p h c", c=HD)

                    def parity(v, par):
                        return v.rearrange("p (g two c) -> p g two c", two=2, c=HD)[:, :, par, :]

                    for par in range(2):
                        eg = SM[:, 9, 6:12].rearrange("p (g two) -> p g two", two=2)[:, :, par].unsqueeze(2)\
                            .broadcast_to([P, 3, HD])
                        dve.wait_ge(*after("filled", "ks", l, par))
                        ps = psum("ks", l, par)
                        do(dve.tensor_tensor(parity(VN[:, 1, :], par), h6(ps[:, 0:3 * HD]), eg, ALU.mult))
                        do(dve.tensor_tensor(parity(O[:, 1, :], par), h6(ps[:, 3 * HD:6 * HD]), eg, ALU.mult),
                           "read", "ks", l, par)
                    own()
                    do(dve.tensor_tensor(BV[:, 1, :], BV[:, 1, :], VN[:, 1, :], ALU.subtract), "bv1", l)
                    dve.wait_ge(*after("filled", "o1", l))
                    do(dve.tensor_tensor(O[:, 1, :], psum("o1", l)[:, 0:HW], O[:, 1, :], ALU.add), "read", "o1", l)
                    dve.wait_ge(*after("silu_z", l))
                    head_squares("o", NH, HD)
                    head_scale("o", O, 1.0, NH)
                    own()
                    for t in range(TT):
                        v = h6(O[:, t, :])
                        do(dve.tensor_tensor(v, v, wide("dn_onorm_2", l, HD).unsqueeze(1).broadcast_to([P, NH, HD]),
                                             ALU.mult))
                    own()
                    do(dve.tensor_tensor(O[:, :, :], O[:, :, :], ZAB[:, :, 0:HW], ALU.mult), "dn_out", l)
                    for b, n in ((0, 2), (1, 1)):
                        dve.wait_ge(*after("filled", "dnoT", l, b))
                        split(lambda z: CAT[:, z, 2 * b:2 * b + n, :],
                              psum("dnoT", l, b)[:, 0:n * S].rearrange("p (a b) -> p a b", a=n), "read", "dnoT", l, b)
                    low(4)
                    add_residual("wout2", l)
                    norm(i0 + 1, X, "norm2_2", 8 * l, HT if l == 0 else None, T2)
                    if l == 0:
                        for i in range(GU2):
                            low(2)
                            dve.wait_ge(*after("read", "gate", i))
                            dve.wait_ge(*after("filled", "up2", i))
                            if i // 2 >= 2:
                                dve.wait_ge(*after("down", "ffn", i // 2 - 2))
                            do(dve.tensor_tensor(PRD[:, i % 2, :], SG[:, i % 2, :], psum("up2", i)[:, :], ALU.mult),
                               "read", "up2", i)
                            own()
                            split(lambda z: UH[:, z, i // 2 % 2, 2 * (i % 2):2 * (i % 2) + 2, :],
                                  PRD[:, i % 2, :].rearrange("p (a b) -> p a b", a=2), "hidden", "ffn", i)
                            if i >= 2 and i % 2 == 0:
                                low(2)
                        low(1)
                        dve.wait_ge(*after("down", "ffn", DN2 - 1))
                        add_banks("x", "ffn")
                        continue

                    LG = GATE
                    dve.wait_ge(*after("filled", "router"))
                    do(dve.tensor_copy(LG[:, :, :], psum("router")[:, 0:TT * NE].rearrange("p (t e) -> p t e", t=TT)),
                       "read", "router")
                    own()
                    RKs = SM[:, 0, :].rearrange("p (t e) -> p t e", t=TT)
                    lane = SM[:, 1, 0:NE]
                    hot = SM[:, 4, :].rearrange("p (t e) -> p t e", t=TT)
                    hot2 = SM[:, 5, :].rearrange("p (t e) -> p t e", t=TT)
                    cur = SM[:, 6, :].rearrange("p (t e) -> p t e", t=TT)
                    m1, m2, mr = SM[:, 7, 0:2], SM[:, 7, 2:4], SM[:, 7, 4:6]
                    for k in range(NE):
                        do(dve.memset(lane[:, k:k + 1], float(NE - k)))
                    own()

                    def bce(v):
                        return v.unsqueeze(2).broadcast_to([P, TT, NE])

                    def one_hot(src, m, dst):
                        do(dve.tensor_reduce(m, src, AX.X, ALU.max))
                        own()
                        do(dve.tensor_tensor(RKs, src, bce(m), ALU.is_equal))
                        own()
                        do(dve.tensor_tensor(RKs, RKs, lane.unsqueeze(1).broadcast_to([P, TT, NE]), ALU.mult))
                        own()
                        do(dve.tensor_reduce(mr, RKs, AX.X, ALU.max))
                        own()
                        do(dve.tensor_tensor(dst, RKs, bce(mr), ALU.is_equal))
                        own()

                    one_hot(LG, m1, hot)
                    do(dve.scalar_tensor_tensor(cur, hot, NEG, LG, ALU.mult, ALU.add))
                    own()
                    one_hot(cur, m2, hot2)
                    do(dve.tensor_tensor(hot, hot, hot2, ALU.add), "hot")
                    do(dve.tensor_tensor(SM[:, 2, :].rearrange("p (t e) -> p t e", t=TT), LG, bce(m1), ALU.subtract),
                       "logit_shift")
                    dve.wait_ge(*after("gate_exp"))
                    own()
                    ex = SM[:, 3, :].rearrange("p (t e) -> p t e", t=TT)
                    do(dve.tensor_tensor(ex, ex, hot, ALU.mult))
                    own()
                    do(dve.tensor_reduce(mr, ex, AX.X, ALU.add))
                    own()
                    do(dve.reciprocal(m2, mr))
                    own()
                    do(dve.tensor_tensor(GATE[:, :, :], ex, bce(m2), ALU.mult))
                    rank = SM[:, 9, :].rearrange("p (t e) -> p t e", t=TT)
                    picked = SM[:, 10, :].rearrange("p (t e) -> p t e", t=TT)
                    over, nth, which = SM[:, 11, 0:NE], SM[:, 12, 0:NE], SM[:, 13, 0:NE]
                    wsum = SM[:, 14, 0:NE]
                    do(dve.memset(PG[:, :, :], -1.0))
                    for e in range(NE):
                        do(dve.memset(ITEM[0:1, e:e + 1], e))
                    do(dve.memset(ITEM[0:1, NE:16], 0))
                    dve.wait_ge(*after("filled", "ranks"))
                    ps = psum("ranks")
                    do(dve.tensor_tensor(rank, ps[:, 0:2 * NE].rearrange("p (t e) -> p t e", t=TT), hot, ALU.mult))
                    do(dve.tensor_scalar(over, ps[:, 2 * NE:3 * NE], float(P), None, ALU.is_gt), "read", "ranks")
                    own()
                    do(dve.tensor_scalar(PG[:, 0:NE, 0:2], rank.rearrange("p t e -> p e t"), -1.0, None, ALU.add))
                    do(dve.tensor_copy(PG[:, 0:NE, 2:4], GATE.rearrange("p t e -> p e t")))
                    own()
                    for t in range(TT):
                        do(dve.tensor_scalar(GSEL[:, t, :], iota, PG[:, 0, t:t + 1], None, ALU.is_equal), "select0")
                    do(dve.tensor_copy(nth[:, 0:1], over[:, 0:1]))
                    for e in range(1, NE):
                        own()
                        do(dve.tensor_tensor(nth[:, e:e + 1], nth[:, e - 1:e], over[:, e:e + 1], ALU.add))
                    own()
                    for j in range(MORE):
                        do(dve.scalar_tensor_tensor(which, nth, float(j + 1), over, ALU.is_equal, ALU.mult))
                        own()
                        wb = which.unsqueeze(1).broadcast_to([P, TT, NE])
                        do(dve.tensor_tensor(picked, rank, wb, ALU.mult))
                        own()
                        do(dve.tensor_reduce(mr, picked, AX.X, ALU.add))
                        own()
                        do(dve.tensor_scalar(PG[:, NE + j, 0:2], mr, -1.0 - P, None, ALU.add))
                        do(dve.tensor_tensor(picked, GATE, wb, ALU.mult))
                        own()
                        do(dve.tensor_reduce(PG[:, NE + j, 2:4], picked, AX.X, ALU.add))
                        do(dve.tensor_tensor(wsum, which, lane, ALU.mult))
                        own()
                        do(dve.tensor_reduce(m1[:, 0:1], wsum, AX.X, ALU.add))
                        own()
                        do(dve.tensor_scalar(m1[:, 0:1], m1[:, 0:1], -1.0, float(NE), ALU.mult, ALU.add))
                        own()
                        do(dve.tensor_scalar(ITEM[0:1, NE + j:NE + j + 1], m1[0:1, 0:1], float(NE - 1), None, ALU.min))
                    do(dve.tensor_scalar(ITEM[0:1, 15:16], nth[0:1, NE - 1:NE], float(NE), None, ALU.add), "items")
                    gain = [cols("norm2_2", 8 + 4 * part, 4).unsqueeze(2).broadcast_to([P, 4, P]) for part in range(2)]

                    def four(ps):
                        return ps[:, :].rearrange("p (k n) -> p k n", k=4)

                    for part in range(2):
                        dve.wait_ge(*after("filled", "gather", part))
                        do(dve.tensor_tensor(HGT[:, 4 * part:4 * part + 4, :], four(psum("gather", part)), gain[part],
                                             ALU.mult), "read", "gather", part)
                    own()
                    split(lambda z: HG[:, z], HGT[:, :, :], "first_gathered")
                    dve.wait_ge(*after("items"))
                    items = dve.value_load(ITEM[0:1, 15:16], min_val=NE, max_val=NE + MORE)
                    base = cdve.n
                    with dve.Fori(0, items) as i:
                        dve.wait_ge(*in_loop(i, "dve", "gathered", before=True))
                        do(dve.tensor_copy(PC[:, 0:4].unsqueeze(1), PG[:, bass.ds(i, 1), :]))
                        do(dve.tensor_copy(PC[:, 4:6].unsqueeze(1), PG[:, bass.ds(i + 1, 1), 0:2]), "item_row")
                        dve.wait_ge(*in_loop(i, "dve", "item_row"))
                        dve.wait_ge(*in_loop(i, "pe", "item", "scatterT", before=True))
                        for t in range(TT):
                            do(dve.tensor_scalar(GGATE[:, t, :], iota, PC[:, t:t + 1], PC[:, 2 + t:3 + t],
                                                 ALU.is_equal, ALU.mult), "gate_rows")

                        def low_item(*ss):
                            for s in ss:
                                j = EXPERT0 + s
                                for b in range(2):
                                    part = slice(b * HALF, (b + 1) * HALF)
                                    dve.wait_ge(*in_loop(i, "act", "hi_item", s, b))
                                    do(dve.tensor_tensor(WS[:, j % SPLIT, 1, part], W[:, j % RING, part],
                                                         WS[:, j % SPLIT, 0, part].bitcast(F32), ALU.subtract),
                                       "lo_item", s, b)

                        def hidden(n):
                            dve.wait_ge(*in_loop(i, "act", "item_read", f"gate{n}"))
                            dve.wait_ge(*in_loop(i, "pe", "item", f"up{n}"))
                            dve.wait_ge(*in_loop(i, "pe", "item", f"hT{n}", before=True))
                            do(dve.tensor_tensor(HH[:, n, :], SGE[:, n, :], item_bank(f"up{n}")[:, :], ALU.mult),
                               "hh", n)
                            cdve.also("item_read", f"up{n}")

                        def hidden_split(n):
                            dve.wait_ge(*in_loop(i, "act", "hhi", n))
                            do(dve.tensor_tensor(HHT[:, 1, 4 * n:4 * n + 4, :], four(item_bank(f"hT{n}")),
                                                 HHT[:, 0, 4 * n:4 * n + 4, :].bitcast(F32), ALU.subtract),
                               "item_read", f"hT{n}")

                        low_item(2, 3, 4, 5)
                        hidden(0)
                        low_item(6, 7, 8, 9)
                        hidden(1)
                        hidden_split(0)
                        low_item(10, 11)
                        dve.wait_ge(*in_loop(i, "pe", "item", "gather1", before=True))
                        for t in range(TT):
                            do(dve.tensor_scalar(GSEL[:, t, :], iota, PC[:, 4 + t:5 + t], None, ALU.is_equal),
                               "select")
                        low_item(12, 13)
                        hidden(2)
                        hidden_split(1)
                        low_item(14, 15)
                        hidden_split(2)
                        low_item(16, 17)
                        for part in range(2):
                            dve.wait_ge(*in_loop(i, "pe", "item", f"gather{part}"))
                            do(dve.tensor_tensor(HGT[:, 4 * part:4 * part + 4, :], four(item_bank(f"gather{part}")),
                                                 gain[part], ALU.mult), "item_read", f"gather{part}")
                        dve.wait_ge(*in_loop(i, "act", "ghi"))
                        do(dve.tensor_tensor(HG[:, 1], HGT[:, :, :], HG[:, 0].bitcast(F32), ALU.subtract))
                        cdve.also("gathered")
                        low_item(18, 19)
                    points[("per", "dve")] = ("dve", cdve.n - base)
                    dve.wait_ge(*in_loop(items - 1, "pe", "item", "scatter"))
                    for b in range(4):
                        dve.tensor_copy(X[:, b // 2, (b % 2) * 512:(b % 2 + 1) * 512], banks[b][:, :])\
                           .then_inc(moe_out, 1)


_INS = ['x', 'mem', 'norm_mix_g', 'w_in', 'conv_w', 'conv_b', 'conv_ln_g', 'conv_ln_b', 'w_out', 'norm_x_g',
        'norm_mem_g', 'w_xq', 'w_xk', 'w_xv', 'w_xo', 'norm_mlp_g', 'w_up', 'w_down', 'norm_final_g', 'norm1_2',
        'w_in_2', 'dn_conv_2', 'dn_a_log_2', 'dn_dt_bias_2', 'dn_onorm_2', 'fx_qnorm_2', 'fx_knorm_2',
        'fx_f_bias_2', 'pool_w_2', 'pool_scale_2', 'w_out_2', 'norm2_2', 'ffn_gate_2', 'ffn_up_2', 'ffn_down_2',
        'router_2', 'moe_gate_2', 'moe_up_2', 'moe_down_2']
_OUTS = [((1, S, D), 'float32')]
STOP = 0


def kernel(**inputs):
    import numpy as _np
    import concourse.bacc as _bacc
    from concourse import mybir as _mybir
    from concourse.bass_utils import run_bass_kernel_spmd as _run

    arrays = {f"in_{name}_dram": _np.ascontiguousarray(inputs[name]) for name in _INS}
    arrays["in_table_dram"] = table()
    points = {}
    for _ in range(2):
        nc = _bacc.Bacc("TRN2", target_bir_lowering=False, num_devices=1)
        args = {name[3:-5]: nc.dram_tensor(name, a.shape, _mybir.dt.from_np(a.dtype), kind="ExternalInput").ap()
                for name, a in arrays.items()}
        outs = [nc.dram_tensor(f"out_{i}_dram", shape, _mybir.dt.from_np(_np.dtype(dtype)), kind="ExternalOutput").ap()
                for i, (shape, dtype) in enumerate(_OUTS)]
        program(nc, args, outs[0], points, STOP)
    r = _run(nc, [arrays], core_ids=[0])
    return r.results[0]["out_0_dram"]
```
